# Optimizing a Trainium2 kernel written in Bass

```python
import math
import numpy as np
import jax
import jax.numpy as jnp
from jax import lax

D_MODEL = 2048
BATCH = 1
SEQ = 256
DEPTH = 1

CHUNK = 64
BLOCK_Q = 128
FOX_HEADS = 8
FOX_HEAD_DIM = 128
FOX_WIDTH = FOX_HEADS * FOX_HEAD_DIM
RET_HEADS = 8
RET_QK_DIM = 128
RET_V_DIM = 128
RET_QK_WIDTH = RET_HEADS * RET_QK_DIM
RET_V_WIDTH = RET_HEADS * RET_V_DIM
N_BRANCHES = 2
MEM_TOKENS = 256
MEM_HEADS = 4
MEM_HEAD_DIM = 128
MEM_WIDTH = MEM_HEADS * MEM_HEAD_DIM
PEER_HEADS = 8
PEER_NKEYS = 128
PEER_QUERY_DIM = 256
PEER_TOPK = 16
N_EXPERTS = PEER_NKEYS * PEER_NKEYS
PEER_TOKEN_BLOCK = 128
ROPE_BASE = 10000.0
EPS = 1e-6
IN_SPLIT_SIZES = (FOX_WIDTH, FOX_WIDTH, FOX_WIDTH, FOX_HEADS, RET_QK_WIDTH, RET_QK_WIDTH, RET_V_WIDTH, RET_V_WIDTH, N_BRANCHES * D_MODEL)
N_IN = sum(IN_SPLIT_SIZES)

kernel_name = 'hybrid_fox_retention_peer_block'

def _rms(x, g):
    xf = x.astype(jnp.float32)
    y = xf * lax.rsqrt(jnp.mean(xf * xf, axis=-1, keepdims=True) + EPS)
    return (y * g.astype(jnp.float32)).astype(x.dtype)

def _split_heads(t, n_heads):
    b, s, _ = t.shape
    return t.reshape(b, s, n_heads, -1).transpose(0, 2, 1, 3)

def _merge_heads(t):
    b, h, s, d = t.shape
    return t.transpose(0, 2, 1, 3).reshape(b, s, h * d)

def _rope(x):
    s, d = x.shape[-2], x.shape[-1]
    half = d // 2
    inv_freq = jnp.exp(-math.log(ROPE_BASE) * jnp.arange(half, dtype=jnp.float32) / half)
    ang = jnp.arange(s, dtype=jnp.float32)[:, None] * inv_freq[None, :]
    cos, sin = jnp.cos(ang), jnp.sin(ang)
    xf = x.astype(jnp.float32)
    x1, x2 = xf[..., :half], xf[..., half:]
    return jnp.concatenate([x1 * cos - x2 * sin, x1 * sin + x2 * cos], axis=-1).astype(x.dtype)

def _fox_attention(q, k, v, cum_logf):
    s_len, d = q.shape[2], q.shape[3]
    scale = d ** -0.5
    neg = jnp.finfo(jnp.float32).min
    outs = []
    for i in range(s_len // BLOCK_Q):
        lo, hi = i * BLOCK_Q, (i + 1) * BLOCK_Q
        qb = q[:, :, lo:hi]
        kb = k[:, :, :hi]
        vb = v[:, :, :hi]
        logits = jnp.einsum('bhqd,bhkd->bhqk', qb, kb).astype(jnp.float32) * scale
        logits = logits + cum_logf[:, :, lo:hi, None] - cum_logf[:, :, None, :hi]
        mask = jnp.arange(hi)[None, :] <= jnp.arange(lo, hi)[:, None]
        logits = jnp.where(mask, logits, neg)
        p = jax.nn.softmax(logits, axis=-1).astype(vb.dtype)
        outs.append(jnp.einsum('bhqk,bhkd->bhqd', p, vb))
    return jnp.concatenate(outs, axis=2)

def _retention(q, k, v):
    b, h, s_len, d = q.shape
    dv = v.shape[-1]
    nc = s_len // CHUNK
    log_g = jnp.log1p(-jnp.exp2(-5.0 - jnp.arange(h, dtype=jnp.float32)))
    idx = jnp.arange(CHUNK, dtype=jnp.float32)
    d_intra = jnp.exp(log_g[:, None, None] * jnp.abs(idx[:, None] - idx[None, :]))
    q_dec = jnp.exp(log_g[:, None] * (idx[None, :] + 1.0))
    k_dec = jnp.exp(log_g[:, None] * (CHUNK - 1.0 - idx[None, :]))
    chunk_dec = jnp.exp(log_g * CHUNK)
    qc = q.astype(jnp.float32).reshape(b, h, nc, CHUNK, d)
    kc = k.astype(jnp.float32).reshape(b, h, nc, CHUNK, d)
    vc = v.astype(jnp.float32).reshape(b, h, nc, CHUNK, dv)
    att = jnp.einsum('bhnid,bhnjd->bhnij', qc, kc) * d_intra[None, :, None]
    y_intra = jnp.einsum('bhnij,bhnje->bhnie', att, vc)
    kv = jnp.einsum('bhncd,bhnce->nbhde', kc * k_dec[None, :, None, :, None], vc)

    def step(state, kv_c):
        return state * chunk_dec[None, :, None, None] + kv_c, state

    _, states = lax.scan(step, jnp.zeros((b, h, d, dv), jnp.float32), kv)
    y_inter = jnp.einsum('bhnid,nbhde->bhnie', qc * q_dec[None, :, None, :, None], states)
    return (y_intra + y_inter).reshape(b, h, s_len, dv)

def _mixer_block(x, ln_g, w_in, b_forget, fox_q_g, fox_k_g, ret_norm_g, w_fox_up, w_ret_up, w_out):
    b, s_len, dm = x.shape
    h = _rms(x, ln_g)
    proj = h @ w_in
    split_pts = np.cumsum(IN_SPLIT_SIZES)[:-1].tolist()
    fq, fk, fv, ff, rq, rk, rv, rg, gate_logits = jnp.split(proj, split_pts, axis=-1)
    q = _rms(_split_heads(fq, FOX_HEADS), fox_q_g)
    k = _rms(_split_heads(fk, FOX_HEADS), fox_k_g)
    v = _split_heads(fv, FOX_HEADS)
    log_f = jax.nn.log_sigmoid(ff.astype(jnp.float32) + b_forget.astype(jnp.float32))
    cum_logf = jnp.cumsum(log_f.transpose(0, 2, 1), axis=-1)
    o_fox = _merge_heads(_fox_attention(q, k, v, cum_logf))
    rq_h = _rope(_split_heads(rq, RET_HEADS))
    rk_h = _rope(_split_heads(rk, RET_HEADS)) * (RET_QK_DIM ** -0.5)
    rv_h = _split_heads(rv, RET_HEADS)
    y = _retention(rq_h, rk_h, rv_h)
    mu = jnp.mean(y, axis=-1, keepdims=True)
    var = jnp.mean(jnp.square(y - mu), axis=-1, keepdims=True)
    y = _merge_heads((y - mu) * lax.rsqrt(var + EPS)) * ret_norm_g.astype(jnp.float32)
    o_ret = (jax.nn.silu(rg.astype(jnp.float32)) * y).astype(x.dtype)
    gates = jax.nn.sigmoid(gate_logits.astype(jnp.float32)).reshape(b, s_len, N_BRANCHES, dm)
    merged = gates[:, :, 0] * (o_fox @ w_fox_up) + gates[:, :, 1] * (o_ret @ w_ret_up)
    return x + merged.astype(x.dtype) @ w_out

def _memory_block(x, mem, ln_g, mem_g, w_mq, w_mkv, q_g, k_g, w_mo):
    b, s_len, _ = x.shape
    m_len = mem.shape[1]
    h = _rms(x, ln_g)
    m = _rms(mem, mem_g)
    q = _rms((h @ w_mq).reshape(b, s_len, MEM_HEADS, MEM_HEAD_DIM), q_g)
    kv = (m @ w_mkv).reshape(b, m_len, 2, MEM_HEADS, MEM_HEAD_DIM)
    k = _rms(kv[:, :, 0], k_g)
    v = kv[:, :, 1]
    logits = jnp.einsum('bshd,bmhd->bhsm', q, k).astype(jnp.float32) * (MEM_HEAD_DIM ** -0.5)
    p = jax.nn.softmax(logits, axis=-1).astype(v.dtype)
    o = jnp.einsum('bhsm,bmhd->bshd', p, v).reshape(b, s_len, MEM_WIDTH)
    return x + o @ w_mo

def _peer_block(x, ln_g, w_q, sub_keys, peer_u, peer_v):
    b, s_len, dm = x.shape
    h = _rms(x, ln_g)
    q = (h @ w_q).reshape(b, s_len, PEER_HEADS, 2, PEER_QUERY_DIM // 2)
    sc = jnp.einsum('bshpd,hpkd->bshpk', q, sub_keys).astype(jnp.float32)
    s_top, i_top = lax.top_k(sc, PEER_TOPK)
    cand = s_top[..., 0, :, None] + s_top[..., 1, None, :]
    cidx = i_top[..., 0, :, None] * PEER_NKEYS + i_top[..., 1, None, :]
    cand = cand.reshape(b, s_len, PEER_HEADS, PEER_TOPK * PEER_TOPK)
    cidx = cidx.reshape(b, s_len, PEER_HEADS, PEER_TOPK * PEER_TOPK)
    s_fin, pos = lax.top_k(cand, PEER_TOPK)
    e_idx = jnp.take_along_axis(cidx, pos, axis=-1)
    gate = jax.nn.softmax(s_fin, axis=-1)
    n_tok = b * s_len
    nb = n_tok // PEER_TOKEN_BLOCK
    hk = PEER_HEADS * PEER_TOPK
    hb = h.reshape(nb, PEER_TOKEN_BLOCK, dm)
    ib = e_idx.reshape(nb, PEER_TOKEN_BLOCK, hk)
    gb = gate.reshape(nb, PEER_TOKEN_BLOCK, hk).astype(h.dtype)

    def expert_block(args):
        hh, ii, gg = args
        act = jnp.einsum('tkd,td->tk', peer_u[ii], hh)
        w = gg * jax.nn.gelu(act)
        return jnp.einsum('tk,tkd->td', w, peer_v[ii])

    out = lax.map(expert_block, (hb, ib, gb)).reshape(b, s_len, dm)
    return x + out

def setup_inputs(seed: int = 0) -> dict:
    key = jax.random.key(seed)
    ks = jax.random.split(key, 24)
    f32 = jnp.float32
    L = DEPTH

    def nrm(k, shape, scale):
        return jax.random.normal(k, shape, f32) * scale

    def gain(k, n):
        return 1.0 + 0.02 * jax.random.normal(k, (L, n), f32)

    return {
        'x': nrm(ks[0], (BATCH, SEQ, D_MODEL), 1.0),
        'mem': nrm(ks[1], (BATCH, MEM_TOKENS, D_MODEL), 1.0),
        'ln_mix_g': gain(ks[2], D_MODEL),
        'w_in': nrm(ks[3], (L, D_MODEL, N_IN), D_MODEL ** -0.5),
        'b_forget': jax.random.uniform(ks[4], (L, FOX_HEADS), f32, 1.0, 6.0),
        'fox_q_norm_g': gain(ks[5], FOX_HEAD_DIM),
        'fox_k_norm_g': gain(ks[6], FOX_HEAD_DIM),
        'ret_norm_g': gain(ks[7], RET_V_WIDTH),
        'w_fox_up': nrm(ks[8], (L, FOX_WIDTH, D_MODEL), FOX_WIDTH ** -0.5),
        'w_ret_up': nrm(ks[9], (L, RET_V_WIDTH, D_MODEL), RET_V_WIDTH ** -0.5),
        'w_out': nrm(ks[10], (L, D_MODEL, D_MODEL), D_MODEL ** -0.5),
        'ln_mem_g': gain(ks[11], D_MODEL),
        'mem_norm_g': gain(ks[12], D_MODEL),
        'w_mq': nrm(ks[13], (L, D_MODEL, MEM_WIDTH), D_MODEL ** -0.5),
        'w_mkv': nrm(ks[14], (L, D_MODEL, 2 * MEM_WIDTH), D_MODEL ** -0.5),
        'mem_q_norm_g': gain(ks[15], MEM_HEAD_DIM),
        'mem_k_norm_g': gain(ks[16], MEM_HEAD_DIM),
        'w_mo': nrm(ks[17], (L, MEM_WIDTH, D_MODEL), MEM_WIDTH ** -0.5),
        'ln_ffn_g': gain(ks[18], D_MODEL),
        'w_peer_q': nrm(ks[19], (L, D_MODEL, PEER_HEADS * PEER_QUERY_DIM), D_MODEL ** -0.5),
        'peer_sub_keys': nrm(ks[20], (L, PEER_HEADS, 2, PEER_NKEYS, PEER_QUERY_DIM // 2), (PEER_QUERY_DIM // 2) ** -0.5),
        'peer_u': nrm(ks[21], (L, N_EXPERTS, D_MODEL), D_MODEL ** -0.5),
        'peer_v': nrm(ks[22], (L, N_EXPERTS, D_MODEL), 0.5),
    }

def reference(x, mem, ln_mix_g, w_in, b_forget, fox_q_norm_g, fox_k_norm_g, ret_norm_g, w_fox_up, w_ret_up, w_out, ln_mem_g, mem_norm_g, w_mq, w_mkv, mem_q_norm_g, mem_k_norm_g, w_mo, ln_ffn_g, w_peer_q, peer_sub_keys, peer_u, peer_v):
    for l in range(DEPTH):
        x = _mixer_block(x, ln_mix_g[l], w_in[l], b_forget[l], fox_q_norm_g[l], fox_k_norm_g[l], ret_norm_g[l], w_fox_up[l], w_ret_up[l], w_out[l])
        x = _memory_block(x, mem, ln_mem_g[l], mem_norm_g[l], w_mq[l], w_mkv[l], mem_q_norm_g[l], mem_k_norm_g[l], w_mo[l])
        x = _peer_block(x, ln_ffn_g[l], w_peer_q[l], peer_sub_keys[l], peer_u[l], peer_v[l])
    return x


_drawn_inputs = setup_inputs


def setup_inputs(seed=0):
    import zlib

    import numpy as np

    out = dict(_drawn_inputs(seed))
    spreads = {}
    factors = {'fox_q_norm_g': 3.803,
     'fox_k_norm_g': 4.058,
     'ret_norm_g': 2.78,
     'ln_mem_g': 5.513,
     'mem_norm_g': 4.335,
     'mem_q_norm_g': 5.488,
     'mem_k_norm_g': 4.537,
     'ln_ffn_g': 6.226}
    for name, (base, spread) in spreads.items():
        noise = np.random.default_rng([zlib.crc32(name.encode()), seed]).standard_normal(out[name].shape)
        drawn = base * np.exp(spread * noise) if base else spread * noise
        out[name] = jnp.asarray(drawn.astype(out[name].dtype))
    for name, factor in factors.items():
        out[name] = (out[name] * factor).astype(out[name].dtype)
    return out
```

```python
import math
from contextlib import ExitStack

import numpy as np
import concourse.bass as bass
from concourse import mybir

D = 2048
SEQ = 256
P = 128
TT = SEQ // P
KT = D // P
HD = 128
FOXH = RETH = 8
MEMH = 4
PH = 8
TOPK = 16
NKEY = 128
CW = 512
CH = CW // HD
KH = KT // 2
RET_CHUNK = 64
EPS = 1e-6
MASKED = -1.0e30
LOWEST = -3.0e38
SLOTS = PH * TOPK
GS = 4
PAIRS = SLOTS // (2 * GS)

FQ, FK, FV, FF = 0, 1024, 2048, 3072
RQ, RK, RV, RG, GATE = 3080, 4104, 5128, 6152, 7176

C_FV, C_RV, C_GATE, C_MK, C_MV = 8, 10, 14, 22, 23
C_UP, C_OUT, C_MQ, C_MO = 24, 32, 36, 37

ST_RET, ST_MK, ST_MERGED, ST_MQ = 8, 12, 13, 17


def build(nc, x, mem, ln_mix_g, w_in, b_forget, fox_q_g, fox_k_g, ret_g, w_fox_up, w_ret_up, w_out,
          ln_mem_g, mem_g, w_mq, w_mkv, mem_q_g, mem_k_g, w_mo, ln_ffn_g, w_pq, sub_keys, peer_u, peer_v,
          t_ident, t_tri, t_mask, t_rope, t_decay, t_delta, t_iota, out):
    f32, u32 = mybir.dt.float32, mybir.dt.uint32
    ALU, ACT, AX = mybir.AluOpType, mybir.ActivationFunctionType, mybir.AxisListType
    ds = bass.ds

    with ExitStack() as ctx:
        def sb(name, shape, dt=f32):
            return ctx.enter_context(nc.sbuf_tensor(name, shape, dt))

        def sem(name):
            return ctx.enter_context(nc.semaphore(name))

        ring = sb("weight_ring", [P, 4, KH, CW])
        urows = ring[:, :, :, :].rearrange("p s k n -> p (s k n)").rearrange("p (r d) -> p r d", d=D)
        xa = sb("resid", [P, TT, D])
        hh = sb("normed", [P, TT, D])
        hT = sb("normedT", [P, KT, SEQ])
        big = sb("big", [P, 18432])
        vrows = big[:, 0:8 * D].rearrange("p (r d) -> p r d", d=D)
        qk = big[:, 0:8192].rearrange("p (c n) -> p c n", n=CH * SEQ)
        qkh = big[:, 0:8192].rearrange("p (h t) -> p h t", t=SEQ)
        val = big[:, 8192:14336].rearrange("p (c t n) -> p c t n", t=TT, n=CW)
        oT = big[:, 14336:18432].rearrange("p (h t) -> p h t", t=SEQ)
        gatesA = hh[:, :, :].rearrange("p t d -> p (t d)").rearrange("p (c t n) -> p c t n", t=TT, n=CW)
        gatesB = big[:, 4096:8192].rearrange("p (c t n) -> p c t n", t=TT, n=CW)
        memx = big[:, 0:4096].rearrange("p (t d) -> p t d", d=D)
        memT = big[:, 8192:12288].rearrange("p (k t) -> p k t", t=SEQ)
        mem_junk = big[:, 8192:12288].rearrange("p (t d) -> p t d", d=D)
        kmT = big[:, 12288:13312].rearrange("p (h t) -> p h t", t=SEQ)
        vm = big[:, 13312:14336].rearrange("p (t n) -> p t n", n=CW)
        keys_raw = big[:, 0:2048].rearrange("p (h d) -> p h d", d=HD)
        keysT = big[:, 2048:4096].rearrange("p (h d) -> p h d", d=NKEY)
        qTm = big[:, 8192:9216].rearrange("p (h t) -> p h t", t=SEQ)
        oTm = big[:, 9216:10240].rearrange("p (h t) -> p h t", t=SEQ)
        mp = big[:, 4096:6144].rearrange("p (g m) -> p g m", m=SEQ)
        mpT = big[:, 6144:8192].rearrange("p (h m q) -> p h m q", m=2, q=SEQ)
        qTp = big[:, 4096:8192].rearrange("p (h t) -> p h t", t=SEQ)
        ffn_gain = big[:, 16384:18432]
        stage = sb("stage", [P, TT, CW])
        att = sb("att", [P, 2, 2, 384])
        pb, pT = att[:, 0], att[:, 1]
        flat_att = att[:, :, :, :].rearrange("p a b c -> p (a b c)")
        sq = flat_att[:, 0:1024].rearrange("p (t n) -> p t n", n=CW)
        ropeA, ropeB = flat_att[:, 0:CW], flat_att[:, CW:2 * CW]
        qs = sb("head_q", [P, 2, SEQ])
        vs = sb("head_v", [P, 2, TT, HD])
        ident = sb("ident", [P, P])
        tri = sb("tri", [P, SEQ])
        mask = sb("mask", [P, 384])
        rope = sb("rope", [P, 2, TT, HD // 2])
        iota = sb("iota", [P, TOPK])
        delta = sb("delta", [40, 8])
        gains = sb("gains", [P, 3, KT])
        hgain = sb("head_gains", [P, 6])
        rgain = sb("ret_gain", [P, RETH])
        eps = sb("eps", [P, 1])
        ss = sb("sumsq", [P, 4, TT])
        rr = sb("rms", [P, 4, TT])
        ssh = sb("head_sumsq", [P, TT, CH])
        wff = sb("w_forget", [P, KT, 8])
        bf = sb("b_forget", [P, 8])
        lf = sb("logf", [P, TT, 40])
        lx = sb("logf_x", [P, TT, 8])
        le = sb("logf_e", [P, TT, 8])
        cq = sb("cum_q", [40, SEQ])
        rh = hh[0:40, :, :].rearrange("p t d -> p (t d)")[:, 0:8 * SEQ].rearrange("p (h t) -> p h t", t=SEQ)
        nm = sb("neg_max", [P, 8])
        rs = sb("row_sum", [P, 8])
        bst = sb("bn", [P, 4, 6])
        mv = sb("mean_var", [P, 4, 2])
        ps = ctx.enter_context(nc.psum_tensor("ps", [P, 8, CW], f32))
        M = 4

        tables_in, x_in, mem_in, keys_in, ffg_in = (sem(n) for n in
            ("tables_in", "x_in", "mem_in", "keys_in", "ffg_in"))
        decay_in = [sem("decay_in0"), sem("decay_in1")]
        w_ready = [sem(f"w_ready{s}") for s in range(4)]
        first_half_used, projected = sem("first_half_used"), sem("projected")
        evacuated = [sem("evacuated0"), sem("evacuated1")]
        prepared = sem("prepared")
        norm_ss, norm_rms, norm_ready = sem("norm_ss"), sem("norm_rms"), sem("norm_ready")
        rows_T, rowsT_dve, rowsT_act = sem("rows_T"), sem("rowsT_dve"), sem("rowsT_act")
        sq_ready, ssq_ready, rms_ready = sem("sq_ready"), sem("ssq_ready"), sem("rms_ready")
        stage_ready, transposed, tstored = sem("stage_ready"), sem("transposed"), sem("tstored")
        ff_done, lf_x, lf_e, lf_ready, cum_done, cum_ready = (sem(n) for n in
            ("ff_done", "lf_x", "lf_e", "lf_ready", "cum_done", "cum_ready"))
        head_staged, logits_done, masked, exped, probs_ready = (sem(n) for n in
            ("head_staged", "logits_done", "masked", "exped", "probs_ready"))
        probs_T, probsT_ready, fox_done, fox_stored = (sem(n) for n in
            ("probs_T", "probsT_ready", "fox_done", "fox_stored"))
        rhead_staged, rscores, rdecayed, ry_done, rvar, rstd = (sem(n) for n in
            ("rhead_staged", "rscores", "rdecayed", "ry_done", "rvar", "rstd"))
        x1_ready, keys_T, keys_stored = sem("x1_ready"), sem("keys_T"), sem("keys_stored")
        mlog, mmax, mexp, mprobs, mpT_done, mpT_ready, mo_done, moT_ready = (sem(n) for n in
            ("mlog", "mmax", "mexp", "mprobs", "mpT_done", "mpT_ready", "mo_done", "moT_ready"))
        pq_done, pq_stored, scores_done, scores_read = (sem(n) for n in
            ("pq_done", "pq_stored", "scores_done", "scores_read"))
        sfin_ready, gexp, gate_ready, routed = (sem(n) for n in ("sfin_ready", "gexp", "gate_ready", "routed"))
        idx_staged = sem("idx_staged")
        u_ready = [sem(f"u_ready{s}") for s in range(8)]
        v_ready = [sem(f"v_ready{s}") for s in range(8)]
        dotted, gelued, weighted, diag_ready, accumulated = (sem(n) for n in
            ("dotted", "gelued", "weighted", "diag_ready", "accumulated"))
        tile_done, out_ready, stored = sem("tile_done"), sem("out_ready"), sem("stored")
        dve_step, act_step = sem("dve_step"), sem("act_step")

        class Steps:
            def __init__(self, eng, s):
                self.eng, self.s, self.n, self.base = eng, s, 0, 0

            def mark(self, ins):
                ins.then_inc(self.s, 1)
                self.n += 1
                return ins

            def settle(self):
                self.eng.wait_ge(self.s, self.base + self.n)

            def link(self, ins):
                self.mark(ins)
                self.settle()

            def enter(self, i, per):
                self.start, self.per = self.n, per
                self.base = i * per

            def leave(self, count):
                assert self.n - self.start == self.per, (self.n - self.start, self.per)
                self.n = self.start + self.per * count
                self.base = 0

        NG = 2 * GS
        idx = sb("expert_idx", [P, TT, SLOTS], u32)
        gate = sb("expert_gate", [P, TT * PH, TOPK])
        ibuf = sb("idx_stage", [P, 2, NG], u32)
        acts = sb("acts", [P, NG])
        gel = sb("gelus", [P, NG])
        wgt = sb("weights", [P, NG])
        diag = [stage[:, s // 4, (s % 4) * P:(s % 4 + 1) * P] for s in range(NG)]
        tv = flat_att[:, 0:64].rearrange("p (q k) -> p q k", k=TOPK)
        tif = flat_att[:, 64:128].rearrange("p (t h k) -> p t h k", h=2, k=TOPK)
        af = flat_att[:, 128:160]
        bfl = flat_att[:, 160:192]
        e0 = flat_att[:, 192:224]
        e1 = flat_att[:, 224:256]
        tmp = flat_att[:, 256:768].rearrange("p (q k) -> p q k", k=NKEY)
        cand = flat_att[:, 768:1280].rearrange("p (t k) -> p t k", k=256)
        tmp2 = qs[:, :, :]
        eq = vs[:, :, :, :].rearrange("p a b c -> p (a b c)").rearrange("p (j a) -> p j a", a=TOPK)
        ti = sb("top_idx", [P, 4, TOPK], u32)
        pos = sb("top_pos", [P, TT, TOPK], u32)
        pab = sb("pos_ab", [P, 2, TT * TOPK], u32)
        gsum = sb("gate_sum", [P, TT * PH])

        block = ctx.enter_context(nc.Block())

        def cols(w, rows0, kt, c0, n):
            v = w[0, rows0:rows0 + kt * P, :].rearrange("(k p) n -> p k n", p=P)
            return v[:, :, ds(c0, n)] if not isinstance(c0, int) else v[:, :, c0:c0 + n]

        @block.sync
        def _(sp):
            for t in range(TT):
                sp.dma_start(xa[:, t, :], x[0, t * P:(t + 1) * P, :]).then_inc(x_in, 16)

            def load_chunk(w, c, par, col):
                for half in range(2):
                    if not (isinstance(c, int) and c < 2):
                        sp.wait_ge(*((first_half_used, c - 1) if half == 0 else (projected, 2 * c - 2)))
                    sp.dma_start(ring[:, 2 * par + half], cols(w, half * KH * P, KH, col, CW)) \
                        .then_inc(w_ready[2 * par + half], 16)

            for c in range(2):
                load_chunk(w_in, c, c, FQ + c * CW)
            for par in range(2):
                load_chunk(w_in, 2 + par, par, FK + par * CW)
            with sp.Fori(0, 2) as i:
                for par in range(2):
                    load_chunk(w_in, 2 * i + (4 + par), par, i * 1024 + (RQ + par * CW))
            for par in range(2):
                load_chunk(w_in, C_FV + par, par, FV + par * CW)
            with sp.Fori(0, 6) as i:
                for par in range(2):
                    load_chunk(w_in, 2 * i + (C_RV + par), par, i * 1024 + (RV + par * CW))
            for par in range(2):
                load_chunk(w_mkv, C_MK + par, par, par * CW)
            for c in range(C_UP, C_UP + 8):
                sp.wait_ge(projected, 2 * (23 if c < 26 else 24 if c < 28 else c - 3))
                w = w_ret_up if c % 2 else w_fox_up
                sp.dma_start(ring[:, c % 4], cols(w, 0, KH, (c - C_UP) // 2 * CW, CW)).then_inc(w_ready[c % 4], 16)
            for c in range(C_OUT, C_MQ + 1):
                for half in range(2):
                    sp.wait_ge(projected, 2 * (30 if c == 32 else 32 if c == 33 else c - 1))
                    w, col = (w_out, (c - C_OUT) * CW) if c < C_MQ else (w_mq, 0)
                    sp.dma_start(ring[:, 2 * (c % 2) + half], cols(w, half * KH * P, KH, col, CW)) \
                        .then_inc(w_ready[2 * (c % 2) + half], 16)
            for s in range(2):
                sp.wait_ge(projected, 2 * C_MQ)
                sp.dma_start(ring[:, 2 + s].rearrange("p k n -> p (k n)").rearrange("p (k n) -> p k n", k=MEMH),
                             cols(w_mo, 0, MEMH, s * 1024, 1024)).then_inc(w_ready[2 + s], 16)
            for cc in range(4):
                for half in range(2):
                    if cc == 0:
                        sp.wait_ge(projected, 2 * (C_MQ + 1))
                    elif cc == 1:
                        sp.wait_ge(projected, 2 * (C_MO + 4))
                    else:
                        sp.wait_ge(pq_done, 4 * (cc - 1))
                    s = 2 * (cc % 2) + half
                    sp.dma_start(ring[:, s], cols(w_pq, half * KH * P, KH, cc * CW, CW)).then_inc(w_ready[s], 16)
            for t in range(TT):
                sp.wait_ge(out_ready, t + 1)
                sp.dma_start(out[0, t * P:(t + 1) * P, :], xa[:, t, :]).then_inc(stored, 16)
            sp.wait_ge(stored, 16 * TT)

        @block.gpsimd
        def _(pool):
            pool.wait_ge(fox_stored, 4)
            for h in range(RETH):
                if h >= 2:
                    pool.wait_ge(rdecayed, h - 1)
                pool.dma_start(pT[:, h % 2, :], t_decay[h]).then_inc(decay_in[h % 2], 16)
                if h == 1:
                    for t in range(TT):
                        pool.dma_start(memx[:, t, :], mem[0, t * P:(t + 1) * P, :]).then_inc(mem_in, 16)
            pool.wait_ge(rows_T, KT)
            pool.dma_start(keys_raw[:, :, :], sub_keys[0].rearrange("h q k d -> k (h q) d")).then_inc(keys_in, 16)
            pool.wait_ge(projected, 2 * C_OUT)
            pool.dma_start(ffn_gain, ln_ffn_g[0:1, :].to_broadcast([P, D])).then_inc(ffg_in, 16)

            def stage_idx(tile, p, par):
                pool.tensor_copy(ibuf[:, par, :], idx[:, tile, ds(p * NG, NG)] if not isinstance(p, int)
                                 else idx[:, tile, p * NG:(p + 1) * NG]).then_inc(idx_staged, 1)

            def gather(rows, k, table, par, sems):
                pool.indirect_dma_start(out=rows[:, k, :], out_offset=None, in_=table[0],
                                        in_offset=bass.IndirectOffsetOnAxis(ap=ibuf[:, par, k:k + 1], axis=0)) \
                    .then_inc(sems[k], 16)

            pool.wait_ge(routed, 1)
            stage_idx(0, 0, 0)
            pool.wait_ge(idx_staged, 1)
            for k in range(NG):
                gather(urows, k, peer_u, 0, u_ready)
                gather(vrows, k, peer_v, 0, v_ready)

            for tile in range(TT):
                for p in range(PAIRS):
                    g = tile * PAIRS + p
                    if g == 0:
                        continue
                    par = g % 2
                    if g >= 2:
                        pool.wait_ge(accumulated, (g - 1) * NG)
                    stage_idx(tile, p, par)
                    pool.wait_ge(idx_staged, g + 1)
                    for k in range(NG):
                        pool.wait_ge(dotted, (g - 1) * NG + k + 1)
                        gather(urows, k, peer_u, par, u_ready)
                        pool.wait_ge(accumulated, (g - 1) * NG + k + 1)
                        gather(vrows, k, peer_v, par, v_ready)

        @block.scalar
        def _(act):
            st = Steps(act, act_step)
            for dst, src in ((ident[:, :], t_ident), (tri[:, :], t_tri), (mask[:, :], t_mask),
                             (rope[:, :, :, :], t_rope), (iota[:, :], t_iota), (delta[:, :], t_delta),
                             (bf[:, :], b_forget[0:1, :].to_broadcast([P, 8])),
                             (wff[:, :, :], w_in[0, :, FF:FF + 8].rearrange("(k p) n -> p k n", p=P)),
                             (gains[:, 0, :], ln_mix_g[0].rearrange("(k p) -> p k", p=P)),
                             (gains[:, 1, :], mem_g[0].rearrange("(k p) -> p k", p=P)),
                             (gains[:, 2, :], ln_mem_g[0].rearrange("(k p) -> p k", p=P)),
                             (hgain[:, 0:1], fox_q_g.rearrange("o p -> p o")),
                             (hgain[:, 1:2], fox_k_g.rearrange("o p -> p o")),
                             (hgain[:, 4:5], mem_k_g.rearrange("o p -> p o")),
                             (hgain[:, 5:6], mem_q_g.rearrange("o p -> p o")),
                             (rgain[:, :], ret_g[0].rearrange("(h p) -> p h", p=P))):
                act.dma_start(dst, src, allow_slow_non_contiguous=True).then_inc(tables_in, 16)

            def norm(n, src, junk, ready, value):
                for t in range(TT):
                    act.wait_ge(ready, value[t])
                    st.link(nc.scalar.activation(junk[:, t, :], src[:, t, :], ACT.Square,
                                                 accum_out=ss[:, n, t:t + 1]))
                    nc.scalar.activation(rr[:, n, t:t + 1], ss[:, n, t:t + 1], ACT.Sqrt, bias=eps[:, :],
                                         scale=1.0 / D).then_inc(norm_rms, 1)

            def store_rowsT(n, dst, gain):
                for k in range(KT):
                    if k // 2 % 2 == 0:
                        continue
                    if k % 2 == 0:
                        act.wait_ge(rows_T, (n * KT + k) // 2 + 1)
                    src = ps[:, M + k // 2 % 4, (k % 2) * SEQ:(k % 2 + 1) * SEQ]
                    if gain is None:
                        nc.scalar.activation(dst[:, k, :], src, ACT.Copy).then_inc(rowsT_act, 1)
                    else:
                        nc.scalar.activation(dst[:, k, :], src, ACT.Copy,
                                             scale=gains[:, gain, k:k + 1]).then_inc(rowsT_act, 1)

            def square_chunk(c, par, s):
                for t in range(TT):
                    act.wait_ge(projected, 2 * c + t + 1)
                    if s >= 1:
                        act.wait_ge(ssq_ready, 2 * (s - 1) + t + 1)
                    nc.scalar.activation(sq[:, t, :], ps[:, 2 * par + t, :], ACT.Square).then_inc(sq_ready, 1)
                    act.wait_ge(ssq_ready, 2 * s + t + 1)
                    nc.scalar.activation(ssh[:, t, :], ssh[:, t, :], ACT.Sqrt, bias=eps[:, :],
                                         scale=1.0 / HD).then_inc(rms_ready, 1)

            def store_stage(s, dst, gain):
                for t in range(TT):
                    act.wait_ge(transposed, 2 * s + t + 1)
                    nc.scalar.activation(dst[:, :, t * P:(t + 1) * P],
                                         ps[:, M + t, :].rearrange("p (h q) -> p h q", q=P), ACT.Copy,
                                         scale=gain).then_inc(tstored, 1)

            act.wait_ge(prepared, 1)
            act.wait_ge(tables_in, 16 * 16)
            norm(0, xa, hh, x_in, (16 * TT, 16 * TT))
            store_rowsT(0, hT, 0)
            for c in range(4):
                if c:
                    store_stage(c - 1, qk[:, c - 1].rearrange("p (h t) -> p h t", t=SEQ), hgain[:, (c - 1) // 2:(c - 1) // 2 + 1])
                square_chunk(c, c % 2, c)
            for c in range(4, 9):
                store_stage(c - 1, qk[:, c - 1].rearrange("p (h t) -> p h t", t=SEQ), hgain[:, (c - 1) // 2:(c - 1) // 2 + 1])

            def copy_chunk(c, dst, func):
                for t in range(TT):
                    act.wait_ge(projected, 2 * c + t + 1)
                    nc.scalar.activation(dst[:, t, :], ps[:, 2 * (c % 2) + t, :], func).then_inc(evacuated[c % 2], 1)

            copy_chunk(8, val[:, 0], ACT.Copy)
            act.wait_ge(lf_x, 1)
            st.link(nc.scalar.activation(le[:, :, :], lx[:, :, :], ACT.Abs))
            st.link(nc.scalar.activation(le[:, :, :], le[:, :, :], ACT.Exp, scale=-1.0))
            nc.scalar.activation(le[:, :, :], le[:, :, :], ACT.Ln, bias=1.0).then_inc(lf_e, 1)
            copy_chunk(9, val[:, 1], ACT.Copy)
            for f in range(4):
                if f == 0:
                    act.wait_ge(tstored, 16)
                    act.wait_ge(evacuated[0], 2 * 5)
                    act.wait_ge(evacuated[1], 2 * 5)
                if f >= 1:
                    act.wait_ge(fox_done, f)
                for e in range(2):
                    h = 2 * f + e
                    nc.scalar.activation(qs[:, e, :], qkh[:, h, :], ACT.Copy).then_inc(head_staged, 1)
                    nc.scalar.activation(vs[:, e], val[:, h // 4, :, (h % 4) * HD:(h % 4 + 1) * HD],
                                         ACT.Copy).then_inc(head_staged, 1)
                for e in range(2):
                    act.wait_ge(masked, 2 * f + e + 1)
                    for t, (a, b) in enumerate(((0, 128), (128, 384))):
                        nc.scalar.activation(pb[:, e, a:b], pb[:, e, a:b], ACT.Exp, bias=nm[:, 2 * e + t:2 * e + t + 1],
                                             accum_out=rs[:, 2 * e + t:2 * e + t + 1]).then_inc(exped, 1)
                for e in range(2):
                    act.wait_ge(probs_T, 2 * f + e + 1)
                    if f:
                        act.wait_ge(fox_done, f)
                    nc.scalar.activation(pT[:, e, :], ps[:, M + e, 0:384], ACT.Copy).then_inc(probsT_ready, 1)
                c = C_RV + f
                copy_chunk(c, val[:, 2 + f], ACT.Copy if f < 2 else ACT.Silu)
                act.wait_ge(fox_done, f + 1)
                nc.scalar.activation(oT[:, 2 * f:2 * f + 2, :], ps[:, M + 2, :].rearrange("p (e q) -> p e q", q=SEQ),
                                     ACT.Copy).then_inc(fox_stored, 1)
            for r in range(4):
                if r == 0:
                    act.wait_ge(evacuated[0], 2 * 7)
                    act.wait_ge(evacuated[1], 2 * 7)
                if r >= 1:
                    act.wait_ge(rscores, 2 * r)
                for e in range(2):
                    nc.scalar.activation(qs[:, e, :], qkh[:, 24 + 2 * r + e, :], ACT.Copy).then_inc(rhead_staged, 1)
                act.wait_ge(rvar, r + 1)
                nc.scalar.activation(mv[:, :, 1:2], mv[:, :, 1:2], ACT.Sqrt, bias=eps[:, :]).then_inc(rstd, 1)
                c = C_GATE + r
                copy_chunk(c, gatesA[:, r], ACT.Sigmoid)
                for t in range(TT):
                    act.wait_ge(transposed, 2 * (ST_RET + r) + t + 1)
                    for e in range(2):
                        h = 2 * r + e
                        ins = nc.scalar.activation(oT[:, RETH + h, t * P:(t + 1) * P],
                                                   ps[:, M + t, e * P:(e + 1) * P], ACT.Copy, scale=rgain[:, h:h + 1])
                    ins.then_inc(tstored, 1)
            norm(1, memx, mem_junk, mem_in, (16 * TT, 16 * TT))
            for c in range(18, 20):
                copy_chunk(c, gatesB[:, c - 18], ACT.Sigmoid)
            copy_chunk(20, gatesB[:, 2], ACT.Sigmoid)
            store_rowsT(1, memT, 1)
            copy_chunk(21, gatesB[:, 3], ACT.Sigmoid)
            square_chunk(C_MK, 0, 4)
            store_stage(ST_MK, kmT, hgain[:, 4:5])
            copy_chunk(C_MV, vm, ACT.Copy)
            for i in range(4):
                store_stage(ST_MERGED + i, hT[:, 4 * i:4 * i + 4, :], 1.0)
            for k in range(4):
                act.wait_ge(keys_T, k + 1)
                nc.scalar.activation(keysT[:, 4 * k:4 * k + 4, :], ps[:, M + 2 + k % 2, :].rearrange("p (h q) -> p h q", q=P),
                                     ACT.Copy).then_inc(keys_stored, 1)
            norm(2, xa, hh, x1_ready, (7, 8))
            store_rowsT(2, hT, 2)
            square_chunk(C_MQ, 0, 5)
            store_stage(ST_MQ, qTm, hgain[:, 5:6])
            act.wait_ge(mmax, 1)
            for g in range(8):
                nc.scalar.activation(mp[:, g, :], ps[:, M + g // 2, (g % 2) * SEQ:(g % 2 + 1) * SEQ], ACT.Exp,
                                     bias=nm[:, g:g + 1], accum_out=rs[:, g:g + 1]).then_inc(mexp, 1)
            for h in range(MEMH):
                act.wait_ge(mpT_done, h + 1)
                nc.scalar.activation(mpT[:, h], ps[:, h, :].rearrange("p (m q) -> p m q", q=SEQ),
                                     ACT.Copy).then_inc(mpT_ready, 1)
            for j in range(2):
                act.wait_ge(mo_done, j + 1)
                nc.scalar.activation(oTm[:, 2 * j:2 * j + 2, :], ps[:, M + j, :].rearrange("p (e q) -> p e q", q=SEQ),
                                     ACT.Copy).then_inc(moT_ready, 1)
            norm(3, xa, hh, x1_ready, (15, 16))
            store_rowsT(3, hT, None)
            for q in range(16):
                act.wait_ge(pq_done, q + 1)
                nc.scalar.activation(qTp[:, q, :], ps[:, q % 4, 0:SEQ], ACT.Copy).then_inc(pq_stored, 1)
            act.wait_ge(sfin_ready, 1)
            nc.scalar.activation(gate[:, :, :], gate[:, :, :], ACT.Exp).then_inc(gexp, 1)
            act.wait_ge(gate_ready, 1)
            for tile in range(TT):
                g0 = tile * PAIRS
                gview = gate[:, tile * PH:(tile + 1) * PH, :].rearrange("p h k -> p (h k)")

                def act_pair(p):
                    g = p + g0
                    for half in range(2):
                        a, b = half * GS, (half + 1) * GS
                        act.wait_ge(dotted, g * NG + b)
                        nc.scalar.activation(gel[:, a:b], acts[:, a:b], ACT.Gelu_apprx_tanh).then_inc(gelued, 1)
                        act.wait_ge(gelued, 2 * g + half + 1)
                        for k in range(a, b):
                            col = slice(p * NG + k, p * NG + k + 1) if isinstance(p, int) else ds(p * NG + k, 1)
                            nc.scalar.activation(wgt[:, k:k + 1], gel[:, k:k + 1], ACT.Copy,
                                                 scale=gview[:, col]).then_inc(weighted, 1)
                        for k in range(a, b):
                            act.wait_ge(weighted, g * NG + k + 1)
                            if not isinstance(g, int):
                                act.wait_ge(accumulated, (g - 1) * NG + k + 1)
                            nc.scalar.activation(diag[k], ident[:, :], ACT.Copy,
                                                 scale=wgt[:, k:k + 1]).then_inc(diag_ready, 1)

                if tile == 0:
                    act_pair(0)
                with act.Fori(1 - tile, PAIRS) as p:
                    act_pair(p)
                act.wait_ge(tile_done, tile + 1)
                nc.scalar.activation(xa[:, tile, :].rearrange("p (b n) -> p b n", n=CW), ps[:, 4 * tile:4 * tile + 4, :],
                                     ACT.Copy).then_inc(out_ready, 1)

        @block.vector
        def _(dve):
            V = nc.vector
            st = Steps(dve, dve_step)
            st.mark(V.memset(eps[:, :], EPS))
            st.mark(V.memset(lf[:, :, :], 0.0))
            st.mark(V.memset(cq[:, :], 1.0))
            st.mark(V.memset(hgain[:, 2:3], 1.0))
            st.mark(V.memset(hgain[:, 3:4], HD ** -0.5))
            dve.wait_ge(tables_in, 16 * 16)
            st.mark(V.tensor_scalar(hgain[:, 0:1], hgain[:, 0:1], HD ** -0.5, None, ALU.mult))
            st.settle()
            V.tensor_scalar(hgain[:, 5:6], hgain[:, 5:6], HD ** -0.5, None, ALU.mult).then_inc(prepared, 1)

            def norm(n, src, dst, gain=None):
                for t in range(TT):
                    dve.wait_ge(norm_rms, 2 * n + t + 1)
                    st.link(V.reciprocal(rr[:, n, t:t + 1], rr[:, n, t:t + 1]))
                    if gain is None:
                        V.tensor_scalar(dst[:, t, :], src[:, t, :], rr[:, n, t:t + 1], None,
                                        ALU.mult).then_inc(norm_ready, 1)
                    else:
                        V.scalar_tensor_tensor(dst[:, t, :], src[:, t, :], rr[:, n, t:t + 1], gain,
                                               ALU.mult, ALU.mult).then_inc(norm_ready, 1)

            def store_rowsT(n, dst, gain):
                for k in range(KT):
                    if k // 2 % 2:
                        continue
                    if k % 2 == 0:
                        dve.wait_ge(rows_T, (n * KT + k) // 2 + 1)
                    src = ps[:, M + k // 2 % 4, (k % 2) * SEQ:(k % 2 + 1) * SEQ]
                    if gain is None:
                        V.tensor_copy(dst[:, k, :], src).then_inc(rowsT_dve, 1)
                    else:
                        V.tensor_scalar(dst[:, k, :], src, gains[:, gain, k:k + 1], None,
                                        ALU.mult).then_inc(rowsT_dve, 1)

            def norm_chunk(par, sqn, s):
                for t in range(TT):
                    dve.wait_ge(sq_ready, 2 * sqn + t + 1)
                    V.tensor_reduce(ssh[:, t, :], sq[:, t, :].rearrange("p (h d) -> p h d", d=HD), AX.X,
                                    ALU.add).then_inc(ssq_ready, 1)
                    dve.wait_ge(rms_ready, 2 * sqn + t + 1)
                    st.link(V.reciprocal(ssh[:, t, :], ssh[:, t, :]))
                    if s:
                        dve.wait_ge(transposed, 2 * s - 1 + t)
                    st.link(V.tensor_tensor(stage[:, t, :].rearrange("p (h d) -> p h d", d=HD),
                                            ps[:, 2 * par + t, :].rearrange("p (h d) -> p h d", d=HD),
                                            ssh[:, t, :].unsqueeze(2).to_broadcast([P, CH, HD]), ALU.mult))
                    dve.sem_inc(evacuated[par], 1)
                    dve.sem_inc(stage_ready, 1)

            norm(0, xa, hh)
            store_rowsT(0, hT, 0)
            for c in range(4):
                norm_chunk(c % 2, c, c)
            for c in range(4, 8):
                for t in range(TT):
                    dve.wait_ge(projected, 2 * c + t + 1)
                    src = ps[:, 2 * (c % 2) + t, :].rearrange("p (g d) -> p g d", d=64)
                    cos = rope[:, 0, t, :].unsqueeze(1).to_broadcast([P, 8, 64])
                    sin = rope[:, 1, t, :].unsqueeze(1).to_broadcast([P, 8, 64])
                    st.mark(V.tensor_tensor(ropeA.rearrange("p (g d) -> p g d", d=64), src, cos, ALU.mult))
                    st.link(V.tensor_tensor(ropeB.rearrange("p (g d) -> p g d", d=64), src, sin, ALU.mult))
                    dve.sem_inc(evacuated[c % 2], 1)
                    dve.wait_ge(transposed, 2 * c - 1 + t)
                    a = ropeA.rearrange("p (h g d) -> p h g d", g=2, d=64)
                    b = ropeB.rearrange("p (h g d) -> p h g d", g=2, d=64)
                    o = stage[:, t, :].rearrange("p (h g d) -> p h g d", g=2, d=64)
                    st.mark(V.tensor_tensor(o[:, :, 0, :], a[:, :, 0, :], b[:, :, 1, :], ALU.subtract))
                    st.link(V.tensor_tensor(o[:, :, 1, :], a[:, :, 1, :], b[:, :, 0, :], ALU.add))
                    dve.sem_inc(stage_ready, 1)
            dve.wait_ge(ff_done, 1)
            V.tensor_tensor(lx[:, :, :], ps[:, M + 2, 0:16].rearrange("p (t h) -> p t h", h=8),
                            bf[:, :].unsqueeze(1).to_broadcast([P, TT, 8]), ALU.add).then_inc(lf_x, 1)
            dve.wait_ge(lf_e, 1)
            st.mark(V.scalar_tensor_tensor(lf[:, :, 0:8], lx[:, :, :], 0.0, le[:, :, :], ALU.min, ALU.subtract))
            V.scalar_tensor_tensor(lf[:, :, 32:40], lx[:, :, :], 0.0, le[:, :, :], ALU.min, ALU.subtract).then_inc(lf_ready, 1)
            dve.wait_ge(cum_done, 1)
            st.mark(V.tensor_copy(cq[0:8, :], ps[0:8, M + 3, 0:SEQ]))
            db = delta[:, :].unsqueeze(2).to_broadcast([40, 8, SEQ])
            st.link(V.scalar_tensor_tensor(rh, db, -1.0, ps[0:40, M + 3, 0:SEQ].unsqueeze(1).to_broadcast([40, 8, SEQ]),
                                           ALU.mult, ALU.mult))
            V.tensor_copy(rh[0:8], db[0:8]).then_inc(cum_ready, 1)
            for f in range(4):
                for e in range(2):
                    dve.wait_ge(logits_done, 2 * f + e + 1)
                    if f:
                        dve.wait_ge(probs_T, 2 * (f - 1) + e + 1)
                    st.link(V.tensor_tensor(pb[:, e, :], ps[:, M + 2 + e, 0:384], mask[:, :], ALU.add))
                    st.mark(V.tensor_reduce(nm[:, 2 * e:2 * e + 1], pb[:, e, 0:128], AX.X, ALU.max, negate=True))
                    V.tensor_reduce(nm[:, 2 * e + 1:2 * e + 2], pb[:, e, 128:384], AX.X, ALU.max,
                                    negate=True).then_inc(masked, 1)
                for e in range(2):
                    dve.wait_ge(exped, 4 * f + 2 * e + 2)
                    st.link(V.reciprocal(rs[:, 2 * e:2 * e + 2], rs[:, 2 * e:2 * e + 2]))
                    st.mark(V.tensor_scalar(pb[:, e, 0:128], pb[:, e, 0:128], rs[:, 2 * e:2 * e + 1], None, ALU.mult))
                    V.tensor_scalar(pb[:, e, 128:384], pb[:, e, 128:384], rs[:, 2 * e + 1:2 * e + 2], None,
                                    ALU.mult).then_inc(probs_ready, 1)
            for r in range(4):
                for e in range(2):
                    dve.wait_ge(rscores, 2 * r + e + 1)
                    dve.wait_ge(decay_in[e], 16 * (r + 1))
                    if r:
                        dve.wait_ge(ry_done, r)
                    else:
                        dve.wait_ge(probs_T, 8)
                    V.tensor_tensor(pb[:, e, :], ps[:, M + 2 + e, 0:384], pT[:, e, :], ALU.mult).then_inc(rdecayed, 1)
                dve.wait_ge(ry_done, r + 1)
                for q in range(4):
                    st.mark(V.bn_stats(bst[:, q, :], ps[:, M + 2, q * HD:(q + 1) * HD]))
                st.settle()
                for q in range(4):
                    st.mark(V.bn_aggr(mv[:, q, :], bst[:, q, :]))
                st.settle()
                dve.sem_inc(rvar, 1)
                dve.wait_ge(rstd, r + 1)
                st.link(V.reciprocal(mv[:, :, 1:2], mv[:, :, 1:2]))
                for t in range(TT):
                    dve.wait_ge(transposed, 2 * (ST_RET + r) - 1 + t)
                    for e in range(2):
                        q = 2 * t + e
                        st.mark(V.tensor_scalar(stage[:, t, e * HD:(e + 1) * HD], ps[:, M + 2, q * HD:(q + 1) * HD],
                                                mv[:, q, 0:1], mv[:, q, 1:2], ALU.subtract, ALU.mult))
                    st.settle()
                    h = 2 * r
                    V.tensor_tensor(stage[:, t, 0:256], stage[:, t, 0:256],
                                    val[:, 4 + h // 4, t, (h % 4) * HD:(h % 4 + 2) * HD], ALU.mult).then_inc(stage_ready, 1)
            norm(1, memx, memx)
            store_rowsT(1, memT, 1)
            norm_chunk(0, 4, ST_MK)
            for i in range(4):
                for t in range(TT):
                    g = gatesA[:, i, t, :], gatesB[:, i, t, :]
                    dve.wait_ge(projected, 2 * (C_UP + 2 * i) + t + 1)
                    st.mark(V.tensor_tensor(g[0], ps[:, t, :], g[0], ALU.mult))
                st.settle()
                dve.sem_inc(evacuated[0], 2)
                for t in range(TT):
                    g = gatesA[:, i, t, :], gatesB[:, i, t, :]
                    dve.wait_ge(projected, 2 * (C_UP + 2 * i + 1) + t + 1)
                    st.link(V.tensor_tensor(g[1], ps[:, 2 + t, :], g[1], ALU.mult))
                    dve.wait_ge(transposed, 2 * (ST_MERGED + i) - 1 + t)
                    V.tensor_tensor(stage[:, t, :], g[0], g[1], ALU.add).then_inc(stage_ready, 1)
                dve.sem_inc(evacuated[1], 2)

            def add_chunk(c, col):
                for t in range(TT):
                    dve.wait_ge(projected, 2 * c + t + 1)
                    st.link(V.tensor_tensor(xa[:, t, col:col + CW], ps[:, 2 * (c % 2) + t, :], xa[:, t, col:col + CW], ALU.add))
                    dve.sem_inc(evacuated[c % 2], 1)
                    dve.sem_inc(x1_ready, 1)

            for c in range(C_OUT, C_MQ):
                add_chunk(c, (c - C_OUT) * CW)
            norm(2, xa, hh)
            store_rowsT(2, hT, 2)
            norm_chunk(0, 5, ST_MQ)
            dve.wait_ge(mlog, 1)
            V.tensor_reduce(nm[:, :], ps[:, M:M + 4, :].rearrange("p b (t m) -> p (b t) m", m=SEQ), AX.X, ALU.max,
                            negate=True).then_inc(mmax, 1)
            dve.wait_ge(mexp, 8)
            st.link(V.reciprocal(rs[:, :], rs[:, :]))
            V.tensor_tensor(mp[:, :, :], mp[:, :, :], rs[:, :].unsqueeze(2).to_broadcast([P, 8, SEQ]),
                            ALU.mult).then_inc(mprobs, 1)
            for c in range(C_MO, C_MO + 4):
                add_chunk(c, (c - C_MO) * CW)
            dve.wait_ge(ffg_in, 16)
            norm(3, xa, hh, ffn_gain)
            store_rowsT(3, hT, None)

            def topk(dst_v, dst_i, srcs, tmps):
                n = len(srcs)
                for q in range(n):
                    st.mark(V.max(dst_v[q][:, 0:8], srcs[q]))
                st.settle()
                for q in range(n):
                    st.mark(V.max_index(dst_i[q][:, 0:8], dst_v[q][:, 0:8], srcs[q]))
                    st.mark(V.match_replace(tmps[q], dst_v[q][:, 0:8], srcs[q], LOWEST))
                st.settle()
                for q in range(n):
                    st.mark(V.max(dst_v[q][:, 8:16], tmps[q]))
                st.settle()
                for q in range(n):
                    st.mark(V.max_index(dst_i[q][:, 8:16], dst_v[q][:, 8:16], tmps[q]))
                st.settle()

            for h in range(PH):
                dve.wait_ge(scores_done, h + 1)
                topk([tv[:, q, :] for q in range(4)], [ti[:, q, :] for q in range(4)],
                     [ps[:, M + h % 4, q * NKEY:(q + 1) * NKEY] for q in range(4)], [tmp[:, q, :] for q in range(4)])
                dve.sem_inc(scores_read, 1)
                st.mark(V.tensor_copy(tif[:, :, :, :], ti[:, :, :].rearrange("p (t h) k -> p t h k", h=2)))
                for t in range(TT):
                    st.mark(V.tensor_tensor(cand[:, t, :].rearrange("p (a b) -> p a b", b=TOPK),
                                            tv[:, 2 * t, :].unsqueeze(2).to_broadcast([P, TOPK, TOPK]),
                                            tv[:, 2 * t + 1, :].unsqueeze(1).to_broadcast([P, TOPK, TOPK]), ALU.add))
                st.settle()
                topk([gate[:, t * PH + h, :] for t in range(TT)], [pos[:, t, :] for t in range(TT)],
                     [cand[:, t, :] for t in range(TT)], [tmp2[:, t, :] for t in range(TT)])
                posf = pos[:, :, :].rearrange("p t k -> p (t k)")
                st.mark(V.tensor_scalar(pab[:, 0, :], posf, 4, None, ALU.logical_shift_right))
                st.link(V.tensor_scalar(pab[:, 1, :], posf, TOPK - 1, None, ALU.bitwise_and))
                st.mark(V.tensor_copy(af, pab[:, 0, :]))
                st.link(V.tensor_copy(bfl, pab[:, 1, :]))
                for half, (pf, e) in enumerate(((af, e0), (bfl, e1))):
                    st.link(V.tensor_tensor(eq, pf.unsqueeze(2).to_broadcast([P, 32, TOPK]),
                                            iota[:, :].unsqueeze(1).to_broadcast([P, 32, TOPK]), ALU.is_equal))
                    for t in range(TT):
                        st.mark(V.tensor_tensor(eq[:, t * 16:(t + 1) * 16, :], eq[:, t * 16:(t + 1) * 16, :],
                                                tif[:, t, half, :].unsqueeze(1).to_broadcast([P, TOPK, TOPK]), ALU.mult))
                    st.settle()
                    st.link(V.tensor_reduce(e, eq, AX.X, ALU.add))
                st.link(V.scalar_tensor_tensor(idx[:, :, h * TOPK:(h + 1) * TOPK], e0.rearrange("p (t k) -> p t k", k=TOPK),
                                               float(NKEY), e1.rearrange("p (t k) -> p t k", k=TOPK), ALU.mult, ALU.add))
            dve.sem_inc(routed, 1)
            st.link(V.tensor_copy(gsum[:, :], gate[:, :, 0]))
            V.tensor_tensor(gate[:, :, :], gate[:, :, :], gsum[:, :].unsqueeze(2).to_broadcast([P, TT * PH, TOPK]),
                            ALU.subtract).then_inc(sfin_ready, 1)
            dve.wait_ge(gexp, 1)
            st.link(V.tensor_reduce(gsum[:, :], gate[:, :, :], AX.X, ALU.add))
            st.link(V.reciprocal(gsum[:, :], gsum[:, :]))
            V.tensor_tensor(gate[:, :, :], gate[:, :, :], gsum[:, :].unsqueeze(2).to_broadcast([P, TT * PH, TOPK]),
                            ALU.mult).then_inc(gate_ready, 1)
            for tile in range(TT):
                def dot_pair(p):
                    g = p + tile * PAIRS
                    for k in range(NG):
                        if not isinstance(g, int) and k % GS == 0:
                            dve.wait_ge(gelued, 2 * g - 1 + k // GS)
                        dve.wait_ge(u_ready[k], g * 16 + 16)
                        V.tensor_tensor_reduce(out=urows[:, k, :], in0=urows[:, k, :], in1=hh[:, tile, :], scale=1.0,
                                               scalar=0.0, op0=ALU.mult, op1=ALU.add,
                                               accum_out=acts[:, k:k + 1]).then_inc(dotted, 1)

                if tile == 0:
                    dot_pair(0)
                with dve.Fori(1 - tile, PAIRS) as p:
                    dot_pair(p)

        @block.tensor
        def _(pe):
            T = nc.tensor

            def half_chunk(c, r, par, half, lhs):
                pe.wait_ge(w_ready[2 * par + half], 16 * r + 16)
                if half == 0 and not (isinstance(r, int) and r == 0):
                    pe.wait_ge(evacuated[par], 2 * r)
                for t in range(TT):
                    for k in range(KH):
                        ins = T.matmul(ps[:, 2 * par + t, :], lhs[:, half * KH + k, t * P:(t + 1) * P],
                                       ring[:, 2 * par + half, k, :], start=half == 0 and k == 0,
                                       stop=half == 1 and k == KH - 1)
                    if half:
                        ins.then_inc(projected, 1)
                if not half:
                    ins.then_inc(first_half_used, 1)

            def transpose_rows(n, src, k0, k1):
                if k0 == 0:
                    pe.wait_ge(norm_ready, 2 * n + 2)
                for k in range(k0, k1):
                    if k >= 8 and k % 2 == 0:
                        pe.wait_ge(rowsT_act if k // 2 % 2 else rowsT_dve, 8 * n + (k // 2 - 4) // 2 * 2 + 2)
                    for t in range(TT):
                        ins = T.transpose(ps[:, M + k // 2 % 4, (k % 2) * SEQ + t * P:(k % 2) * SEQ + (t + 1) * P],
                                          src[:, t, k * P:(k + 1) * P], ident[:, :])
                    if k % 2:
                        ins.then_inc(rows_T, 1)

            def rowsT_stored(n):
                pe.wait_ge(rowsT_act, 8 * (n + 1))
                pe.wait_ge(rowsT_dve, 8 * (n + 1))

            def transpose_stage(s, blocks=CH):
                for t in range(TT):
                    pe.wait_ge(stage_ready, 2 * s + t + 1)
                    if s:
                        pe.wait_ge(tstored, 2 * s - 1 + t)
                    for b in range(blocks):
                        ins = T.transpose(ps[:, M + t, b * P:(b + 1) * P], stage[:, t, b * P:(b + 1) * P], ident[:, :])
                    ins.then_inc(transposed, 1)

            pe.wait_ge(tables_in, 16 * 16)
            transpose_rows(0, hh, 0, KT)
            rowsT_stored(0)
            for c in range(C_RV):
                half_chunk(c, c // 2, c % 2, 0, hT)
                if 1 <= c <= 8:
                    transpose_stage(c - 1)
                if c == 8:
                    for t in range(TT):
                        for k in range(KT):
                            ins = T.matmul(ps[:, M + 2, t * 8:(t + 1) * 8], hT[:, k, t * P:(t + 1) * P], wff[:, k, :],
                                           start=k == 0, stop=k == KT - 1)
                    ins.then_inc(ff_done, 1)
                if c == 9:
                    pe.wait_ge(lf_ready, 1)
                    T.matmul(ps[0:40, M + 3, 0:SEQ], lf[:, 0, :], tri[:, :], start=True, stop=False)
                    T.matmul(ps[0:40, M + 3, P:SEQ], lf[:, 1, :], tri[:, 0:P], start=False, stop=True).then_inc(cum_done, 1)
                half_chunk(c, c // 2, c % 2, 1, hT)
            pe.wait_ge(cum_ready, 1)
            for f in range(4):
                c = C_RV + f
                pe.wait_ge(head_staged, 4 * (f + 1))
                if f:
                    pe.wait_ge(fox_stored, f)
                for e in range(2):
                    h = 2 * f + e
                    for t, (a, w) in enumerate(((0, P), (P, SEQ))):
                        T.matmul(ps[:, M + 2 + e, a:a + w], qs[:, e, t * P:(t + 1) * P], qkh[:, 8 + h, 0:w], start=True, stop=False)
                        ins = T.matmul(ps[:, M + 2 + e, a:a + w], cq[:, t * P:(t + 1) * P], rh[:, h, 0:w], start=False, stop=True)
                    ins.then_inc(logits_done, 1)
                half_chunk(c, c // 2, c % 2, 0, hT)
                if f == 0:
                    pe.wait_ge(tstored, 16)
                for e in range(2):
                    pe.wait_ge(probs_ready, 2 * f + e + 1)
                    if f:
                        pe.wait_ge(probsT_ready, 2 * (f - 1) + e + 1)
                    for b in range(3):
                        ins = T.transpose(ps[:, M + e, b * P:(b + 1) * P], pb[:, e, b * P:(b + 1) * P], ident[:, :])
                    ins.then_inc(probs_T, 1)
                half_chunk(c, c // 2, c % 2, 1, hT)
                pe.wait_ge(probsT_ready, 2 * f + 2)
                for e in range(2):
                    o = ps[:, M + 2, e * SEQ:(e + 1) * SEQ]
                    T.matmul(o, vs[:, e, 0, :], pT[:, e, 0:SEQ], start=e == 0, stop=False, skip_group_check=True)
                    ins = T.matmul(o[:, P:SEQ], vs[:, e, 1, :], pT[:, e, SEQ:384], start=False, stop=e == 1,
                                   skip_group_check=True)
                ins.then_inc(fox_done, 1)
            for r in range(4):
                c = C_GATE + r
                pe.wait_ge(rhead_staged, 2 * (r + 1))
                if r == 0:
                    pe.wait_ge(fox_stored, 4)
                    pe.wait_ge(probsT_ready, 8)
                if r:
                    pe.wait_ge(stage_ready, 2 * (ST_RET + r))
                for e in range(2):
                    h = 2 * r + e
                    T.matmul(ps[:, M + 2 + e, 0:SEQ], qs[:, e, 0:P], qkh[:, 16 + h, :], start=True, stop=True)
                    T.matmul(ps[:, M + 2 + e, SEQ:384], qs[:, e, P:SEQ], qkh[:, 16 + h, P:SEQ], start=True,
                             stop=True).then_inc(rscores, 1)
                half_chunk(c, c // 2, c % 2, 0, hT)
                pe.wait_ge(rdecayed, 2 * (r + 1))
                for e in range(2):
                    h = 2 * r + e
                    cc, o = 2 + h // 4, (h % 4) * HD
                    T.matmul(ps[:, M + 2, e * HD:(e + 1) * HD], pb[:, e, 0:P], val[:, cc, 0, o:o + HD], start=True, stop=True)
                    y1 = ps[:, M + 2, (2 + e) * HD:(3 + e) * HD]
                    T.matmul(y1, pb[:, e, P:SEQ], val[:, cc, 0, o:o + HD], start=True, stop=False)
                    ins = T.matmul(y1, pb[:, e, SEQ:384], val[:, cc, 1, o:o + HD], start=False, stop=True)
                ins.then_inc(ry_done, 1)
                half_chunk(c, c // 2, c % 2, 1, hT)
                transpose_stage(ST_RET + r, 2)
            for c in range(18, C_MK):
                half_chunk(c, c // 2, c % 2, 0, hT)
                half_chunk(c, c // 2, c % 2, 1, hT)
                if c == 20:
                    pe.wait_ge(tstored, 2 * ST_MK)
                    transpose_rows(1, memx, 0, KT)
            rowsT_stored(1)
            for c in (C_MK, C_MV):
                half_chunk(c, c // 2, c % 2, 0, memT)
                if c == C_MV:
                    transpose_stage(ST_MK)
                half_chunk(c, c // 2, c % 2, 1, memT)

            def up_chunk(c):
                n = 12 + (c - C_UP) // 4
                pe.wait_ge(w_ready[c % 4], 16 * (n + 1))
                pe.wait_ge(evacuated[c % 2], 2 * (c // 2))
                for t in range(TT):
                    for k in range(KH):
                        ins = T.matmul(ps[:, 2 * (c % 2) + t, :], oT[:, (c % 2) * 8 + k, t * P:(t + 1) * P],
                                       ring[:, c % 4, k, :], start=k == 0, stop=k == KH - 1)
                    ins.then_inc(projected, 1)

            for i in range(4):
                up_chunk(C_UP + 2 * i)
                if i:
                    transpose_stage(ST_MERGED + i - 1)
                up_chunk(C_UP + 2 * i + 1)
            transpose_stage(ST_MERGED + 3)
            pe.wait_ge(tstored, 2 * (ST_MERGED + 4))
            pe.wait_ge(keys_in, 16)

            def out_chunk(c, lhs, rnd):
                for half in range(2):
                    s = 2 * (c % 2) + half
                    pe.wait_ge(w_ready[s], 16 * rnd)
                    if half == 0:
                        pe.wait_ge(evacuated[c % 2], 2 * (c // 2))
                    for t in range(TT):
                        for k in range(KH):
                            ins = T.matmul(ps[:, 2 * (c % 2) + t, :], lhs[:, half * KH + k, t * P:(t + 1) * P],
                                           ring[:, s, k, :], start=half == 0 and k == 0, stop=half == 1 and k == KH - 1)
                        if half:
                            ins.then_inc(projected, 1)

            for j in range(4):
                out_chunk(C_OUT + j, hT, 15 + j // 2)
                if j >= 2:
                    pe.wait_ge(keys_stored, j - 1)
                for b in range(4):
                    ins = T.transpose(ps[:, M + 2 + j % 2, b * P:(b + 1) * P], keys_raw[:, 4 * j + b, :], ident[:, :])
                ins.then_inc(keys_T, 1)
            pe.wait_ge(keys_stored, 4)
            transpose_rows(2, hh, 0, KT)
            rowsT_stored(2)
            out_chunk(C_MQ, hT, 17)
            transpose_stage(ST_MQ)
            pe.wait_ge(tstored, 2 * (ST_MQ + 1))
            for g in range(8):
                h, t = g // 2, g % 2
                ins = T.matmul(ps[:, M + h, t * SEQ:(t + 1) * SEQ], qTm[:, h, t * P:(t + 1) * P], kmT[:, h, :], start=True, stop=True)
            ins.then_inc(mlog, 1)
            pe.wait_ge(mprobs, 1)
            pe.wait_ge(evacuated[0], 2 * 19)
            pe.wait_ge(evacuated[1], 2 * 18)
            for h in range(MEMH):
                for m in range(2):
                    for t in range(TT):
                        ins = T.transpose(ps[:, h, m * SEQ + t * P:m * SEQ + (t + 1) * P],
                                          mp[:, 2 * h + t, m * P:(m + 1) * P], ident[:, :])
                ins.then_inc(mpT_done, 1)
            for h in range(MEMH):
                pe.wait_ge(mpT_ready, h + 1)
                o = ps[:, M + h // 2, (h % 2) * SEQ:(h % 2 + 1) * SEQ]
                for m in range(2):
                    ins = T.matmul(o, vm[:, m, h * HD:(h + 1) * HD], mpT[:, h, m, :], start=m == 0, stop=m == 1)
                if h % 2:
                    ins.then_inc(mo_done, 1)
            pe.wait_ge(moT_ready, 2)
            for c in range(C_MO, C_MO + 4):
                j = c - C_MO
                w = ring[:, 2 + j // 2].rearrange("p k n -> p (k n)").rearrange("p (k n) -> p k n", k=MEMH)
                pe.wait_ge(w_ready[2 + j // 2], 16 * 17)
                pe.wait_ge(evacuated[c % 2], 2 * (c // 2))
                for t in range(TT):
                    for k in range(MEMH):
                        ins = T.matmul(ps[:, 2 * (c % 2) + t, :], oTm[:, k, t * P:(t + 1) * P],
                                       w[:, k, (j % 2) * CW:(j % 2 + 1) * CW], start=k == 0, stop=k == MEMH - 1)
                    ins.then_inc(projected, 1)
            transpose_rows(3, hh, 0, KT)
            rowsT_stored(3)
            pe.wait_ge(evacuated[0], 2 * 21)
            pe.wait_ge(evacuated[1], 2 * 20)

            def scores(q):
                h, half = q // 2, q % 2
                pe.wait_ge(pq_stored, q + 1)
                if half == 0 and h >= 4:
                    pe.wait_ge(scores_read, h - 3)
                for t in range(TT):
                    b = (2 * t + half) * NKEY
                    ins = T.matmul(ps[:, M + h % 4, b:b + NKEY], qTp[:, q, t * P:(t + 1) * P], keysT[:, q, :], start=True, stop=True)
                if half:
                    ins.then_inc(scores_done, 1)

            for q in range(16):
                cc, n = q // 4, q % 4
                if n == 0:
                    for half in range(2):
                        s = 2 * (cc % 2) + half
                        pe.wait_ge(w_ready[s], 16 * (18 + cc // 2))
                if q >= 4:
                    pe.wait_ge(pq_stored, q - 3)
                for k in range(KT):
                    ins = T.matmul(ps[:, q % 4, 0:SEQ], ring[:, 2 * (cc % 2) + k // KH, k % KH, n * P:(n + 1) * P], hT[:, k, :],
                                   start=k == 0, stop=k == KT - 1)
                ins.then_inc(pq_done, 1)
                if q:
                    scores(q - 1)
            scores(15)
            pe.wait_ge(pq_stored, 16)
            pe.wait_ge(scores_read, PH)
            for tile in range(TT):
                for b in range(4):
                    T.matmul(ps[:, 4 * tile + b, :], ident[:, :], xa[:, tile, b * CW:(b + 1) * CW], start=True, stop=False)

                def pair(p, last):
                    for k in range(NG):
                        pe.wait_ge(diag_ready, p * NG + (tile * PAIRS * NG + k + 1))
                        pe.wait_ge(v_ready[k], p * 16 + 16 * (tile * PAIRS + 1))
                        for b in range(4):
                            ins = T.matmul(ps[:, 4 * tile + b, :], diag[k], vrows[:, k, b * CW:(b + 1) * CW],
                                           start=False, stop=last and k == NG - 1)
                        ins.then_inc(accumulated, 1)
                with pe.Fori(0, PAIRS - 1) as p:
                    pair(p, False)
                pair(PAIRS - 1, True)
                pe.wait_ge(accumulated, (tile + 1) * PAIRS * NG)
                pe.nop().then_inc(tile_done, 1)


def tables():
    f = np.float32
    ident = np.eye(P, dtype=f)
    s = np.arange(P)[:, None]
    tri = (s <= np.arange(SEQ)[None, :]).astype(f)
    q, k = np.arange(P)[:, None], np.arange(P)[None, :]
    causal = np.where(k <= q, 0.0, MASKED).astype(f)
    mask = np.concatenate([causal, np.zeros((P, P), f), causal], axis=1)
    half = HD // 2
    inv = np.exp(-math.log(10000.0) * np.arange(half, dtype=f) / half).astype(f)
    ang = (np.arange(SEQ, dtype=f)[:, None] * inv[None, :]).reshape(TT, P, half).transpose(1, 0, 2)
    rope = np.stack([np.cos(ang.astype(f)), np.sin(ang.astype(f))], axis=1).astype(f)
    lg = np.log1p(-np.exp2(-5.0 - np.arange(RETH, dtype=f))).astype(f)
    i, j = np.arange(SEQ)[None, :], np.arange(SEQ)[:, None]
    dec = np.exp(lg[:, None, None].astype(np.float64) * np.abs(i - j)) * (j // RET_CHUNK <= i // RET_CHUNK)
    dec = np.concatenate([dec[:, 0:P, :], dec[:, P:SEQ, P:SEQ]], axis=2).astype(f)
    delta = np.zeros((40, 8), f)
    delta[np.arange(8), np.arange(8)] = 1
    delta[32 + np.arange(8), np.arange(8)] = 1
    iota = np.tile(np.arange(TOPK, dtype=f), (P, 1))
    return {"t_ident": ident, "t_tri": tri, "t_mask": mask, "t_rope": rope, "t_decay": dec, "t_delta": delta, "t_iota": iota}


_INS = ['x', 'mem', 'ln_mix_g', 'w_in', 'b_forget', 'fox_q_norm_g', 'fox_k_norm_g', 'ret_norm_g', 'w_fox_up',
        'w_ret_up', 'w_out', 'ln_mem_g', 'mem_norm_g', 'w_mq', 'w_mkv', 'mem_q_norm_g', 'mem_k_norm_g', 'w_mo',
        'ln_ffn_g', 'w_peer_q', 'peer_sub_keys', 'peer_u', 'peer_v']


def kernel(**inputs):
    import concourse.bacc as _bacc
    from concourse.bass_utils import run_bass_kernel_spmd as _run

    nc = _bacc.Bacc("TRN2", target_bir_lowering=False, num_devices=1)
    arrays, args = {}, []
    for name, a in [(n, inputs[n]) for n in _INS] + list(tables().items()):
        a = np.ascontiguousarray(a)
        arrays[f"in_{name}"] = a
        args.append(nc.dram_tensor(f"in_{name}", a.shape, mybir.dt.from_np(a.dtype), kind="ExternalInput").ap())
    args.append(nc.dram_tensor("out", (1, SEQ, D), mybir.dt.float32, kind="ExternalOutput").ap())
    build(nc, *args)
    r = _run(nc, [arrays], core_ids=[0])
    return r.results[0]["out"]
```

```python
import math
from contextlib import ExitStack

import numpy as np
import concourse.bass as bass
from concourse import mybir

D = 2048
SEQ = 256
P = 128
TT = SEQ // P
KT = D // P
HD = 128
FOXH = RETH = 8
MEMH = 4
PH = 8
TOPK = 16
NKEY = 128
CW = 512
CH = CW // HD
KU = 2
KPC = 2 * KU
NU = KT // KU
NRING = 4
RET_CHUNK = 64
EPS = 1e-6
MASKED = -1.0e30
LOWEST = -3.0e38
SLOTS = PH * TOPK
GS = 4
PAIRS = SLOTS // (2 * GS)

FQ, FK, FV, FF = 0, 1024, 2048, 3072
RQ, RK, RV, RG, GATE = 3080, 4104, 5128, 6152, 7176

C_FV, C_RV, C_GATE, C_MK, C_MV = 8, 10, 14, 22, 23
C_UP, C_OUT, C_MQ, C_MO = 24, 32, 36, 37



def first_unit(c):
    if c <= C_UP:
        return NU * c
    if c <= C_OUT:
        return NU * C_UP + NU // 2 * (c - C_UP)
    if c <= C_MO:
        return NU * C_UP + NU // 2 * 8 + NU * (c - C_OUT)
    return NU * C_UP + NU // 2 * 8 + NU * (C_MO - C_OUT) + 2 * (c - C_MO)


ST_RET, ST_MK, ST_MERGED, ST_MQ = 8, 12, 13, 17


def build(nc, x, mem, ln_mix_g, w_in, b_forget, fox_q_g, fox_k_g, ret_g, w_fox_up, w_ret_up, w_out,
          ln_mem_g, mem_g, w_mq, w_mkv, mem_q_g, mem_k_g, w_mo, ln_ffn_g, w_pq, sub_keys, peer_u, peer_v,
          t_ident, t_tri, t_mask, t_rope, t_decay, t_delta, t_iota, out):
    f32, u32 = mybir.dt.float32, mybir.dt.uint32
    ALU, ACT, AX = mybir.AluOpType, mybir.ActivationFunctionType, mybir.AxisListType
    ds = bass.ds

    with ExitStack() as ctx:
        def sb(name, shape, dt=f32):
            return ctx.enter_context(nc.sbuf_tensor(name, shape, dt))

        def sem(name):
            return ctx.enter_context(nc.semaphore(name))

        f32r = mybir.dt.float32r
        xa = sb("resid", [P, TT, D])
        hh = sb("normed", [P, TT, D])
        oT = xa[:, :, :].rearrange("p t d -> p (t d)").rearrange("p (h t) -> p h t", t=SEQ)
        stage = sb("stage", [P, TT, CW])
        att = sb("att", [P, 2, 2, 384])
        pb, pT = att[:, 0], att[:, 1]
        flat_att = att[:, :, :, :].rearrange("p a b c -> p (a b c)")
        sq = flat_att[:, 0:1024].rearrange("p (t n) -> p t n", n=CW)
        ropeA, ropeB = flat_att[:, 0:CW], flat_att[:, CW:2 * CW]
        qs = sb("head_q", [P, 2, SEQ])
        vs = sb("head_v", [P, 2, TT, HD])
        ident = sb("ident", [P, P])
        tri = sb("tri", [P, SEQ])
        mask = sb("mask", [P, 384])
        rope = sb("rope", [P, 2, TT, HD // 2])
        iota = sb("iota", [P, TOPK])
        delta = sb("delta", [40, 8])
        gains = sb("gains", [P, 3, KT])
        hgain = sb("head_gains", [P, 6])
        rgain = sb("ret_gain", [P, RETH])
        eps = sb("eps", [P, 1])
        ss = sb("sumsq", [P, 4, TT])
        rr = sb("rms", [P, 4, TT])
        ssh = sb("head_sumsq", [P, TT, CH])
        wff = sb("w_forget", [P, KT, 8])
        wffs = sb("w_forget_parts", [P, 2, KT, 8], mybir.dt.float32r)
        bf = sb("b_forget", [P, 8])
        lf = sb("logf", [P, TT, 40])
        lx = sb("logf_x", [P, TT, 8])
        le = sb("logf_e", [P, TT, 8])
        cq = hh[0:40, 1, 0:SEQ]
        rh = hh[0:40, :, :].rearrange("p t d -> p (t d)")[:, 0:8 * SEQ].rearrange("p (h t) -> p h t", t=SEQ)
        nm = sb("neg_max", [P, 8])
        rs = sb("row_sum", [P, 8])
        bst = sb("bn", [P, 4, 6])
        mv = sb("mean_var", [P, 4, 2])
        NG = 2 * GS
        idx = sb("expert_idx", [P, TT, SLOTS], u32)
        gate = sb("expert_gate", [P, TT * PH, TOPK])
        ibuf = sb("idx_stage", [P, 2, NG], u32)
        acts = sb("acts", [P, NG])
        gel = sb("gelus", [P, NG])
        wgt = sb("weights", [P, NG])
        diag = [stage[:, s // 4, (s % 4) * P:(s % 4 + 1) * P] for s in range(NG)]
        tv = flat_att[:, 0:64].rearrange("p (q k) -> p q k", k=TOPK)
        tif = flat_att[:, 64:128].rearrange("p (t h k) -> p t h k", h=2, k=TOPK)
        af = flat_att[:, 128:160]
        bfl = flat_att[:, 160:192]
        e0 = flat_att[:, 192:224]
        e1 = flat_att[:, 224:256]
        tmp = flat_att[:, 256:768].rearrange("p (q k) -> p q k", k=NKEY)
        cand = flat_att[:, 768:1280].rearrange("p (t k) -> p t k", k=256)
        tmp2 = qs[:, :, :]
        eq = vs[:, :, :, :].rearrange("p a b c -> p (a b c)").rearrange("p (j a) -> p j a", a=TOPK)
        ti = sb("top_idx", [P, 4, TOPK], u32)
        pos = sb("top_pos", [P, TT, TOPK], u32)
        pab = sb("pos_ab", [P, 2, TT * TOPK], u32)
        gsum = sb("gate_sum", [P, TT * PH])

        with ExitStack() as early:
            def esb(name, shape, dt=f32):
                return early.enter_context(nc.sbuf_tensor(name, shape, dt))
            raw = esb("weight_ring", [P, NRING, KPC, CW])
            ws = esb("weight_parts", [P, 2, NRING, KU, CW], f32r)
            hTs = esb("rowsT_parts", [P, 2, KT, SEQ], f32r)
            big = esb("big", [P, 14336])
        rows = sb("expert_rows", [P, 16, D])
        urows, vrows = rows[:, 0:8], rows[:, 8:16]
        ws_hi, hT_hi = ws[:, 0].bitcast(f32), hTs[:, 0].bitcast(f32)
        qk = big[:, 0:8192].rearrange("p (c n) -> p c n", n=CH * SEQ)
        qkh = big[:, 0:8192].rearrange("p (h t) -> p h t", t=SEQ)
        xin = big[:, 0:4096].rearrange("p (t d) -> p t d", d=D)
        val = big[:, 8192:14336].rearrange("p (c t n) -> p c t n", t=TT, n=CW)
        gatesA = hh[:, :, :].rearrange("p t d -> p (t d)").rearrange("p (c t n) -> p c t n", t=TT, n=CW)
        gatesB = big[:, 4096:8192].rearrange("p (c t n) -> p c t n", t=TT, n=CW)
        memx = big[:, 0:4096].rearrange("p (t d) -> p t d", d=D)
        memT = big[:, 8192:12288].rearrange("p (k t) -> p k t", t=SEQ)
        mem_junk = big[:, 8192:12288].rearrange("p (t d) -> p t d", d=D)
        kmT = big[:, 12288:13312].rearrange("p (h t) -> p h t", t=SEQ)
        vm = big[:, 13312:14336].rearrange("p (t n) -> p t n", n=CW)
        keys_raw = big[:, 0:2048].rearrange("p (h d) -> p h d", d=HD)
        keysT = big[:, 2048:4096].rearrange("p (h d) -> p h d", d=NKEY)
        qTm = big[:, 8192:9216].rearrange("p (h t) -> p h t", t=SEQ)
        oTm = big[:, 9216:10240].rearrange("p (h t) -> p h t", t=SEQ)
        mp = big[:, 4096:6144].rearrange("p (g m) -> p g m", m=SEQ)
        mpT = big[:, 6144:8192].rearrange("p (h m q) -> p h m q", m=2, q=SEQ)
        qTp = big[:, 4096:8192].rearrange("p (h t) -> p h t", t=SEQ)
        ffn_gain = big[:, 0:2048]
        hT = memT
        mergedT = memT
        ps = ctx.enter_context(nc.psum_tensor("ps", [P, 8, CW], f32))
        M = 4

        tables_in, x_in, mem_in, keys_in, ffg_in = (sem(n) for n in
            ("tables_in", "x_in", "mem_in", "keys_in", "ffg_in"))
        decay_in = [sem("decay_in0"), sem("decay_in1")]
        w_ready = [sem(f"w_ready{s}") for s in range(4)]
        projected, units_used = sem("projected"), sem("units_used")
        hi_ready, lo_ready, raw_used = sem("hi_ready"), sem("lo_ready"), sem("raw_used")
        rows_hi, rows_lo, src_hi, src_lo = sem("rows_hi"), sem("rows_lo"), sem("src_hi"), sem("src_lo")
        wff_hi, wff_lo = sem("wff_hi"), sem("wff_lo")
        evacuated = [sem("evacuated0"), sem("evacuated1")]
        prepared = sem("prepared")
        norm_ss, norm_rms, norm_ready = sem("norm_ss"), sem("norm_rms"), sem("norm_ready")
        rows_T, rowsT_dve, rowsT_act = sem("rows_T"), sem("rowsT_dve"), sem("rowsT_act")
        sq_ready, ssq_ready, rms_ready = sem("sq_ready"), sem("ssq_ready"), sem("rms_ready")
        stage_ready, transposed, tstored = sem("stage_ready"), sem("transposed"), sem("tstored")
        ff_done, lf_x, lf_e, lf_ready, cum_done, cum_ready = (sem(n) for n in
            ("ff_done", "lf_x", "lf_e", "lf_ready", "cum_done", "cum_ready"))
        head_staged, logits_done, masked, exped, probs_ready = (sem(n) for n in
            ("head_staged", "logits_done", "masked", "exped", "probs_ready"))
        probs_T, probsT_ready, fox_done, fox_stored = (sem(n) for n in
            ("probs_T", "probsT_ready", "fox_done", "fox_stored"))
        rhead_staged, rscores, rdecayed, ry_done, rvar, rstd = (sem(n) for n in
            ("rhead_staged", "rscores", "rdecayed", "ry_done", "rvar", "rstd"))
        x_again = sem("x_again")
        x1_ready, keys_T, keys_stored = sem("x1_ready"), sem("keys_T"), sem("keys_stored")
        mlog, mmax, mexp, mprobs, mpT_done, mpT_ready, mo_done, moT_ready = (sem(n) for n in
            ("mlog", "mmax", "mexp", "mprobs", "mpT_done", "mpT_ready", "mo_done", "moT_ready"))
        moT_hi = sem("moT_hi")
        pq_done, pq_stored, scores_done, scores_read = (sem(n) for n in
            ("pq_done", "pq_stored", "scores_done", "scores_read"))
        sfin_ready, gexp, gate_ready, routed = (sem(n) for n in ("sfin_ready", "gexp", "gate_ready", "routed"))
        idx_staged = sem("idx_staged")
        u_ready = [sem(f"u_ready{s}") for s in range(8)]
        v_ready = [sem(f"v_ready{s}") for s in range(8)]
        dotted, gelued, weighted, diag_ready, accumulated = (sem(n) for n in
            ("dotted", "gelued", "weighted", "diag_ready", "accumulated"))
        tile_done, out_ready, stored = sem("tile_done"), sem("out_ready"), sem("stored")
        dve_step, act_step = sem("dve_step"), sem("act_step")

        class Steps:
            def __init__(self, eng, s):
                self.eng, self.s, self.n, self.base = eng, s, 0, 0

            def mark(self, ins):
                ins.then_inc(self.s, 1)
                self.n += 1
                return ins

            def settle(self):
                self.eng.wait_ge(self.s, self.base + self.n)

            def link(self, ins):
                self.mark(ins)
                self.settle()

            def enter(self, i, per):
                self.start, self.per = self.n, per
                self.base = i * per

            def leave(self, count):
                assert self.n - self.start == self.per, (self.n - self.start, self.per)
                self.n = self.start + self.per * count
                self.base = 0

        block = ctx.enter_context(nc.Block())

        def wait_chunk(eng, c, t):
            if t == 0:
                eng.wait_ge(projected, c + 1)
            else:
                eng.wait_ge(units_used, first_unit(c + 1))

        def cols(w, rows0, kt, c0, n):
            v = w[0, rows0:rows0 + kt * P, :].rearrange("(k p) n -> p k n", p=P)
            return v[:, :, ds(c0, n)] if not isinstance(c0, int) else v[:, :, c0:c0 + n]

        @block.sync
        def _(sp):
            for t in range(TT):
                sp.dma_start(xin[:, t, :], x[0, t * P:(t + 1) * P, :]).then_inc(x_in, 16)

            def load_chunk(w, c, col, first=False):
                for j in range(NRING):
                    if not first:
                        sp.wait_ge(lo_ready, NU * c + (2 * j + 2 - NU))
                    sp.dma_start(raw[:, j], cols(w, j * KPC * P, KPC, col, CW)).then_inc(w_ready[j], 16)

            load_chunk(w_in, 0, FQ, first=True)
            with sp.Fori(1, 4) as c:
                load_chunk(w_in, c, c * CW + FQ)
            with sp.Fori(0, 4) as i:
                load_chunk(w_in, i + 4, i * CW + RQ)
            for i in range(2):
                load_chunk(w_in, C_FV + i, FV + i * CW)
            with sp.Fori(0, 12) as i:
                load_chunk(w_in, i + C_RV, i * CW + RV)
            for i in range(2):
                load_chunk(w_mkv, C_MK + i, i * CW)
            m = first_unit(C_UP) // 2

            def piece(m, src):
                sp.wait_ge(lo_ready, 2 * m - 6)
                sp.dma_start(raw[:, m % NRING], src).then_inc(w_ready[m % NRING], 16)

            for c in range(C_UP, C_OUT):
                for j in range(2):
                    piece(m, cols(w_ret_up if c % 2 else w_fox_up, j * KPC * P, KPC, (c - C_UP) // 2 * CW, CW))
                    m += 1
                if c == C_UP + 3:
                    sp.wait_ge(src_lo, 16)
                    for t in range(TT):
                        sp.dma_start(xa[:, t, :], x[0, t * P:(t + 1) * P, :]).then_inc(x_again, 16)
            for c in range(C_OUT, C_MO):
                for j in range(NRING):
                    w, col = (w_out, (c - C_OUT) * CW) if c < C_MQ else (w_mq, 0)
                    piece(m, cols(w, j * KPC * P, KPC, col, CW))
                    m += 1
            for c in range(C_MO, C_MO + 4):
                piece(m, cols(w_mo, 0, KPC, (c - C_MO) * CW, CW))
                m += 1
            for cc in range(4):
                for j in range(NRING):
                    if cc == 0:
                        piece(m, cols(w_pq, j * KPC * P, KPC, 0, CW))
                    else:
                        sp.wait_ge(*((pq_done, cc) if j == NRING - 1 else (raw_used, 3 * cc + j - 2)))
                        sp.dma_start(raw[:, j], cols(w_pq, j * KPC * P, KPC, cc * CW, CW)).then_inc(w_ready[j], 16)
                    m += 1
            for t in range(TT):
                sp.wait_ge(out_ready, t + 1)
                sp.dma_start(out[0, t * P:(t + 1) * P, :], xa[:, t, :]).then_inc(stored, 16)
            sp.wait_ge(stored, 16 * TT)

        @block.gpsimd
        def _(pool):
            pool.wait_ge(fox_stored, 4)
            for h in range(RETH):
                if h >= 2:
                    pool.wait_ge(rdecayed, h - 1)
                pool.dma_start(pT[:, h % 2, :], t_decay[h]).then_inc(decay_in[h % 2], 16)
                if h == 1:
                    for t in range(TT):
                        pool.dma_start(memx[:, t, :], mem[0, t * P:(t + 1) * P, :]).then_inc(mem_in, 16)
            pool.wait_ge(rows_T, KT)
            pool.dma_start(keys_raw[:, :, :], sub_keys[0].rearrange("h q k d -> k (h q) d")).then_inc(keys_in, 16)
            pool.wait_ge(keys_T, 4)
            pool.dma_start(ffn_gain, ln_ffn_g[0:1, :].to_broadcast([P, D])).then_inc(ffg_in, 16)

            def stage_idx(tile, p, par):
                pool.tensor_copy(ibuf[:, par, :], idx[:, tile, ds(p * NG, NG)] if not isinstance(p, int)
                                 else idx[:, tile, p * NG:(p + 1) * NG]).then_inc(idx_staged, 1)

            def gather(rows, k, table, par, sems):
                pool.indirect_dma_start(out=rows[:, k, :], out_offset=None, in_=table[0],
                                        in_offset=bass.IndirectOffsetOnAxis(ap=ibuf[:, par, k:k + 1], axis=0)) \
                    .then_inc(sems[k], 16)

            pool.wait_ge(routed, 1)
            stage_idx(0, 0, 0)
            pool.wait_ge(idx_staged, 1)
            for k in range(NG):
                gather(urows, k, peer_u, 0, u_ready)
                gather(vrows, k, peer_v, 0, v_ready)

            for tile in range(TT):
                for p in range(PAIRS):
                    g = tile * PAIRS + p
                    if g == 0:
                        continue
                    par = g % 2
                    if g >= 2:
                        pool.wait_ge(accumulated, (g - 1) * NG)
                    stage_idx(tile, p, par)
                    pool.wait_ge(idx_staged, g + 1)
                    for k in range(NG):
                        pool.wait_ge(dotted, (g - 1) * NG + k + 1)
                        gather(urows, k, peer_u, par, u_ready)
                        pool.wait_ge(accumulated, (g - 1) * NG + k + 1)
                        gather(vrows, k, peer_v, par, v_ready)

        @block.scalar
        def _(act):
            st = Steps(act, act_step)
            for dst, src in ((ident[:, :], t_ident), (tri[:, :], t_tri), (mask[:, :], t_mask),
                             (rope[:, :, :, :], t_rope), (iota[:, :], t_iota), (delta[:, :], t_delta),
                             (bf[:, :], b_forget[0:1, :].to_broadcast([P, 8])),
                             (wff[:, :, :], w_in[0, :, FF:FF + 8].rearrange("(k p) n -> p k n", p=P)),
                             (gains[:, 0, :], ln_mix_g[0].rearrange("(k p) -> p k", p=P)),
                             (gains[:, 1, :], mem_g[0].rearrange("(k p) -> p k", p=P)),
                             (gains[:, 2, :], ln_mem_g[0].rearrange("(k p) -> p k", p=P)),
                             (hgain[:, 0:1], fox_q_g.rearrange("o p -> p o")),
                             (hgain[:, 1:2], fox_k_g.rearrange("o p -> p o")),
                             (hgain[:, 4:5], mem_k_g.rearrange("o p -> p o")),
                             (hgain[:, 5:6], mem_q_g.rearrange("o p -> p o")),
                             (rgain[:, :], ret_g[0].rearrange("(h p) -> p h", p=P))):
                act.dma_start(dst, src, allow_slow_non_contiguous=True).then_inc(tables_in, 16)

            def split_w(a, b):
                for n in range(a, b):
                    if n % 2 == 0:
                        act.wait_ge(w_ready[n // 2 % NRING], 16 * (n // 2 // NRING + 1))
                    if n >= NRING:
                        act.wait_ge(units_used, n - NRING + 1)
                    nc.scalar.activation(ws[:, 0, n % NRING], raw[:, n // 2 % NRING, n % 2 * KU:(n % 2 + 1) * KU],
                                         ACT.Copy).then_inc(hi_ready, 1)

            def split_src(q, u, src, last):
                act.wait_ge(units_used, last + 1)
                nc.scalar.activation(hTs[:, 0, 2 * u:2 * u + 2, :], src[:, 2 * u:2 * u + 2, :], ACT.Copy).then_inc(src_hi, 1)

            def norm(n, src, junk, ready, value):
                for t in range(TT):
                    act.wait_ge(ready, value[t])
                    st.link(nc.scalar.activation(junk[:, t, :], src[:, t, :], ACT.Square,
                                                 accum_out=ss[:, n, t:t + 1]))
                    nc.scalar.activation(rr[:, n, t:t + 1], ss[:, n, t:t + 1], ACT.Sqrt, bias=eps[:, :],
                                         scale=1.0 / D).then_inc(norm_rms, 1)

            def store_rowsT_hi(n, gain):
                for k in range(KT):
                    if k % 2 == 0:
                        act.wait_ge(rows_T, (n * KT + k) // 2 + 1)
                    nc.scalar.activation(hTs[:, 0, k, :], ps[:, M + k // 2 % 4, (k % 2) * SEQ:(k % 2 + 1) * SEQ], ACT.Copy,
                                         scale=gains[:, gain, k:k + 1]).then_inc(rows_hi, 1)

            def store_rowsT(n, dst, gain):
                for k in range(KT):
                    if k // 2 % 2 == 0:
                        continue
                    if k % 2 == 0:
                        act.wait_ge(rows_T, (n * KT + k) // 2 + 1)
                    src = ps[:, M + k // 2 % 4, (k % 2) * SEQ:(k % 2 + 1) * SEQ]
                    nc.scalar.activation(dst[:, k, :], src, ACT.Copy,
                                         scale=1.0 if gain is None else gains[:, gain, k:k + 1]).then_inc(rowsT_act, 1)

            def square_chunk(c, s):
                for t in range(TT):
                    wait_chunk(act, c, t)
                    if s >= 1:
                        act.wait_ge(ssq_ready, 2 * (s - 1) + t + 1)
                    nc.scalar.activation(sq[:, t, :], ps[:, 2 * (c % 2) + t, :], ACT.Square).then_inc(sq_ready, 1)
                    act.wait_ge(ssq_ready, 2 * s + t + 1)
                    nc.scalar.activation(ssh[:, t, :], ssh[:, t, :], ACT.Sqrt, bias=eps[:, :],
                                         scale=1.0 / HD).then_inc(rms_ready, 1)

            def store_stage(s, dst, gain):
                for t in range(TT):
                    act.wait_ge(transposed, 2 * s + t + 1)
                    nc.scalar.activation(dst[:, :, t * P:(t + 1) * P],
                                         ps[:, M + t, :].rearrange("p (h q) -> p h q", q=P), ACT.Copy,
                                         scale=gain).then_inc(tstored, 1)

            def copy_chunk(c, dst, func):
                for t in range(TT):
                    wait_chunk(act, c, t)
                    nc.scalar.activation(dst[:, t, :], ps[:, 2 * (c % 2) + t, :], func).then_inc(evacuated[c % 2], 1)

            def store_qk(c):
                store_stage(c, qk[:, c].rearrange("p (h t) -> p h t", t=SEQ), hgain[:, c // 2:c // 2 + 1])

            def stage_fox_heads(f):
                if f == 0:
                    act.wait_ge(tstored, 16)
                    act.wait_ge(evacuated[0], 2 * 5)
                    act.wait_ge(evacuated[1], 2 * 5)
                for e in range(2):
                    h = 2 * f + e
                    nc.scalar.activation(qs[:, e, :], qkh[:, h, :], ACT.Copy).then_inc(head_staged, 1)
                    nc.scalar.activation(vs[:, e], val[:, h // 4, :, (h % 4) * HD:(h % 4 + 1) * HD],
                                         ACT.Copy).then_inc(head_staged, 1)

            def stage_ret_heads(r):
                if r == 0:
                    act.wait_ge(evacuated[0], 2 * 7)
                    act.wait_ge(evacuated[1], 2 * 7)
                else:
                    act.wait_ge(rscores, 2 * r)
                for e in range(2):
                    nc.scalar.activation(qs[:, e, :], qkh[:, 24 + 2 * r + e, :], ACT.Copy).then_inc(rhead_staged, 1)

            def store_keys(k):
                act.wait_ge(keys_T, k + 1)
                nc.scalar.activation(keysT[:, 4 * k:4 * k + 4, :],
                                     ps[:, M + 2 + k % 2, :].rearrange("p (h q) -> p h q", q=P),
                                     ACT.Copy).then_inc(keys_stored, 1)

            split_w(0, NRING)
            act.wait_ge(tables_in, 16 * 16)
            act.wait_ge(prepared, 1)
            norm(0, xin, hh, x_in, (16 * TT, 16 * TT))
            nc.scalar.activation(wffs[:, 0], wff[:, :, :], ACT.Copy).then_inc(wff_hi, 1)
            store_rowsT_hi(0, 0)
            for c in range(C_RV):
                u = NU * c
                split_w(u + 4, u + 10)
                if 1 <= c <= 8:
                    store_qk(c - 1)
                split_w(u + 10, u + 12)
                if c < 4:
                    square_chunk(c, c)
                if c == 8:
                    act.wait_ge(lf_x, 1)
                    st.link(nc.scalar.activation(le[:, :, :], lx[:, :, :], ACT.Abs))
                    st.link(nc.scalar.activation(le[:, :, :], le[:, :, :], ACT.Exp, scale=-1.0))
                    nc.scalar.activation(le[:, :, :], le[:, :, :], ACT.Ln, bias=1.0).then_inc(lf_e, 1)
                if c >= C_FV:
                    copy_chunk(c, val[:, c - C_FV], ACT.Copy)
            stage_fox_heads(0)
            for f in range(4):
                c = C_RV + f
                u = NU * c
                split_w(u + 4, u + 6)
                for e in range(2):
                    act.wait_ge(masked, 2 * f + e + 1)
                    for t, (a, b) in enumerate(((0, 128), (128, 384))):
                        nc.scalar.activation(pb[:, e, a:b], pb[:, e, a:b], ACT.Exp, bias=nm[:, 2 * e + t:2 * e + t + 1],
                                             accum_out=rs[:, 2 * e + t:2 * e + t + 1]).then_inc(exped, 1)
                split_w(u + 6, u + 9)
                for e in range(2):
                    act.wait_ge(probs_T, 2 * f + e + 1)
                    if f:
                        act.wait_ge(fox_done, f)
                    nc.scalar.activation(pT[:, e, :], ps[:, M + e, 0:384], ACT.Copy).then_inc(probsT_ready, 1)
                split_w(u + 9, u + 12)
                copy_chunk(c, val[:, 2 + f], ACT.Copy if f < 2 else ACT.Silu)
                act.wait_ge(fox_done, f + 1)
                nc.scalar.activation(oT[:, 2 * f:2 * f + 2, :], ps[:, M + 2, :].rearrange("p (e q) -> p e q", q=SEQ),
                                     ACT.Copy).then_inc(fox_stored, 1)
                if f < 3:
                    stage_fox_heads(f + 1)
            stage_ret_heads(0)
            for r in range(4):
                c = C_GATE + r
                u = NU * c
                split_w(u + 4, u + 9)
                act.wait_ge(rvar, r + 1)
                nc.scalar.activation(mv[:, :, 1:2], mv[:, :, 1:2], ACT.Sqrt, bias=eps[:, :]).then_inc(rstd, 1)
                split_w(u + 9, u + 12)
                copy_chunk(c, gatesA[:, r], ACT.Sigmoid)
                for t in range(TT):
                    act.wait_ge(transposed, 2 * (ST_RET + r) + t + 1)
                    for e in range(2):
                        h = 2 * r + e
                        ins = nc.scalar.activation(oT[:, RETH + h, t * P:(t + 1) * P],
                                                   ps[:, M + t, e * P:(e + 1) * P], ACT.Copy, scale=rgain[:, h:h + 1])
                        if e == 0:
                            st.mark(ins)
                    ins.then_inc(tstored, 1)
                if r < 3:
                    stage_ret_heads(r + 1)
            for c in range(18, C_UP):
                u = NU * c
                if c == C_MV:
                    st.settle()
                    act.wait_ge(tstored, 2 * (ST_RET + 4))
                    act.wait_ge(fox_stored, 4)
                for i in range(NU):
                    split_w(u + 4 + i, u + 5 + i)
                    if c == 21:
                        act.wait_ge(rowsT_dve, NU)
                        act.wait_ge(rowsT_act, NU)
                        split_src(0, i, memT, u + i)
                    if c == C_MV:
                        split_src(1, i, oT, u + i)
                    if c == C_MV and i == 5:
                        store_stage(ST_MK, kmT, hgain[:, 4:5])
                if c < C_MK:
                    copy_chunk(c, gatesB[:, c - 18], ACT.Sigmoid)
                if c == 18:
                    norm(1, memx, mem_junk, mem_in, (16 * TT, 16 * TT))
                if c == 20:
                    store_rowsT(1, memT, 1)
                if c == C_MK:
                    square_chunk(c, 4)
                if c == C_MV:
                    copy_chunk(c, vm, ACT.Copy)

            def store_merged(i):
                store_stage(ST_MERGED + i, mergedT[:, 4 * i:4 * i + 4, :], 1.0)

            for c in range(C_UP, C_OUT):
                u = first_unit(c)
                for i in range(4):
                    split_w(u + 4 + i, u + 5 + i)
                    if c == C_OUT - 1:
                        if i == 0:
                            act.wait_ge(tstored, 2 * (ST_MERGED + 3))
                        split_src(2, i, mergedT, u - 1)
                if c > C_UP and c % 2 == 0:
                    store_merged((c - C_UP) // 2 - 1)
            for i in range(4, 6):
                split_src(2, i, mergedT, first_unit(C_OUT) - 1)
            for c in range(C_OUT, C_MQ):
                u = first_unit(c)
                split_w(u + 4, u + 8)
                if c == C_OUT:
                    store_merged(3)
                    act.wait_ge(tstored, 2 * (ST_MERGED + 4))
                    for i in range(6, 8):
                        split_src(2, i, mergedT, first_unit(C_OUT) - 1)
                else:
                    store_keys(c - C_OUT - 1)
                split_w(u + 8, u + 12)
            store_keys(3)
            norm(2, xa, hh, x1_ready, (7, 8))
            store_rowsT_hi(2, 2)
            u = first_unit(C_MQ)
            split_w(u + 4, u + 12)
            square_chunk(C_MQ, 5)
            store_stage(ST_MQ, qTm, hgain[:, 5:6])
            act.wait_ge(mmax, 1)
            for g in range(8):
                nc.scalar.activation(mp[:, g, :], ps[:, M + g // 2, (g % 2) * SEQ:(g % 2 + 1) * SEQ], ACT.Exp,
                                     bias=nm[:, g:g + 1], accum_out=rs[:, g:g + 1]).then_inc(mexp, 1)
            for h in range(MEMH):
                act.wait_ge(mpT_done, h + 1)
                nc.scalar.activation(mpT[:, h], ps[:, h, :].rearrange("p (m q) -> p m q", q=SEQ),
                                     ACT.Copy).then_inc(mpT_ready, 1)
            for j in range(2):
                act.wait_ge(mo_done, j + 1)
                nc.scalar.activation(hTs[:, 0, 2 * j:2 * j + 2, :], ps[:, M + j, :].rearrange("p (e q) -> p e q", q=SEQ),
                                     ACT.Copy).then_inc(moT_hi, 1)
            split_w(first_unit(C_MO) + 4, first_unit(C_MO) + 8)
            norm(3, xa, hh, x1_ready, (15, 16))
            store_rowsT(3, hT, None)
            for q in range(16):
                act.wait_ge(pq_done, q // 4 + 1)
                b = 2 * (q // 4 % 2) + q % 4 // 2
                nc.scalar.activation(qTp[:, q, :], ps[:, b, (q % 2) * SEQ:(q % 2 + 1) * SEQ], ACT.Copy).then_inc(pq_stored, 1)
            act.wait_ge(sfin_ready, 1)
            nc.scalar.activation(gate[:, :, :], gate[:, :, :], ACT.Exp).then_inc(gexp, 1)
            act.wait_ge(gate_ready, 1)
            for tile in range(TT):
                g0 = tile * PAIRS
                gview = gate[:, tile * PH:(tile + 1) * PH, :].rearrange("p h k -> p (h k)")

                def act_pair(p):
                    g = p + g0
                    for half in range(2):
                        a, b = half * GS, (half + 1) * GS
                        act.wait_ge(dotted, g * NG + b)
                        nc.scalar.activation(gel[:, a:b], acts[:, a:b], ACT.Gelu_apprx_tanh).then_inc(gelued, 1)
                        act.wait_ge(gelued, 2 * g + half + 1)
                        for k in range(a, b):
                            col = slice(p * NG + k, p * NG + k + 1) if isinstance(p, int) else ds(p * NG + k, 1)
                            nc.scalar.activation(wgt[:, k:k + 1], gel[:, k:k + 1], ACT.Copy,
                                                 scale=gview[:, col]).then_inc(weighted, 1)
                        for k in range(a, b):
                            act.wait_ge(weighted, g * NG + k + 1)
                            if not isinstance(g, int):
                                act.wait_ge(accumulated, (g - 1) * NG + k + 1)
                            nc.scalar.activation(diag[k], ident[:, :], ACT.Copy,
                                                 scale=wgt[:, k:k + 1]).then_inc(diag_ready, 1)

                if tile == 0:
                    act_pair(0)
                with act.Fori(1 - tile, PAIRS) as p:
                    act_pair(p)
                act.wait_ge(tile_done, tile + 1)
                nc.scalar.activation(xa[:, tile, :].rearrange("p (b n) -> p b n", n=CW), ps[:, 4 * tile:4 * tile + 4, :],
                                     ACT.Copy).then_inc(out_ready, 1)

        @block.vector
        def _(dve):
            V = nc.vector
            st = Steps(dve, dve_step)
            st.mark(V.memset(eps[:, :], EPS))
            st.mark(V.memset(lf[:, :, :], 0.0))
            st.mark(V.memset(hgain[:, 2:3], 1.0))
            st.mark(V.memset(hgain[:, 3:4], HD ** -0.5))
            dve.wait_ge(tables_in, 16 * 16)
            st.mark(V.tensor_scalar(hgain[:, 0:1], hgain[:, 0:1], HD ** -0.5, None, ALU.mult))
            st.settle()
            V.tensor_scalar(hgain[:, 5:6], hgain[:, 5:6], HD ** -0.5, None, ALU.mult).then_inc(prepared, 1)

            def split_w(a, b):
                for n in range(a, b):
                    dve.wait_ge(hi_ready, n + 1)
                    V.tensor_tensor(ws[:, 1, n % NRING], raw[:, n // 2 % NRING, n % 2 * KU:(n % 2 + 1) * KU],
                                    ws_hi[:, n % NRING], ALU.subtract).then_inc(lo_ready, 1)

            def split_src(q, u, src):
                dve.wait_ge(src_hi, NU * q + u + 1)
                V.tensor_tensor(hTs[:, 1, 2 * u:2 * u + 2, :], src[:, 2 * u:2 * u + 2, :], hT_hi[:, 2 * u:2 * u + 2, :],
                                ALU.subtract).then_inc(src_lo, 1)

            def store_rowsT_lo(n, gain):
                for k in range(KT):
                    dve.wait_ge(rows_hi, KT * (n // 2) + (k | 1) + 1)
                    V.scalar_tensor_tensor(hTs[:, 1, k, :], ps[:, M + k // 2 % 4, (k % 2) * SEQ:(k % 2 + 1) * SEQ],
                                           gains[:, gain, k:k + 1], hT_hi[:, k, :], ALU.mult,
                                           ALU.subtract).then_inc(rows_lo, 1)

            def norm(n, src, dst, gain=None):
                for t in range(TT):
                    dve.wait_ge(norm_rms, 2 * n + t + 1)
                    st.link(V.reciprocal(rr[:, n, t:t + 1], rr[:, n, t:t + 1]))
                    if gain is None:
                        V.tensor_scalar(dst[:, t, :], src[:, t, :], rr[:, n, t:t + 1], None,
                                        ALU.mult).then_inc(norm_ready, 1)
                    else:
                        V.scalar_tensor_tensor(dst[:, t, :], src[:, t, :], rr[:, n, t:t + 1], gain,
                                               ALU.mult, ALU.mult).then_inc(norm_ready, 1)

            def store_rowsT(n, dst, gain):
                for k in range(KT):
                    if k // 2 % 2:
                        continue
                    if k % 2 == 0:
                        dve.wait_ge(rows_T, (n * KT + k) // 2 + 1)
                    src = ps[:, M + k // 2 % 4, (k % 2) * SEQ:(k % 2 + 1) * SEQ]
                    if gain is None:
                        V.tensor_copy(dst[:, k, :], src).then_inc(rowsT_dve, 1)
                    else:
                        V.tensor_scalar(dst[:, k, :], src, gains[:, gain, k:k + 1], None,
                                        ALU.mult).then_inc(rowsT_dve, 1)

            def norm_chunk(par, sqn, s):
                for t in range(TT):
                    dve.wait_ge(sq_ready, 2 * sqn + t + 1)
                    V.tensor_reduce(ssh[:, t, :], sq[:, t, :].rearrange("p (h d) -> p h d", d=HD), AX.X,
                                    ALU.add).then_inc(ssq_ready, 1)
                    dve.wait_ge(rms_ready, 2 * sqn + t + 1)
                    st.link(V.reciprocal(ssh[:, t, :], ssh[:, t, :]))
                    if s:
                        dve.wait_ge(transposed, 2 * s - 1 + t)
                    st.link(V.tensor_tensor(stage[:, t, :].rearrange("p (h d) -> p h d", d=HD),
                                            ps[:, 2 * par + t, :].rearrange("p (h d) -> p h d", d=HD),
                                            ssh[:, t, :].unsqueeze(2).to_broadcast([P, CH, HD]), ALU.mult))
                    dve.sem_inc(evacuated[par], 1)
                    dve.sem_inc(stage_ready, 1)

            def rope_chunk(c):
                for t in range(TT):
                    wait_chunk(dve, c, t)
                    src = ps[:, 2 * (c % 2) + t, :].rearrange("p (g d) -> p g d", d=64)
                    cos = rope[:, 0, t, :].unsqueeze(1).to_broadcast([P, 8, 64])
                    sin = rope[:, 1, t, :].unsqueeze(1).to_broadcast([P, 8, 64])
                    st.mark(V.tensor_tensor(ropeA.rearrange("p (g d) -> p g d", d=64), src, cos, ALU.mult))
                    st.link(V.tensor_tensor(ropeB.rearrange("p (g d) -> p g d", d=64), src, sin, ALU.mult))
                    dve.sem_inc(evacuated[c % 2], 1)
                    dve.wait_ge(transposed, 2 * c - 1 + t)
                    a = ropeA.rearrange("p (h g d) -> p h g d", g=2, d=64)
                    b = ropeB.rearrange("p (h g d) -> p h g d", g=2, d=64)
                    o = stage[:, t, :].rearrange("p (h g d) -> p h g d", g=2, d=64)
                    st.mark(V.tensor_tensor(o[:, :, 0, :], a[:, :, 0, :], b[:, :, 1, :], ALU.subtract))
                    st.link(V.tensor_tensor(o[:, :, 1, :], a[:, :, 1, :], b[:, :, 0, :], ALU.add))
                    dve.sem_inc(stage_ready, 1)

            def mask_logits(f):
                for e in range(2):
                    dve.wait_ge(logits_done, 2 * f + e + 1)
                    if f:
                        dve.wait_ge(probs_T, 2 * (f - 1) + e + 1)
                    st.link(V.tensor_tensor(pb[:, e, :], ps[:, M + 2 + e, 0:384], mask[:, :], ALU.add))
                    st.mark(V.tensor_reduce(nm[:, 2 * e:2 * e + 1], pb[:, e, 0:128], AX.X, ALU.max, negate=True))
                    V.tensor_reduce(nm[:, 2 * e + 1:2 * e + 2], pb[:, e, 128:384], AX.X, ALU.max,
                                    negate=True).then_inc(masked, 1)

            def divide_probs(f):
                for e in range(2):
                    dve.wait_ge(exped, 4 * f + 2 * e + 2)
                    st.link(V.reciprocal(rs[:, 2 * e:2 * e + 2], rs[:, 2 * e:2 * e + 2]))
                    st.mark(V.tensor_scalar(pb[:, e, 0:128], pb[:, e, 0:128], rs[:, 2 * e:2 * e + 1], None, ALU.mult))
                    V.tensor_scalar(pb[:, e, 128:384], pb[:, e, 128:384], rs[:, 2 * e + 1:2 * e + 2], None,
                                    ALU.mult).then_inc(probs_ready, 1)

            def decay_scores(r):
                for e in range(2):
                    dve.wait_ge(rscores, 2 * r + e + 1)
                    dve.wait_ge(decay_in[e], 16 * (r + 1))
                    if r:
                        dve.wait_ge(ry_done, r)
                    else:
                        dve.wait_ge(probs_T, 8)
                    V.tensor_tensor(pb[:, e, :], ps[:, M + 2 + e, 0:384], pT[:, e, :], ALU.mult).then_inc(rdecayed, 1)

            def group_norm(r):
                dve.wait_ge(ry_done, r + 1)
                for q in range(4):
                    st.mark(V.bn_stats(bst[:, q, :], ps[:, M + 2, q * HD:(q + 1) * HD]))
                st.settle()
                for q in range(4):
                    st.mark(V.bn_aggr(mv[:, q, :], bst[:, q, :]))
                st.settle()
                dve.sem_inc(rvar, 1)
                dve.wait_ge(rstd, r + 1)
                st.link(V.reciprocal(mv[:, :, 1:2], mv[:, :, 1:2]))
                for t in range(TT):
                    dve.wait_ge(transposed, 2 * (ST_RET + r) - 1 + t)
                    for e in range(2):
                        q = 2 * t + e
                        st.mark(V.tensor_scalar(stage[:, t, e * HD:(e + 1) * HD], ps[:, M + 2, q * HD:(q + 1) * HD],
                                                mv[:, q, 0:1], mv[:, q, 1:2], ALU.subtract, ALU.mult))
                    st.settle()
                    h = 2 * r
                    V.tensor_tensor(stage[:, t, 0:256], stage[:, t, 0:256],
                                    val[:, 4 + h // 4, t, (h % 4) * HD:(h % 4 + 2) * HD], ALU.mult).then_inc(stage_ready, 1)

            def gate_fox(i):
                for t in range(TT):
                    wait_chunk(dve, C_UP + 2 * i, t)
                    st.mark(V.tensor_tensor(gatesA[:, i, t, :], ps[:, t, :], gatesA[:, i, t, :], ALU.mult))
                st.settle()
                dve.sem_inc(evacuated[0], 2)

            def gate_ret(i):
                for t in range(TT):
                    wait_chunk(dve, C_UP + 2 * i + 1, t)
                    st.link(V.tensor_tensor(gatesB[:, i, t, :], ps[:, 2 + t, :], gatesB[:, i, t, :], ALU.mult))
                    dve.sem_inc(evacuated[1], 1)
                    dve.wait_ge(transposed, 2 * (ST_MERGED + i) - 1 + t)
                    V.tensor_tensor(stage[:, t, :], gatesA[:, i, t, :], gatesB[:, i, t, :], ALU.add).then_inc(stage_ready, 1)

            def add_chunk(c, col):
                for t in range(TT):
                    wait_chunk(dve, c, t)
                    st.link(V.tensor_tensor(xa[:, t, col:col + CW], ps[:, 2 * (c % 2) + t, :], xa[:, t, col:col + CW], ALU.add))
                    dve.sem_inc(evacuated[c % 2], 1)
                    dve.sem_inc(x1_ready, 1)

            split_w(0, NRING)
            norm(0, xin, hh)
            dve.wait_ge(wff_hi, 1)
            V.tensor_tensor(wffs[:, 1], wff[:, :, :], wffs[:, 0].bitcast(f32), ALU.subtract).then_inc(wff_lo, 1)
            store_rowsT_lo(0, 0)
            for c in range(C_RV):
                u = NU * c
                split_w(u + 4, u + 12)
                if c < 4:
                    norm_chunk(c % 2, c, c)
                elif c < 8:
                    rope_chunk(c)
                elif c == 8:
                    dve.wait_ge(ff_done, 1)
                    V.tensor_tensor(lx[:, :, :], ps[:, M + 2, 0:16].rearrange("p (t h) -> p t h", h=8),
                                    bf[:, :].unsqueeze(1).to_broadcast([P, TT, 8]), ALU.add).then_inc(lf_x, 1)
                    dve.wait_ge(lf_e, 1)
                    st.mark(V.scalar_tensor_tensor(lf[:, :, 0:8], lx[:, :, :], 0.0, le[:, :, :], ALU.min, ALU.subtract))
                    st.link(V.scalar_tensor_tensor(lf[:, :, 32:40], lx[:, :, :], 0.0, le[:, :, :], ALU.min, ALU.subtract))
                    dve.sem_inc(lf_ready, 1)
                else:
                    dve.wait_ge(cum_done, 1)
                    st.link(V.memset(cq, 1.0))
                    st.mark(V.tensor_copy(cq[0:8, :], ps[0:8, M + 3, 0:SEQ]))
                    db = delta[:, :].unsqueeze(2).to_broadcast([40, 8, SEQ])
                    st.link(V.scalar_tensor_tensor(rh, db, -1.0, ps[0:40, M + 3, 0:SEQ].unsqueeze(1).to_broadcast([40, 8, SEQ]),
                                                   ALU.mult, ALU.mult))
                    V.tensor_copy(rh[0:8], db[0:8]).then_inc(cum_ready, 1)
            for f in range(4):
                u = NU * (C_RV + f)
                split_w(u + 4, u + 6)
                mask_logits(f)
                divide_probs(f)
                split_w(u + 6, u + 12)
            for r in range(4):
                u = NU * (C_GATE + r)
                split_w(u + 4, u + 6)
                decay_scores(r)
                split_w(u + 6, u + 9)
                group_norm(r)
                split_w(u + 9, u + 12)
            for c in range(18, C_UP):
                u = NU * c
                for i in range(NU):
                    split_w(u + 4 + i, u + 5 + i)
                    if c == 21:
                        split_src(0, i, memT)
                    if c == C_MV:
                        split_src(1, i, oT)
                if c == 18:
                    norm(1, memx, memx)
                if c == 20:
                    store_rowsT(1, memT, 1)
                if c == C_MK:
                    norm_chunk(0, 4, ST_MK)
            for c in range(C_UP, C_OUT):
                u = first_unit(c)
                for i in range(4):
                    split_w(u + 4 + i, u + 5 + i)
                    if c == C_OUT - 1:
                        split_src(2, i, mergedT)
                if c % 2:
                    gate_ret((c - C_UP) // 2)
                else:
                    gate_fox((c - C_UP) // 2)
            for i in range(4, 6):
                split_src(2, i, mergedT)
            for c in range(C_OUT, C_MQ):
                u = first_unit(c)
                split_w(u + 4, u + 8)
                if c == C_OUT:
                    for i in range(6, 8):
                        split_src(2, i, mergedT)
                    dve.wait_ge(x_again, 16 * TT)
                split_w(u + 8, u + 12)
                add_chunk(c, (c - C_OUT) * CW)
            norm(2, xa, hh)
            store_rowsT_lo(2, 2)
            u = first_unit(C_MQ)
            split_w(u + 4, u + 12)
            norm_chunk(0, 5, ST_MQ)
            dve.wait_ge(mlog, 1)
            V.tensor_reduce(nm[:, :], ps[:, M:M + 4, :].rearrange("p b (t m) -> p (b t) m", m=SEQ), AX.X, ALU.max,
                            negate=True).then_inc(mmax, 1)
            dve.wait_ge(mexp, 8)
            st.link(V.reciprocal(rs[:, :], rs[:, :]))
            V.tensor_tensor(mp[:, :, :], mp[:, :, :], rs[:, :].unsqueeze(2).to_broadcast([P, 8, SEQ]),
                            ALU.mult).then_inc(mprobs, 1)
            for j in range(2):
                dve.wait_ge(moT_hi, j + 1)
                V.tensor_tensor(hTs[:, 1, 2 * j:2 * j + 2, :], ps[:, M + j, :].rearrange("p (e q) -> p e q", q=SEQ),
                                hT_hi[:, 2 * j:2 * j + 2, :], ALU.subtract).then_inc(moT_ready, 1)
            split_w(first_unit(C_MO) + 4, first_unit(C_MO) + 8)
            for c in range(C_MO, C_MO + 4):
                add_chunk(c, (c - C_MO) * CW)
            dve.wait_ge(ffg_in, 16)
            norm(3, xa, hh, ffn_gain)
            store_rowsT(3, hT, None)

            def topk(dst_v, dst_i, srcs, tmps):
                n = len(srcs)
                for q in range(n):
                    st.mark(V.max(dst_v[q][:, 0:8], srcs[q]))
                st.settle()
                for q in range(n):
                    st.mark(V.max_index(dst_i[q][:, 0:8], dst_v[q][:, 0:8], srcs[q]))
                    st.mark(V.match_replace(tmps[q], dst_v[q][:, 0:8], srcs[q], LOWEST))
                st.settle()
                for q in range(n):
                    st.mark(V.max(dst_v[q][:, 8:16], tmps[q]))
                st.settle()
                for q in range(n):
                    st.mark(V.max_index(dst_i[q][:, 8:16], dst_v[q][:, 8:16], tmps[q]))
                st.settle()

            for h in range(PH):
                dve.wait_ge(scores_done, h + 1)
                topk([tv[:, q, :] for q in range(4)], [ti[:, q, :] for q in range(4)],
                     [ps[:, M + h % 4, q * NKEY:(q + 1) * NKEY] for q in range(4)], [tmp[:, q, :] for q in range(4)])
                dve.sem_inc(scores_read, 1)
                st.mark(V.tensor_copy(tif[:, :, :, :], ti[:, :, :].rearrange("p (t h) k -> p t h k", h=2)))
                for t in range(TT):
                    st.mark(V.tensor_tensor(cand[:, t, :].rearrange("p (a b) -> p a b", b=TOPK),
                                            tv[:, 2 * t, :].unsqueeze(2).to_broadcast([P, TOPK, TOPK]),
                                            tv[:, 2 * t + 1, :].unsqueeze(1).to_broadcast([P, TOPK, TOPK]), ALU.add))
                st.settle()
                topk([gate[:, t * PH + h, :] for t in range(TT)], [pos[:, t, :] for t in range(TT)],
                     [cand[:, t, :] for t in range(TT)], [tmp2[:, t, :] for t in range(TT)])
                posf = pos[:, :, :].rearrange("p t k -> p (t k)")
                st.mark(V.tensor_scalar(pab[:, 0, :], posf, 4, None, ALU.logical_shift_right))
                st.link(V.tensor_scalar(pab[:, 1, :], posf, TOPK - 1, None, ALU.bitwise_and))
                st.mark(V.tensor_copy(af, pab[:, 0, :]))
                st.link(V.tensor_copy(bfl, pab[:, 1, :]))
                for half, (pf, e) in enumerate(((af, e0), (bfl, e1))):
                    st.link(V.tensor_tensor(eq, pf.unsqueeze(2).to_broadcast([P, 32, TOPK]),
                                            iota[:, :].unsqueeze(1).to_broadcast([P, 32, TOPK]), ALU.is_equal))
                    for t in range(TT):
                        st.mark(V.tensor_tensor(eq[:, t * 16:(t + 1) * 16, :], eq[:, t * 16:(t + 1) * 16, :],
                                                tif[:, t, half, :].unsqueeze(1).to_broadcast([P, TOPK, TOPK]), ALU.mult))
                    st.settle()
                    st.link(V.tensor_reduce(e, eq, AX.X, ALU.add))
                st.link(V.scalar_tensor_tensor(idx[:, :, h * TOPK:(h + 1) * TOPK], e0.rearrange("p (t k) -> p t k", k=TOPK),
                                               float(NKEY), e1.rearrange("p (t k) -> p t k", k=TOPK), ALU.mult, ALU.add))
            dve.sem_inc(routed, 1)
            st.link(V.tensor_copy(gsum[:, :], gate[:, :, 0]))
            V.tensor_tensor(gate[:, :, :], gate[:, :, :], gsum[:, :].unsqueeze(2).to_broadcast([P, TT * PH, TOPK]),
                            ALU.subtract).then_inc(sfin_ready, 1)
            dve.wait_ge(gexp, 1)
            st.link(V.tensor_reduce(gsum[:, :], gate[:, :, :], AX.X, ALU.add))
            st.link(V.reciprocal(gsum[:, :], gsum[:, :]))
            V.tensor_tensor(gate[:, :, :], gate[:, :, :], gsum[:, :].unsqueeze(2).to_broadcast([P, TT * PH, TOPK]),
                            ALU.mult).then_inc(gate_ready, 1)
            for tile in range(TT):
                def dot_pair(p):
                    g = p + tile * PAIRS
                    for k in range(NG):
                        if not isinstance(g, int) and k % GS == 0:
                            dve.wait_ge(gelued, 2 * g - 1 + k // GS)
                        dve.wait_ge(u_ready[k], g * 16 + 16)
                        V.tensor_tensor_reduce(out=urows[:, k, :], in0=urows[:, k, :], in1=hh[:, tile, :], scale=1.0,
                                               scalar=0.0, op0=ALU.mult, op1=ALU.add,
                                               accum_out=acts[:, k:k + 1]).then_inc(dotted, 1)

                if tile == 0:
                    dot_pair(0)
                with dve.Fori(1 - tile, PAIRS) as p:
                    dot_pair(p)

        @block.tensor
        def _(pe):
            T = nc.tensor

            PARTS = ((0, 0), (0, 1), (1, 0))

            def units(c, a, b, k0=0, n_units=NU):
                par = c % 2
                if a == 0 and c >= 2:
                    pe.wait_ge(evacuated[par], 2 * (c // 2))
                for i in range(a, b):
                    n = first_unit(c) + i
                    pe.wait_ge(lo_ready, n + 1)
                    if c in SOURCE:
                        pe.wait_ge(src_lo, SOURCE[c] + i + 1)
                    for t in range(TT):
                        for kk in range(KU):
                            for rp, wp in PARTS:
                                ins = T.matmul(ps[:, 2 * par + t, :],
                                               hTs[:, rp, k0 + KU * i + kk, t * P:(t + 1) * P], ws[:, wp, n % NRING, kk, :],
                                               start=i == 0 and kk == 0 and rp + wp == 0,
                                               stop=i == n_units - 1 and kk == KU - 1 and rp == 1)
                        if t == 0 and i == n_units - 1:
                            ins.then_inc(projected, 1)
                    ins.then_inc(units_used, 1)

            SOURCE = {C_MK: 0, C_UP: NU, C_UP + 1: NU + 4, C_OUT: 2 * NU}

            def transpose_rows(n, src, k0, k1):
                if k0 == 0:
                    pe.wait_ge(norm_ready, 2 * n + 2)
                for k in range(k0, k1):
                    if k >= 8 and k % 2 == 0:
                        if n % 2 == 0:
                            pe.wait_ge(rows_lo, KT * (n // 2) + k - 6)
                        else:
                            pe.wait_ge(rowsT_act if k // 2 % 2 else rowsT_dve, 8 * (n // 2) + (k // 2 - 4) // 2 * 2 + 2)
                    for t in range(TT):
                        ins = T.transpose(ps[:, M + k // 2 % 4, (k % 2) * SEQ + t * P:(k % 2) * SEQ + (t + 1) * P],
                                          src[:, t, k * P:(k + 1) * P], ident[:, :])
                    if k % 2:
                        ins.then_inc(rows_T, 1)

            def transpose_stage(s, blocks=CH):
                for t in range(TT):
                    pe.wait_ge(stage_ready, 2 * s + t + 1)
                    if s:
                        pe.wait_ge(tstored, 2 * s - 1 + t)
                    for b in range(blocks):
                        ins = T.transpose(ps[:, M + t, b * P:(b + 1) * P], stage[:, t, b * P:(b + 1) * P], ident[:, :])
                    ins.then_inc(transposed, 1)

            pe.wait_ge(tables_in, 16 * 16)
            transpose_rows(0, hh, 0, KT)
            pe.wait_ge(rows_lo, KT)
            for c in range(C_RV):
                units(c, 0, 6)
                if 1 <= c <= 8:
                    transpose_stage(c - 1)
                if c == 8:
                    pe.wait_ge(wff_lo, 1)
                    for t in range(TT):
                        for k in range(KT):
                            for rp, wp in PARTS:
                                ins = T.matmul(ps[:, M + 2, t * 8:(t + 1) * 8], hTs[:, rp, k, t * P:(t + 1) * P],
                                               wffs[:, wp, k, :], start=k == 0 and rp + wp == 0, stop=k == KT - 1 and rp == 1)
                    ins.then_inc(ff_done, 1)
                if c == 9:
                    pe.wait_ge(lf_ready, 1)
                    T.matmul(ps[0:40, M + 3, 0:SEQ], lf[:, 0, :], tri[:, :], start=True, stop=False)
                    T.matmul(ps[0:40, M + 3, P:SEQ], lf[:, 1, :], tri[:, 0:P], start=False, stop=True).then_inc(cum_done, 1)
                units(c, 6, NU)
            pe.wait_ge(cum_ready, 1)
            for f in range(4):
                c = C_RV + f
                units(c, 0, 2)
                pe.wait_ge(head_staged, 4 * (f + 1))
                if f:
                    pe.wait_ge(fox_stored, f)
                for e in range(2):
                    h = 2 * f + e
                    for t, (a, w) in enumerate(((0, P), (P, SEQ))):
                        T.matmul(ps[:, M + 2 + e, a:a + w], qs[:, e, t * P:(t + 1) * P], qkh[:, 8 + h, 0:w], start=True, stop=False)
                        ins = T.matmul(ps[:, M + 2 + e, a:a + w], cq[:, t * P:(t + 1) * P], rh[:, h, 0:w], start=False, stop=True)
                    ins.then_inc(logits_done, 1)
                units(c, 2, 5)
                if f == 0:
                    pe.wait_ge(tstored, 16)
                for e in range(2):
                    pe.wait_ge(probs_ready, 2 * f + e + 1)
                    if f:
                        pe.wait_ge(probsT_ready, 2 * (f - 1) + e + 1)
                    for b in range(3):
                        ins = T.transpose(ps[:, M + e, b * P:(b + 1) * P], pb[:, e, b * P:(b + 1) * P], ident[:, :])
                    ins.then_inc(probs_T, 1)
                units(c, 5, NU)
                pe.wait_ge(probsT_ready, 2 * f + 2)
                for e in range(2):
                    o = ps[:, M + 2, e * SEQ:(e + 1) * SEQ]
                    T.matmul(o, vs[:, e, 0, :], pT[:, e, 0:SEQ], start=e == 0, stop=False, skip_group_check=True)
                    ins = T.matmul(o[:, P:SEQ], vs[:, e, 1, :], pT[:, e, SEQ:384], start=False, stop=e == 1,
                                   skip_group_check=True)
                ins.then_inc(fox_done, 1)
            for r in range(4):
                c = C_GATE + r
                units(c, 0, 2)
                pe.wait_ge(rhead_staged, 2 * (r + 1))
                if r == 0:
                    pe.wait_ge(fox_stored, 4)
                    pe.wait_ge(probsT_ready, 8)
                if r:
                    pe.wait_ge(stage_ready, 2 * (ST_RET + r))
                for e in range(2):
                    h = 2 * r + e
                    T.matmul(ps[:, M + 2 + e, 0:SEQ], qs[:, e, 0:P], qkh[:, 16 + h, :], start=True, stop=True)
                    T.matmul(ps[:, M + 2 + e, SEQ:384], qs[:, e, P:SEQ], qkh[:, 16 + h, P:SEQ], start=True,
                             stop=True).then_inc(rscores, 1)
                units(c, 2, 5)
                pe.wait_ge(rdecayed, 2 * (r + 1))
                for e in range(2):
                    h = 2 * r + e
                    cc, o = 2 + h // 4, (h % 4) * HD
                    T.matmul(ps[:, M + 2, e * HD:(e + 1) * HD], pb[:, e, 0:P], val[:, cc, 0, o:o + HD], start=True, stop=True)
                    y1 = ps[:, M + 2, (2 + e) * HD:(3 + e) * HD]
                    T.matmul(y1, pb[:, e, P:SEQ], val[:, cc, 0, o:o + HD], start=True, stop=False)
                    ins = T.matmul(y1, pb[:, e, SEQ:384], val[:, cc, 1, o:o + HD], start=False, stop=True)
                ins.then_inc(ry_done, 1)
                units(c, 5, NU)
                transpose_stage(ST_RET + r, 2)
            for c in range(18, C_MK):
                units(c, 0, 4)
                units(c, 4, NU)
                if c == 20:
                    pe.wait_ge(tstored, 2 * ST_MK)
                    transpose_rows(1, memx, 0, KT)
            for c in (C_MK, C_MV):
                units(c, 0, 6)
                if c == C_MV:
                    transpose_stage(ST_MK)
                units(c, 6, NU)
            for i in range(4):
                units(C_UP + 2 * i, 0, 4, 0, 4)
                if i:
                    transpose_stage(ST_MERGED + i - 1)
                units(C_UP + 2 * i + 1, 0, 4, 8, 4)
            units(C_OUT, 0, 4)
            transpose_stage(ST_MERGED + 3)
            units(C_OUT, 4, NU)
            pe.wait_ge(keys_in, 16)
            for j in range(4):
                if j:
                    units(C_OUT + j, 0, NU)
                if j >= 2:
                    pe.wait_ge(keys_stored, j - 1)
                for b in range(4):
                    ins = T.transpose(ps[:, M + 2 + j % 2, b * P:(b + 1) * P], keys_raw[:, 4 * j + b, :], ident[:, :])
                ins.then_inc(keys_T, 1)
            pe.wait_ge(keys_stored, 4)
            transpose_rows(2, hh, 0, KT)
            pe.wait_ge(rows_lo, 2 * KT)
            units(C_MQ, 0, NU)
            transpose_stage(ST_MQ)
            pe.wait_ge(tstored, 2 * (ST_MQ + 1))
            for g in range(8):
                h, t = g // 2, g % 2
                ins = T.matmul(ps[:, M + h, t * SEQ:(t + 1) * SEQ], qTm[:, h, t * P:(t + 1) * P], kmT[:, h, :], start=True, stop=True)
            ins.then_inc(mlog, 1)
            pe.wait_ge(mprobs, 1)
            pe.wait_ge(evacuated[0], 2 * 19)
            pe.wait_ge(evacuated[1], 2 * 18)
            for h in range(MEMH):
                for m in range(2):
                    for t in range(TT):
                        ins = T.transpose(ps[:, h, m * SEQ + t * P:m * SEQ + (t + 1) * P],
                                          mp[:, 2 * h + t, m * P:(m + 1) * P], ident[:, :])
                ins.then_inc(mpT_done, 1)
            for h in range(MEMH):
                pe.wait_ge(mpT_ready, h + 1)
                o = ps[:, M + h // 2, (h % 2) * SEQ:(h % 2 + 1) * SEQ]
                for m in range(2):
                    ins = T.matmul(o, vm[:, m, h * HD:(h + 1) * HD], mpT[:, h, m, :], start=m == 0, stop=m == 1)
                if h % 2:
                    ins.then_inc(mo_done, 1)
            pe.wait_ge(moT_ready, 2)
            for c in range(C_MO, C_MO + 4):
                units(c, 0, 2, 0, 2)
            transpose_rows(3, hh, 0, KT)
            pe.wait_ge(rowsT_act, NU * 2)
            pe.wait_ge(rowsT_dve, NU * 2)
            pe.wait_ge(evacuated[0], 2 * 21)
            pe.wait_ge(evacuated[1], 2 * 20)

            def scores(q):
                h, half = q // 2, q % 2
                pe.wait_ge(pq_stored, q + 1)
                if half == 0 and h >= 4:
                    pe.wait_ge(scores_read, h - 3)
                for t in range(TT):
                    b = (2 * t + half) * NKEY
                    ins = T.matmul(ps[:, M + h % 4, b:b + NKEY], qTp[:, q, t * P:(t + 1) * P], keysT[:, q, :], start=True, stop=True)
                if half:
                    ins.then_inc(scores_done, 1)

            for cc in range(4):
                if cc >= 2:
                    pe.wait_ge(pq_stored, 4 * (cc - 1))
                for j in range(NRING):
                    m = first_unit(C_MO + 4) // 2 + NRING * cc + j
                    pe.wait_ge(w_ready[m % NRING], 16 * (m // NRING + 1))
                    for n in range(4):
                        for k in range(KPC):
                            first = j == 0 and k == 0
                            ins = T.matmul(ps[:, 2 * (cc % 2) + n // 2, (n % 2) * SEQ:(n % 2 + 1) * SEQ],
                                           raw[:, m % NRING, k, n * P:(n + 1) * P], hT[:, KPC * j + k, :],
                                           start=first and n % 2 == 0, stop=j == NRING - 1 and k == KPC - 1,
                                           skip_group_check=True)
                    if j < NRING - 1:
                        ins.then_inc(raw_used, 1)
                    else:
                        ins.then_inc(pq_done, 1)
                if cc:
                    for q in range(4 * (cc - 1), 4 * cc):
                        scores(q)
            for q in range(12, 16):
                scores(q)
            pe.wait_ge(pq_stored, 16)
            pe.wait_ge(scores_read, PH)
            for tile in range(TT):
                for b in range(4):
                    T.matmul(ps[:, 4 * tile + b, :], ident[:, :], xa[:, tile, b * CW:(b + 1) * CW], start=True, stop=False)

                def pair(p, last):
                    for k in range(NG):
                        pe.wait_ge(diag_ready, p * NG + (tile * PAIRS * NG + k + 1))
                        pe.wait_ge(v_ready[k], p * 16 + 16 * (tile * PAIRS + 1))
                        for b in range(4):
                            ins = T.matmul(ps[:, 4 * tile + b, :], diag[k], vrows[:, k, b * CW:(b + 1) * CW],
                                           start=False, stop=last and k == NG - 1)
                        ins.then_inc(accumulated, 1)
                with pe.Fori(0, PAIRS - 1) as p:
                    pair(p, False)
                pair(PAIRS - 1, True)
                pe.wait_ge(accumulated, (tile + 1) * PAIRS * NG)
                pe.nop().then_inc(tile_done, 1)


def tables():
    f = np.float32
    ident = np.eye(P, dtype=f)
    s = np.arange(P)[:, None]
    tri = (s <= np.arange(SEQ)[None, :]).astype(f)
    q, k = np.arange(P)[:, None], np.arange(P)[None, :]
    causal = np.where(k <= q, 0.0, MASKED).astype(f)
    mask = np.concatenate([causal, np.zeros((P, P), f), causal], axis=1)
    half = HD // 2
    inv = np.exp(-math.log(10000.0) * np.arange(half, dtype=f) / half).astype(f)
    ang = (np.arange(SEQ, dtype=f)[:, None] * inv[None, :]).reshape(TT, P, half).transpose(1, 0, 2)
    rope = np.stack([np.cos(ang.astype(f)), np.sin(ang.astype(f))], axis=1).astype(f)
    lg = np.log1p(-np.exp2(-5.0 - np.arange(RETH, dtype=f))).astype(f)
    i, j = np.arange(SEQ)[None, :], np.arange(SEQ)[:, None]
    dec = np.exp(lg[:, None, None].astype(np.float64) * np.abs(i - j)) * (j // RET_CHUNK <= i // RET_CHUNK)
    dec = np.concatenate([dec[:, 0:P, :], dec[:, P:SEQ, P:SEQ]], axis=2).astype(f)
    delta = np.zeros((40, 8), f)
    delta[np.arange(8), np.arange(8)] = 1
    delta[32 + np.arange(8), np.arange(8)] = 1
    iota = np.tile(np.arange(TOPK, dtype=f), (P, 1))
    return {"t_ident": ident, "t_tri": tri, "t_mask": mask, "t_rope": rope, "t_decay": dec, "t_delta": delta, "t_iota": iota}


_INS = ['x', 'mem', 'ln_mix_g', 'w_in', 'b_forget', 'fox_q_norm_g', 'fox_k_norm_g', 'ret_norm_g', 'w_fox_up',
        'w_ret_up', 'w_out', 'ln_mem_g', 'mem_norm_g', 'w_mq', 'w_mkv', 'mem_q_norm_g', 'mem_k_norm_g', 'w_mo',
        'ln_ffn_g', 'w_peer_q', 'peer_sub_keys', 'peer_u', 'peer_v']


def kernel(**inputs):
    import concourse.bacc as _bacc
    from concourse.bass_utils import run_bass_kernel_spmd as _run

    nc = _bacc.Bacc("TRN2", target_bir_lowering=False, num_devices=1)
    arrays, args = {}, []
    for name, a in [(n, inputs[n]) for n in _INS] + list(tables().items()):
        a = np.ascontiguousarray(a)
        arrays[f"in_{name}"] = a
        args.append(nc.dram_tensor(f"in_{name}", a.shape, mybir.dt.from_np(a.dtype), kind="ExternalInput").ap())
    args.append(nc.dram_tensor("out", (1, SEQ, D), mybir.dt.float32, kind="ExternalOutput").ap())
    build(nc, *args)
    r = _run(nc, [arrays], core_ids=[0])
    return r.results[0]["out"]
```

```python
import math
from contextlib import ExitStack

import numpy as np
import concourse.bass as bass
from concourse import mybir

D = 2048
SEQ = 256
P = 128
TT = SEQ // P
KT = D // P
HD = 128
FOXH = RETH = 8
MEMH = 4
PH = 8
TOPK = 16
NKEY = 128
CW = 512
CH = CW // HD
KU = 2
KPC = 2 * KU
NU = KT // KU
NRING = 4
RET_CHUNK = 64
EPS = 1e-6
MASKED = -1.0e30
LOWEST = -3.0e38
SLOTS = PH * TOPK
NG = 8
GROUPS = SLOTS // NG
AHEAD = 4
LAG = 2

FQ, FK, FV, FF = 0, 1024, 2048, 3072
RQ, RK, RV, RG, GATE = 3080, 4104, 5128, 6152, 7176

C_FV, C_RV, C_GATE, C_MK, C_MV = 8, 10, 14, 22, 23
C_UP, C_OUT, C_MQ, C_MO = 24, 32, 36, 37


def first_unit(c):
    if c <= C_UP:
        return NU * c
    if c <= C_OUT:
        return NU * C_UP + NU // 2 * (c - C_UP)
    if c <= C_MO:
        return NU * C_UP + NU // 2 * 8 + NU * (c - C_OUT)
    return NU * C_UP + NU // 2 * 8 + NU * (C_MO - C_OUT) + 2 * (c - C_MO)


ST_RET, ST_MK, ST_MERGED, ST_MQ = 8, 12, 13, 17


def build(nc, x, mem, ln_mix_g, w_in, b_forget, fox_q_g, fox_k_g, ret_g, w_fox_up, w_ret_up, w_out,
          ln_mem_g, mem_g, w_mq, w_mkv, mem_q_g, mem_k_g, w_mo, ln_ffn_g, w_pq, sub_keys, peer_u, peer_v,
          t_ident, t_tri, t_mask, t_rope, t_decay, t_delta, t_iota, out):
    f32, u32 = mybir.dt.float32, mybir.dt.uint32
    ALU, ACT, AX = mybir.AluOpType, mybir.ActivationFunctionType, mybir.AxisListType
    ds = bass.ds

    with ExitStack() as ctx:
        def sb(name, shape, dt=f32):
            return ctx.enter_context(nc.sbuf_tensor(name, shape, dt))

        def sem(name):
            return ctx.enter_context(nc.semaphore(name))

        f32r = mybir.dt.float32r
        xa = sb("resid", [P, TT, D])
        hh = sb("normed", [P, TT, D])
        oT = xa[:, :, :].rearrange("p t d -> p (t d)").rearrange("p (h t) -> p h t", t=SEQ)
        stage = sb("stage", [P, TT, CW])
        att = sb("att", [P, 2, 2, 384])
        pb, pT = att[:, 0], att[:, 1]
        flat_att = att[:, :, :, :].rearrange("p a b c -> p (a b c)")
        sq = flat_att[:, 0:1024].rearrange("p (t n) -> p t n", n=CW)
        ropeA, ropeB = flat_att[:, 0:CW], flat_att[:, CW:2 * CW]
        qs = sb("head_q", [P, 2, SEQ])
        vs = sb("head_v", [P, 2, TT, HD])
        ident = sb("ident", [P, P])
        tri = sb("tri", [P, SEQ])
        mask = sb("mask", [P, 384])
        rope = sb("rope", [P, 2, TT, HD // 2])
        iota = sb("iota", [P, TOPK])
        delta = sb("delta", [40, 8])
        gains = sb("gains", [P, 3, KT])
        hgain = sb("head_gains", [P, 6])
        rgain = sb("ret_gain", [P, RETH])
        eps = sb("eps", [P, 1])
        root = sb("unused_root", [P, 1])
        ss = sb("sumsq", [P, 4, TT])
        rr = sb("rms", [P, 4, TT])
        ssc = sb("sumsq_chunks", [P, 2, TT, D // CW])
        ssh = sb("head_sumsq", [P, TT, CH])
        wff = sb("w_forget", [P, KT, 8])
        wffs = sb("w_forget_parts", [P, KT, 2, 8], f32r)
        bf = sb("b_forget", [P, 8])
        lf = sb("logf", [P, TT, 40])
        lx = sb("logf_x", [P, TT, 8])
        le = sb("logf_e", [P, TT, 8])
        cq = hh[0:40, 1, 0:SEQ]
        rh = hh[0:40, :, :].rearrange("p t d -> p (t d)")[:, 0:8 * SEQ].rearrange("p (h t) -> p h t", t=SEQ)
        nm = sb("neg_max", [P, 8])
        rs = sb("row_sum", [P, 8])
        bst = sb("bn", [P, 4, 6])
        mv = sb("mean_var", [P, 4, 2])
        idx = sb("expert_idx", [P, TT * SLOTS + NG], u32)
        gate = sb("expert_gate", [P, TT * PH, TOPK])
        ibu = sb("idx_u", [P, 2 * NG], u32)
        ibv = sb("idx_v", [P, 2 * NG], u32)
        acts = sb("acts", [P, 2, NG])
        gel = tri
        wgt = sb("weights", [P, NG])
        diag = [stage[:, s // 4, (s % 4) * P:(s % 4 + 1) * P] for s in range(NG)]
        tv = flat_att[:, 0:64].rearrange("p (q k) -> p q k", k=TOPK)
        tif = flat_att[:, 64:128].rearrange("p (t h k) -> p t h k", h=2, k=TOPK)
        af = flat_att[:, 128:160]
        bfl = flat_att[:, 160:192]
        e0 = flat_att[:, 192:224]
        e1 = flat_att[:, 224:256]
        tmp = flat_att[:, 256:768].rearrange("p (q k) -> p q k", k=NKEY)
        cand = flat_att[:, 768:1280].rearrange("p (t k) -> p t k", k=256)
        tmp2 = qs[:, :, :]
        eq = vs[:, :, :, :].rearrange("p a b c -> p (a b c)").rearrange("p (j a) -> p j a", a=TOPK)
        ti = sb("top_idx", [P, 4, TOPK], u32)
        pos = sb("top_pos", [P, TT, TOPK], u32)
        pab = sb("pos_ab", [P, 2, TT * TOPK], u32)
        gsum = sb("gate_sum", [P, TT * PH])

        with ExitStack() as early:
            def esb(name, shape, dt=f32):
                return early.enter_context(nc.sbuf_tensor(name, shape, dt))
            raw = esb("weight_ring", [P, NRING, KPC, CW])
            ws = esb("weight_parts", [P, 2, NRING, KU, CW], f32r)
            hTs = esb("rowsT_parts", [P, 2, KT, SEQ], f32r)
            big = esb("big", [P, 14336])
        rows = sb("expert_rows", [P, 16, D])
        urows = [rows[:, 4 + k, :] for k in range(NG)]
        vrows = [rows[:, k if k < 4 else k + 8, :] for k in range(NG)]
        ws_hi, hT_hi = ws[:, 0].bitcast(f32), hTs[:, 0].bitcast(f32)
        qk = big[:, 0:8192].rearrange("p (c n) -> p c n", n=CH * SEQ)
        qkh = big[:, 0:8192].rearrange("p (h t) -> p h t", t=SEQ)
        xin = big[:, 0:4096].rearrange("p (t d) -> p t d", d=D)
        val = big[:, 8192:14336].rearrange("p (c t n) -> p c t n", t=TT, n=CW)
        gatesA = hh[:, :, :].rearrange("p t d -> p (t d)").rearrange("p (c t n) -> p c t n", t=TT, n=CW)
        gatesB = big[:, 4096:8192].rearrange("p (c t n) -> p c t n", t=TT, n=CW)
        memx = big[:, 0:4096].rearrange("p (t d) -> p t d", d=D)
        memT = big[:, 8192:12288].rearrange("p (k t) -> p k t", t=SEQ)
        mem_junk = big[:, 8192:12288].rearrange("p (t d) -> p t d", d=D)
        kmT = big[:, 12288:13312].rearrange("p (h t) -> p h t", t=SEQ)
        vm = big[:, 13312:14336].rearrange("p (t n) -> p t n", n=CW)
        keys_raw = big[:, 0:2048].rearrange("p (h d) -> p h d", d=HD)
        keysT = big[:, 2048:4096].rearrange("p (h d) -> p h d", d=NKEY)
        qTm = big[:, 8192:9216].rearrange("p (h t) -> p h t", t=SEQ)
        mp = big[:, 4096:6144].rearrange("p (g m) -> p g m", m=SEQ)
        mpT = big[:, 6144:8192].rearrange("p (h m q) -> p h m q", m=2, q=SEQ)
        qTp = [big[:, (0 if q < 4 else 4096) + q * SEQ:][:, 0:SEQ] for q in range(2 * PH)]
        ffn_gain = big[:, 0:2048]
        ffn_junk = big[:, 8192:12288].rearrange("p (t d) -> p t d", d=D)
        scores1 = big[:, 12288:14336].rearrange("p (h n) -> p h n", n=2 * NKEY)
        pq_beside = {p: big[:, a:a + KPC * CW].rearrange("p (k n) -> p k n", n=CW)
                     for p, a in ((3, 4096), (4, 12288), (5, 6144))}
        hT = memT
        mergedT = memT
        ps = ctx.enter_context(nc.psum_tensor("ps", [P, 8, CW], f32))
        M = 4

        first_in, tables_in, mem_in, keys_in, ffg_in = (sem(n) for n in
            ("first_in", "tables_in", "mem_in", "keys_in", "ffg_in"))
        x_in = [sem("x_in0"), sem("x_in1")]
        pq_in = {p: sem(f"pq_in{p}") for p in pq_beside}
        decay_in = [sem("decay_in0"), sem("decay_in1")]
        w_ready = [sem(f"w_ready{s}") for s in range(4)]
        projected, units_used = sem("projected"), sem("units_used")
        hi_ready, lo_ready, raw_used = sem("hi_ready"), sem("lo_ready"), sem("raw_used")
        rows_hi, rows_lo, src_hi, src_lo = sem("rows_hi"), sem("rows_lo"), sem("src_hi"), sem("src_lo")
        wff_hi, wff_lo = sem("wff_hi"), sem("wff_lo")
        evacuated = [sem("evacuated0"), sem("evacuated1")]
        eps_set, hgain_ready = sem("eps_set"), sem("hgain_ready")
        chunk_ss, ss_summed = sem("chunk_ss"), sem("ss_summed")
        norm_ss, norm_rms, norm_ready = sem("norm_ss"), sem("norm_rms"), sem("norm_ready")
        rows_T, rowsT_dve, rowsT_act = sem("rows_T"), sem("rowsT_dve"), sem("rowsT_act")
        sq_ready, ssq_ready, rms_ready = sem("sq_ready"), sem("ssq_ready"), sem("rms_ready")
        stage_ready, transposed, tstored = sem("stage_ready"), sem("transposed"), sem("tstored")
        ff_done, lf_x, lf_e, lf_ready, cum_done, cum_ready = (sem(n) for n in
            ("ff_done", "lf_x", "lf_e", "lf_ready", "cum_done", "cum_ready"))
        head_staged, logits_done, masked, exped, probs_ready = (sem(n) for n in
            ("head_staged", "logits_done", "masked", "exped", "probs_ready"))
        probs_T, probsT_ready, fox_done, fox_stored = (sem(n) for n in
            ("probs_T", "probsT_ready", "fox_done", "fox_stored"))
        rhead_staged, rscores, rdecayed, ry_done, rvar, rstd = (sem(n) for n in
            ("rhead_staged", "rscores", "rdecayed", "ry_done", "rvar", "rstd"))
        x_again = sem("x_again")
        x1_ready, keys_T, keys_stored = sem("x1_ready"), sem("keys_T"), sem("keys_stored")
        mlog, mmax, mexp, mprobs, mpT_done, mpT_ready, mo_done, moT_ready = (sem(n) for n in
            ("mlog", "mmax", "mexp", "mprobs", "mpT_done", "mpT_ready", "mo_done", "moT_ready"))
        moT_hi = sem("moT_hi")
        pq_first = sem("pq_first")
        pq_done, pq_stored, scores_done, scores_read = (sem(n) for n in
            ("pq_done", "pq_stored", "scores_done", "scores_read"))
        sfin_ready, gexp, gate_ready, routed = (sem(n) for n in ("sfin_ready", "gexp", "gate_ready", "routed"))
        idxu_staged, idxv_staged = sem("idxu_staged"), sem("idxv_staged")
        scores1_stored = sem("scores1_stored")
        u_ready = [sem(f"u_ready{s}") for s in range(8)]
        v_ready = [sem(f"v_ready{s}") for s in range(8)]
        dotted, gelued, weighted, diag_ready, accumulated = (sem(n) for n in
            ("dotted", "gelued", "weighted", "diag_ready", "accumulated"))
        bank_done, out_ready, stored = sem("bank_done"), sem("out_ready"), sem("stored")
        dve_step, act_step = sem("dve_step"), sem("act_step")

        class Steps:
            def __init__(self, eng, s):
                self.eng, self.s, self.n = eng, s, 0

            def mark(self, ins):
                ins.then_inc(self.s, 1)
                self.n += 1
                return ins

            def settle(self):
                self.eng.wait_ge(self.s, self.n)

            def link(self, ins):
                self.mark(ins)
                self.settle()

        block = ctx.enter_context(nc.Block())

        def wait_chunk(eng, c, t):
            if t == 0:
                eng.wait_ge(projected, c + 1)
            else:
                eng.wait_ge(units_used, first_unit(c + 1))

        def pq_place(p):
            if p in pq_beside:
                return pq_beside[p], pq_in[p], 16
            m = first_unit(C_MO + 4) // 2 + p - (len(pq_beside) if p > max(pq_beside) else 0)
            return raw[:, m % NRING], w_ready[m % NRING], 16 * (m // NRING + 1)

        def pq_used(p):
            return (pq_done, p // NRING + 1) if p % NRING == NRING - 1 else (raw_used, 3 * (p // NRING) + p % NRING + 1)

        def cols(w, rows0, kt, c0, n):
            v = w[0, rows0:rows0 + kt * P, :].rearrange("(k p) n -> p k n", p=P)
            return v[:, :, ds(c0, n)] if not isinstance(c0, int) else v[:, :, c0:c0 + n]

        @block.sync
        def _(sp):
            for t in range(TT):
                sp.dma_start(xin[:, t, :], x[0, t * P:(t + 1) * P, :]).then_inc(x_in[t], 16)

            def load_chunk(w, c, col, first=False):
                for j in range(NRING):
                    if not first:
                        sp.wait_ge(lo_ready, NU * c + (2 * j + 2 - NU))
                    sp.dma_start(raw[:, j], cols(w, j * KPC * P, KPC, col, CW)).then_inc(w_ready[j], 16)

            load_chunk(w_in, 0, FQ, first=True)
            for dst, src in ((tri[:, :], t_tri), (mask[:, :], t_mask),
                             (rope[:, :, :, :], t_rope), (iota[:, :], t_iota), (delta[:, :], t_delta),
                             (bf[:, :], b_forget[0:1, :].to_broadcast([P, 8])),
                             (wff[:, :, :], w_in[0, :, FF:FF + 8].rearrange("(k p) n -> p k n", p=P)),
                             (gains[:, 1, :], mem_g[0].rearrange("(k p) -> p k", p=P)),
                             (gains[:, 2, :], ln_mem_g[0].rearrange("(k p) -> p k", p=P)),
                             (hgain[:, 0:1], fox_q_g.rearrange("o p -> p o")),
                             (hgain[:, 1:2], fox_k_g.rearrange("o p -> p o")),
                             (hgain[:, 4:5], mem_k_g.rearrange("o p -> p o")),
                             (hgain[:, 5:6], mem_q_g.rearrange("o p -> p o")),
                             (rgain[:, :], ret_g[0].rearrange("(h p) -> p h", p=P))):
                sp.dma_start(dst, src, allow_slow_non_contiguous=True).then_inc(tables_in, 16)
            with sp.Fori(1, 4) as c:
                load_chunk(w_in, c, c * CW + FQ)
            with sp.Fori(0, 4) as i:
                load_chunk(w_in, i + 4, i * CW + RQ)
            for i in range(2):
                load_chunk(w_in, C_FV + i, FV + i * CW)
            with sp.Fori(0, 12) as i:
                load_chunk(w_in, i + C_RV, i * CW + RV)
            for i in range(2):
                load_chunk(w_mkv, C_MK + i, i * CW)
            m = first_unit(C_UP) // 2

            def piece(m, src):
                sp.wait_ge(lo_ready, 2 * m - 6)
                sp.dma_start(raw[:, m % NRING], src).then_inc(w_ready[m % NRING], 16)

            for c in range(C_UP, C_OUT):
                for j in range(2):
                    piece(m, cols(w_ret_up if c % 2 else w_fox_up, j * KPC * P, KPC, (c - C_UP) // 2 * CW, CW))
                    m += 1
                if c == C_UP + 3:
                    sp.wait_ge(src_lo, 16)
                    for t in range(TT):
                        sp.dma_start(xa[:, t, :], x[0, t * P:(t + 1) * P, :]).then_inc(x_again, 16)
            for c in range(C_OUT, C_MO):
                for j in range(NRING):
                    w, col = (w_out, (c - C_OUT) * CW) if c < C_MQ else (w_mq, 0)
                    piece(m, cols(w, j * KPC * P, KPC, col, CW))
                    m += 1
            for c in range(C_MO, C_MO + 4):
                piece(m, cols(w_mo, 0, KPC, (c - C_MO) * CW, CW))
                m += 1
            for p in (0, 1, 3, 4, 5, 2, 6):
                if p == 3:
                    sp.wait_ge(mpT_done, MEMH)
                elif p == 4:
                    sp.wait_ge(mo_done, 2)
                elif p != 5:
                    sp.wait_ge(lo_ready, 2 * (m + min(p, 3)) - 6)
                dst, done, _ = pq_place(p)
                sp.dma_start(dst, cols(w_pq, p % NRING * KPC * P, KPC, p // NRING * CW, CW)).then_inc(done, 16)
            for p in range(7, 4 * NRING):
                sp.wait_ge(*pq_used(p - 7 if p < 10 else p - 4))
                dst, done, _ = pq_place(p)
                sp.dma_start(dst, cols(w_pq, p % NRING * KPC * P, KPC, p // NRING * CW, CW)).then_inc(done, 16)
            for t in range(TT):
                for half in range(2):
                    sp.wait_ge(out_ready, 4 * t + 2 * half + 2)
                    a, b = half * D // 2, (half + 1) * D // 2
                    sp.dma_start(out[0, t * P:(t + 1) * P, a:b], xa[:, t, a:b]).then_inc(stored, 16)
            sp.wait_ge(stored, 2 * 16 * TT)

        @block.gpsimd
        def _(pool):
            pool.wait_ge(fox_stored, 4)
            for h in range(RETH):
                if h >= 2:
                    pool.wait_ge(rdecayed, h - 1)
                pool.dma_start(pT[:, h % 2, :], t_decay[h]).then_inc(decay_in[h % 2], 16)
                if h == 1:
                    for t in range(TT):
                        pool.dma_start(memx[:, t, :], mem[0, t * P:(t + 1) * P, :]).then_inc(mem_in, 16)
            pool.wait_ge(rows_T, KT)
            pool.dma_start(keys_raw[:, :, :], sub_keys[0].rearrange("h q k d -> k (h q) d")).then_inc(keys_in, 16)
            pool.wait_ge(keys_T, 4)
            pool.dma_start(ffn_gain, ln_ffn_g[0:1, :].to_broadcast([P, D])).then_inc(ffg_in, 16)

            def gather(dst, table, index, done):
                pool.indirect_dma_start(out=dst, out_offset=None, in_=table[0],
                                        in_offset=bass.IndirectOffsetOnAxis(ap=index, axis=0)).then_inc(done, 16)

            def column(n):
                return idx[:, n:n + 1] if isinstance(n, int) else idx[:, ds(n, 1)]

            def v_step(m, j, first):
                if not first:
                    pool.wait_ge(accumulated, m - (NG - 1))
                pool.wait_ge(idxv_staged, m + 1)
                pool.tensor_copy(ibv[:, (j + 1) % 16:(j + 1) % 16 + 1], column(m + 1)).then_inc(idxv_staged, 1)
                gather(vrows[j % NG], peer_v, ibv[:, j:j + 1], v_ready[j % NG])

            def u_step(n, j, i=None):
                if not isinstance(n, int) or n >= NG:
                    pool.wait_ge(dotted, n - (NG - 1))
                if not isinstance(n, int):
                    pool.wait_ge(routed, i + (2 if j == 15 else 1))
                elif j == 15:
                    pool.wait_ge(routed, n // 16 + 2)
                pool.wait_ge(idxu_staged, n + 1)
                pool.tensor_copy(ibu[:, (j + 1) % 16:(j + 1) % 16 + 1], column(n + 1)).then_inc(idxu_staged, 1)
                gather(urows[j % NG], peer_u, ibu[:, j:j + 1], u_ready[j % NG])

            pool.wait_ge(routed, 1)
            pool.memset(idx[:, TT * SLOTS:], 0)
            pool.tensor_copy(ibv[:, 0:1], idx[:, 0:1]).then_inc(idxv_staged, 1)
            pool.tensor_copy(ibu[:, 0:1], idx[:, 0:1]).then_inc(idxu_staged, 1)
            for n in range(AHEAD * NG):
                u_step(n, n % 16)

            pool.wait_ge(scores_done, PH)
            n_u = (AHEAD - LAG) * NG
            for m in range(4):
                v_step(m, m, True)
            for j in range(n_u):
                u_step(AHEAD * NG + j, j)
                for m in range(2 * j + 4, min(2 * j + 6, 2 * n_u)):
                    v_step(m, m % 16, m < NG)
            with pool.Fori((2 * AHEAD - LAG) * NG // 16, TT * SLOTS // 16) as i:
                for j in range(16):
                    u_step(16 * i + j, j, i)
                    v_step(16 * i + (j - LAG * NG), j, False)
            for j in range(LAG * NG):
                v_step(TT * SLOTS - LAG * NG + j, j % 16, False)

        @block.scalar
        def _(act):
            st = Steps(act, act_step)
            for dst, src in ((ident[:, :], t_ident), (gains[:, 0, :], ln_mix_g[0].rearrange("(k p) -> p k", p=P))):
                act.dma_start(dst, src, allow_slow_non_contiguous=True).then_inc(first_in, 16)

            def split_w(a, b):
                for n in range(a, b):
                    if n % 2 == 0:
                        act.wait_ge(w_ready[n // 2 % NRING], 16 * (n // 2 // NRING + 1))
                    if n >= NRING:
                        act.wait_ge(units_used, n - NRING + 1)
                    nc.scalar.activation(ws[:, 0, n % NRING], raw[:, n // 2 % NRING, n % 2 * KU:(n % 2 + 1) * KU],
                                         ACT.Copy).then_inc(hi_ready, 1)

            def split_src(q, u, src, last):
                act.wait_ge(units_used, last + 1)
                nc.scalar.activation(hTs[:, 0, 2 * u:2 * u + 2, :], src[:, 2 * u:2 * u + 2, :], ACT.Copy).then_inc(src_hi, 1)

            def load_roots():
                nc.scalar.activation(root[:, :], eps[:, :], ACT.Sqrt)

            def norm(n, src, junk, ready, value):
                for t in range(TT):
                    act.wait_ge(ready[t], value[t])
                    st.link(nc.scalar.activation(junk[:, t, :], src[:, t, :], ACT.Square,
                                                 accum_out=ss[:, n, t:t + 1]))
                    nc.scalar.activation(rr[:, n, t:t + 1], ss[:, n, t:t + 1], ACT.Sqrt, bias=eps[:, :],
                                         scale=1.0 / D).then_inc(norm_rms, 1)

            def square_rows(n, i, junk):
                for t in range(TT):
                    act.wait_ge(x1_ready, 8 * (n - 2) + 2 * i + t + 1)
                    nc.scalar.activation(junk[:, t, i * CW:(i + 1) * CW], xa[:, t, i * CW:(i + 1) * CW], ACT.Square,
                                         accum_out=ssc[:, n - 2, t, i:i + 1]).then_inc(chunk_ss, 1)

            def root_rows(n):
                for t in range(TT):
                    act.wait_ge(ss_summed, 2 * (n - 2) + t + 1)
                    nc.scalar.activation(rr[:, n, t:t + 1], ss[:, n, t:t + 1], ACT.Sqrt, bias=eps[:, :],
                                         scale=1.0 / D).then_inc(norm_rms, 1)

            def store_rowsT_hi(n, gain):
                for k in range(KT):
                    if k % 2 == 0:
                        act.wait_ge(rows_T, (n * KT + k) // 2 + 1)
                    nc.scalar.activation(hTs[:, 0, k, :], ps[:, M + k // 2 % 4, (k % 2) * SEQ:(k % 2 + 1) * SEQ], ACT.Copy,
                                         scale=gains[:, gain, k:k + 1]).then_inc(rows_hi, 1)

            def store_rowsT(n, dst, gain):
                for k in range(KT):
                    if k // 2 % 2 == 0:
                        continue
                    if k % 2 == 0:
                        act.wait_ge(rows_T, (n * KT + k) // 2 + 1)
                    src = ps[:, M + k // 2 % 4, (k % 2) * SEQ:(k % 2 + 1) * SEQ]
                    nc.scalar.activation(dst[:, k, :], src, ACT.Copy,
                                         scale=1.0 if gain is None else gains[:, gain, k:k + 1]).then_inc(rowsT_act, 1)

            def square_chunk(c, s):
                for t in range(TT):
                    wait_chunk(act, c, t)
                    if s >= 1:
                        act.wait_ge(ssq_ready, 2 * (s - 1) + t + 1)
                    nc.scalar.activation(sq[:, t, :], ps[:, 2 * (c % 2) + t, :], ACT.Square).then_inc(sq_ready, 1)
                    act.wait_ge(ssq_ready, 2 * s + t + 1)
                    nc.scalar.activation(ssh[:, t, :], ssh[:, t, :], ACT.Sqrt, bias=eps[:, :],
                                         scale=1.0 / HD).then_inc(rms_ready, 1)

            def store_stage(s, dst, gain):
                for t in range(TT):
                    act.wait_ge(transposed, 2 * s + t + 1)
                    nc.scalar.activation(dst[:, :, t * P:(t + 1) * P],
                                         ps[:, M + t, :].rearrange("p (h q) -> p h q", q=P), ACT.Copy,
                                         scale=gain).then_inc(tstored, 1)

            def copy_chunk(c, dst, func):
                for t in range(TT):
                    wait_chunk(act, c, t)
                    nc.scalar.activation(dst[:, t, :], ps[:, 2 * (c % 2) + t, :], func).then_inc(evacuated[c % 2], 1)

            def store_qk(c):
                store_stage(c, qk[:, c].rearrange("p (h t) -> p h t", t=SEQ), hgain[:, c // 2:c // 2 + 1])

            def stage_fox_heads(f):
                if f == 0:
                    act.wait_ge(tstored, 16)
                    act.wait_ge(evacuated[0], 2 * 5)
                    act.wait_ge(evacuated[1], 2 * 5)
                for e in range(2):
                    h = 2 * f + e
                    nc.scalar.activation(qs[:, e, :], qkh[:, h, :], ACT.Copy).then_inc(head_staged, 1)
                    nc.scalar.activation(vs[:, e], val[:, h // 4, :, (h % 4) * HD:(h % 4 + 1) * HD],
                                         ACT.Copy).then_inc(head_staged, 1)

            def stage_ret_heads(r):
                if r == 0:
                    act.wait_ge(evacuated[0], 2 * 7)
                    act.wait_ge(evacuated[1], 2 * 7)
                else:
                    act.wait_ge(rscores, 2 * r)
                for e in range(2):
                    nc.scalar.activation(qs[:, e, :], qkh[:, 24 + 2 * r + e, :], ACT.Copy).then_inc(rhead_staged, 1)

            def store_keys(k):
                act.wait_ge(keys_T, k + 1)
                nc.scalar.activation(keysT[:, 4 * k:4 * k + 4, :],
                                     ps[:, M + 2 + k % 2, :].rearrange("p (h q) -> p h q", q=P),
                                     ACT.Copy).then_inc(keys_stored, 1)

            act.wait_ge(eps_set, 1)
            load_roots()
            norm(0, xin, hh, x_in, (16, 16))
            split_w(0, 2)
            act.wait_ge(first_in, 2 * 16)
            store_rowsT_hi(0, 0)
            split_w(2, NRING)
            act.wait_ge(tables_in, 14 * 16)
            nc.scalar.activation(wffs[:, :, 0, :], wff[:, :, :], ACT.Copy).then_inc(wff_hi, 1)
            act.wait_ge(hgain_ready, 1)
            for c in range(C_RV):
                u = NU * c
                split_w(u + 4, u + 10)
                if 1 <= c <= 8:
                    store_qk(c - 1)
                split_w(u + 10, u + 12)
                if c < 4:
                    square_chunk(c, c)
                if c == 8:
                    act.wait_ge(lf_x, 1)
                    st.link(nc.scalar.activation(le[:, :, :], lx[:, :, :], ACT.Abs))
                    st.link(nc.scalar.activation(le[:, :, :], le[:, :, :], ACT.Exp, scale=-1.0))
                    nc.scalar.activation(le[:, :, :], le[:, :, :], ACT.Ln, bias=1.0).then_inc(lf_e, 1)
                if c >= C_FV:
                    copy_chunk(c, val[:, c - C_FV], ACT.Copy)
            stage_fox_heads(0)
            for f in range(4):
                c = C_RV + f
                u = NU * c
                split_w(u + 4, u + 6)
                for e in range(2):
                    act.wait_ge(masked, 2 * f + e + 1)
                    for t, (a, b) in enumerate(((0, 128), (128, 384))):
                        nc.scalar.activation(pb[:, e, a:b], pb[:, e, a:b], ACT.Exp, bias=nm[:, 2 * e + t:2 * e + t + 1],
                                             accum_out=rs[:, 2 * e + t:2 * e + t + 1]).then_inc(exped, 1)
                split_w(u + 6, u + 9)
                for e in range(2):
                    act.wait_ge(probs_T, 2 * f + e + 1)
                    if f:
                        act.wait_ge(fox_done, f)
                    nc.scalar.activation(pT[:, e, :], ps[:, M + e, 0:384], ACT.Copy).then_inc(probsT_ready, 1)
                split_w(u + 9, u + 12)
                copy_chunk(c, val[:, 2 + f], ACT.Copy if f < 2 else ACT.Silu)
                act.wait_ge(fox_done, f + 1)
                nc.scalar.activation(oT[:, 2 * f:2 * f + 2, :], ps[:, M + 2, :].rearrange("p (e q) -> p e q", q=SEQ),
                                     ACT.Copy).then_inc(fox_stored, 1)
                if f < 3:
                    stage_fox_heads(f + 1)
            stage_ret_heads(0)
            for r in range(4):
                c = C_GATE + r
                u = NU * c
                split_w(u + 4, u + 9)
                act.wait_ge(rvar, r + 1)
                nc.scalar.activation(mv[:, :, 1:2], mv[:, :, 1:2], ACT.Sqrt, bias=eps[:, :]).then_inc(rstd, 1)
                split_w(u + 9, u + 12)
                copy_chunk(c, gatesA[:, r], ACT.Sigmoid)
                for t in range(TT):
                    act.wait_ge(transposed, 2 * (ST_RET + r) + t + 1)
                    for e in range(2):
                        h = 2 * r + e
                        ins = nc.scalar.activation(oT[:, RETH + h, t * P:(t + 1) * P],
                                                   ps[:, M + t, e * P:(e + 1) * P], ACT.Copy, scale=rgain[:, h:h + 1])
                        if e == 0:
                            st.mark(ins)
                    ins.then_inc(tstored, 1)
                if r < 3:
                    stage_ret_heads(r + 1)
            for c in range(18, C_UP):
                u = NU * c
                if c == C_MV:
                    st.settle()
                    act.wait_ge(tstored, 2 * (ST_RET + 4))
                    act.wait_ge(fox_stored, 4)
                for i in range(NU):
                    split_w(u + 4 + i, u + 5 + i)
                    if c == 21:
                        act.wait_ge(rowsT_dve, NU)
                        act.wait_ge(rowsT_act, NU)
                        split_src(0, i, memT, u + i)
                    if c == C_MV:
                        split_src(1, i, oT, u + i)
                    if c == C_MV and i == 5:
                        store_stage(ST_MK, kmT, hgain[:, 4:5])
                if c < C_MK:
                    copy_chunk(c, gatesB[:, c - 18], ACT.Sigmoid)
                if c == 18:
                    norm(1, memx, mem_junk, (mem_in, mem_in), (16 * TT, 16 * TT))
                if c == 20:
                    store_rowsT(1, memT, 1)
                if c == C_MK:
                    square_chunk(c, 4)
                if c == C_MV:
                    copy_chunk(c, vm, ACT.Copy)

            def store_merged(i):
                store_stage(ST_MERGED + i, mergedT[:, 4 * i:4 * i + 4, :], 1.0)

            for c in range(C_UP, C_OUT):
                u = first_unit(c)
                for i in range(4):
                    split_w(u + 4 + i, u + 5 + i)
                    if c == C_OUT - 1:
                        if i == 0:
                            act.wait_ge(tstored, 2 * (ST_MERGED + 3))
                        split_src(2, i, mergedT, u - 1)
                if c > C_UP and c % 2 == 0:
                    store_merged((c - C_UP) // 2 - 1)
            for i in range(4, 6):
                split_src(2, i, mergedT, first_unit(C_OUT) - 1)
            for c in range(C_OUT, C_MQ):
                u = first_unit(c)
                split_w(u + 4, u + 8)
                if c == C_OUT:
                    store_merged(3)
                    act.wait_ge(tstored, 2 * (ST_MERGED + 4))
                    for i in range(6, 8):
                        split_src(2, i, mergedT, first_unit(C_OUT) - 1)
                else:
                    store_keys(c - C_OUT - 1)
                    square_rows(2, c - C_OUT - 1, hh)
                split_w(u + 8, u + 12)
            store_keys(3)
            square_rows(2, 3, hh)
            root_rows(2)
            store_rowsT_hi(2, 2)
            u = first_unit(C_MQ)
            split_w(u + 4, u + 11)
            square_chunk(C_MQ, 5)
            split_w(u + 11, u + 12)
            store_stage(ST_MQ, qTm, hgain[:, 5:6])
            for g in range(8):
                act.wait_ge(mmax, g // 2 + 1)
                nc.scalar.activation(mp[:, g, :], ps[:, M + g // 2, (g % 2) * SEQ:(g % 2 + 1) * SEQ], ACT.Exp,
                                     bias=nm[:, g:g + 1], accum_out=rs[:, g:g + 1]).then_inc(mexp, 1)
            for h in range(MEMH):
                act.wait_ge(mpT_done, h + 1)
                nc.scalar.activation(mpT[:, h], ps[:, h, :].rearrange("p (m q) -> p m q", q=SEQ),
                                     ACT.Copy).then_inc(mpT_ready, 1)
            for j in range(2):
                act.wait_ge(mo_done, j + 1)
                nc.scalar.activation(hTs[:, 0, 2 * j:2 * j + 2, :], ps[:, M + j, :].rearrange("p (e q) -> p e q", q=SEQ),
                                     ACT.Copy).then_inc(moT_hi, 1)
            load_roots()
            split_w(first_unit(C_MO) + 4, first_unit(C_MO) + 8)
            for i in range(4):
                square_rows(3, i, ffn_junk)
            root_rows(3)
            store_rowsT(3, hT, None)

            def store_queries(cc):
                for q in range(4 * cc, 4 * cc + 4):
                    if q == 0:
                        act.wait_ge(pq_first, 1)
                    elif q % 4 == 0 or q == 2:
                        act.wait_ge(pq_done, cc + 1)
                    b = 2 * (cc % 2) + q % 4 // 2
                    nc.scalar.activation(qTp[q], ps[:, b, (q % 2) * SEQ:(q % 2 + 1) * SEQ],
                                         ACT.Copy).then_inc(pq_stored, 1)
                for h in range(2 * cc, 2 * cc + 2):
                    if h == 0:
                        act.wait_ge(*pq_used(4))
                    act.wait_ge(scores_done, h + 1)
                    nc.scalar.activation(scores1[:, h, :], ps[:, M + 2 + h % 2, 0:2 * NKEY], ACT.Copy).then_inc(scores1_stored, 1)

            def act_gelu(g, par):
                act.wait_ge(dotted, NG * g + NG)
                dst = gel[:, g * NG:(g + 1) * NG] if isinstance(g, int) else gel[:, ds(g * NG, NG)]
                nc.scalar.activation(dst, acts[:, par, :], ACT.Gelu_apprx_tanh).then_inc(gelued, 1)

            gates = gate[:, :, :].rearrange("p h k -> p (h k)")

            def act_weights(g):
                act.wait_ge(gelued, g + 1)
                if not (isinstance(g, int) and g == 0):
                    act.wait_ge(diag_ready, NG * g)
                for k in range(NG):
                    n = g * NG + k
                    a, b = (gel[:, n:n + 1], gates[:, n:n + 1]) if isinstance(n, int) else (gel[:, ds(n, 1)], gates[:, ds(n, 1)])
                    nc.scalar.activation(wgt[:, k:k + 1], a, ACT.Copy, scale=b).then_inc(weighted, 1)
                for k in range(NG):
                    act.wait_ge(weighted, g * NG + k + 1)
                    if not (isinstance(g, int) and g == 0):
                        act.wait_ge(accumulated, (g - 1) * NG + k + 1)
                    nc.scalar.activation(diag[k], ident[:, :], ACT.Copy, scale=wgt[:, k:k + 1]).then_inc(diag_ready, 1)

            def gate_exp(t):
                act.wait_ge(sfin_ready, t + 1)
                nc.scalar.activation(gate[:, t * PH:(t + 1) * PH, :], gate[:, t * PH:(t + 1) * PH, :],
                                     ACT.Exp).then_inc(gexp, 1)

            store_queries(0)
            store_queries(1)
            act_gelu(0, 0)
            store_queries(2)
            act_gelu(1, 1)
            store_queries(3)
            act_gelu(2, 0)
            gate_exp(0)
            act_gelu(3, 1)
            act.wait_ge(gate_ready, 1)
            for g in range(AHEAD):
                act_weights(g)
                if g % 2:
                    act_gelu(AHEAD + g // 2, g // 2)
            for g in range(AHEAD, 2 * AHEAD):
                act_weights(g)
                if g + LAG == 2 * AHEAD:
                    gate_exp(1)
                act_gelu(g + LAG, g % 2)
            act.wait_ge(gate_ready, 2)
            with act.Fori(AHEAD, (TT * GROUPS - LAG) // 2) as i:
                for par in range(2):
                    act_weights(2 * i + par)
                    act_gelu(2 * i + (LAG + par), par)
            with act.Fori(TT * GROUPS - LAG, TT * GROUPS) as g:
                act_weights(g)
            for tile in range(TT):
                for b in range(4):
                    act.wait_ge(*((bank_done, 3 * tile + b + 1) if b < 3 else (accumulated, (tile + 1) * SLOTS)))
                    nc.scalar.activation(xa[:, tile, b * CW:(b + 1) * CW], ps[:, 4 * tile + b, :],
                                         ACT.Copy).then_inc(out_ready, 1)

        @block.vector
        def _(dve):
            V = nc.vector
            st = Steps(dve, dve_step)
            V.memset(eps[:, :], EPS).then_inc(eps_set, 1)
            st.mark(V.memset(lf[:, :, :], 0.0))
            st.mark(V.memset(hgain[:, 2:3], 1.0))
            st.mark(V.memset(hgain[:, 3:4], HD ** -0.5))

            def split_w(a, b):
                for n in range(a, b):
                    dve.wait_ge(hi_ready, n + 1)
                    V.tensor_tensor(ws[:, 1, n % NRING], raw[:, n // 2 % NRING, n % 2 * KU:(n % 2 + 1) * KU],
                                    ws_hi[:, n % NRING], ALU.subtract).then_inc(lo_ready, 1)

            def split_src(q, u, src):
                dve.wait_ge(src_hi, NU * q + u + 1)
                V.tensor_tensor(hTs[:, 1, 2 * u:2 * u + 2, :], src[:, 2 * u:2 * u + 2, :], hT_hi[:, 2 * u:2 * u + 2, :],
                                ALU.subtract).then_inc(src_lo, 1)

            def store_rowsT_lo(n, gain):
                for k in range(KT):
                    dve.wait_ge(rows_hi, KT * (n // 2) + (k | 1) + 1)
                    V.scalar_tensor_tensor(hTs[:, 1, k, :], ps[:, M + k // 2 % 4, (k % 2) * SEQ:(k % 2 + 1) * SEQ],
                                           gains[:, gain, k:k + 1], hT_hi[:, k, :], ALU.mult,
                                           ALU.subtract).then_inc(rows_lo, 1)

            def sum_squares(n):
                for t in range(TT):
                    dve.wait_ge(chunk_ss, 8 * (n - 2) + 6 + t + 1)
                    V.tensor_reduce(ss[:, n, t:t + 1], ssc[:, n - 2, t, :], AX.X, ALU.add).then_inc(ss_summed, 1)

            def norm(n, src, dst):
                for t in range(TT):
                    dve.wait_ge(norm_rms, 2 * n + t + 1)
                    st.link(V.reciprocal(rr[:, n, t:t + 1], rr[:, n, t:t + 1]))
                    V.tensor_scalar(dst[:, t, :], src[:, t, :], rr[:, n, t:t + 1], None, ALU.mult).then_inc(norm_ready, 1)

            def store_rowsT(n, dst, gain):
                for k in range(KT):
                    if k // 2 % 2:
                        continue
                    if k % 2 == 0:
                        dve.wait_ge(rows_T, (n * KT + k) // 2 + 1)
                    src = ps[:, M + k // 2 % 4, (k % 2) * SEQ:(k % 2 + 1) * SEQ]
                    if gain is None:
                        V.tensor_copy(dst[:, k, :], src).then_inc(rowsT_dve, 1)
                    else:
                        V.tensor_scalar(dst[:, k, :], src, gains[:, gain, k:k + 1], None,
                                        ALU.mult).then_inc(rowsT_dve, 1)

            def norm_chunk(par, sqn, s):
                for t in range(TT):
                    dve.wait_ge(sq_ready, 2 * sqn + t + 1)
                    V.tensor_reduce(ssh[:, t, :], sq[:, t, :].rearrange("p (h d) -> p h d", d=HD), AX.X,
                                    ALU.add).then_inc(ssq_ready, 1)
                    dve.wait_ge(rms_ready, 2 * sqn + t + 1)
                    st.link(V.reciprocal(ssh[:, t, :], ssh[:, t, :]))
                    if s:
                        dve.wait_ge(transposed, 2 * s - 1 + t)
                    st.link(V.tensor_tensor(stage[:, t, :].rearrange("p (h d) -> p h d", d=HD),
                                            ps[:, 2 * par + t, :].rearrange("p (h d) -> p h d", d=HD),
                                            ssh[:, t, :].unsqueeze(2).to_broadcast([P, CH, HD]), ALU.mult))
                    dve.sem_inc(evacuated[par], 1)
                    dve.sem_inc(stage_ready, 1)

            def rope_chunk(c):
                for t in range(TT):
                    wait_chunk(dve, c, t)
                    src = ps[:, 2 * (c % 2) + t, :].rearrange("p (g d) -> p g d", d=64)
                    cos = rope[:, 0, t, :].unsqueeze(1).to_broadcast([P, 8, 64])
                    sin = rope[:, 1, t, :].unsqueeze(1).to_broadcast([P, 8, 64])
                    st.mark(V.tensor_tensor(ropeA.rearrange("p (g d) -> p g d", d=64), src, cos, ALU.mult))
                    st.link(V.tensor_tensor(ropeB.rearrange("p (g d) -> p g d", d=64), src, sin, ALU.mult))
                    dve.sem_inc(evacuated[c % 2], 1)
                    dve.wait_ge(transposed, 2 * c - 1 + t)
                    a = ropeA.rearrange("p (h g d) -> p h g d", g=2, d=64)
                    b = ropeB.rearrange("p (h g d) -> p h g d", g=2, d=64)
                    o = stage[:, t, :].rearrange("p (h g d) -> p h g d", g=2, d=64)
                    st.mark(V.tensor_tensor(o[:, :, 0, :], a[:, :, 0, :], b[:, :, 1, :], ALU.subtract))
                    st.link(V.tensor_tensor(o[:, :, 1, :], a[:, :, 1, :], b[:, :, 0, :], ALU.add))
                    dve.sem_inc(stage_ready, 1)

            def mask_logits(f):
                for e in range(2):
                    dve.wait_ge(logits_done, 2 * f + e + 1)
                    if f:
                        dve.wait_ge(probs_T, 2 * (f - 1) + e + 1)
                    st.link(V.tensor_tensor(pb[:, e, :], ps[:, M + 2 + e, 0:384], mask[:, :], ALU.add))
                    st.mark(V.tensor_reduce(nm[:, 2 * e:2 * e + 1], pb[:, e, 0:128], AX.X, ALU.max, negate=True))
                    V.tensor_reduce(nm[:, 2 * e + 1:2 * e + 2], pb[:, e, 128:384], AX.X, ALU.max,
                                    negate=True).then_inc(masked, 1)

            def divide_probs(f):
                for e in range(2):
                    dve.wait_ge(exped, 4 * f + 2 * e + 2)
                    st.link(V.reciprocal(rs[:, 2 * e:2 * e + 2], rs[:, 2 * e:2 * e + 2]))
                    st.mark(V.tensor_scalar(pb[:, e, 0:128], pb[:, e, 0:128], rs[:, 2 * e:2 * e + 1], None, ALU.mult))
                    V.tensor_scalar(pb[:, e, 128:384], pb[:, e, 128:384], rs[:, 2 * e + 1:2 * e + 2], None,
                                    ALU.mult).then_inc(probs_ready, 1)

            def decay_scores(r):
                for e in range(2):
                    dve.wait_ge(rscores, 2 * r + e + 1)
                    dve.wait_ge(decay_in[e], 16 * (r + 1))
                    if r:
                        dve.wait_ge(ry_done, r)
                    else:
                        dve.wait_ge(probs_T, 8)
                    V.tensor_tensor(pb[:, e, :], ps[:, M + 2 + e, 0:384], pT[:, e, :], ALU.mult).then_inc(rdecayed, 1)

            def group_norm(r):
                dve.wait_ge(ry_done, r + 1)
                for q in range(4):
                    st.mark(V.bn_stats(bst[:, q, :], ps[:, M + 2, q * HD:(q + 1) * HD]))
                st.settle()
                for q in range(4):
                    st.mark(V.bn_aggr(mv[:, q, :], bst[:, q, :]))
                st.settle()
                dve.sem_inc(rvar, 1)
                dve.wait_ge(rstd, r + 1)
                st.link(V.reciprocal(mv[:, :, 1:2], mv[:, :, 1:2]))
                for t in range(TT):
                    dve.wait_ge(transposed, 2 * (ST_RET + r) - 1 + t)
                    for e in range(2):
                        q = 2 * t + e
                        st.mark(V.tensor_scalar(stage[:, t, e * HD:(e + 1) * HD], ps[:, M + 2, q * HD:(q + 1) * HD],
                                                mv[:, q, 0:1], mv[:, q, 1:2], ALU.subtract, ALU.mult))
                    st.settle()
                    h = 2 * r
                    V.tensor_tensor(stage[:, t, 0:256], stage[:, t, 0:256],
                                    val[:, 4 + h // 4, t, (h % 4) * HD:(h % 4 + 2) * HD], ALU.mult).then_inc(stage_ready, 1)

            def gate_fox(i):
                for t in range(TT):
                    wait_chunk(dve, C_UP + 2 * i, t)
                    st.mark(V.tensor_tensor(gatesA[:, i, t, :], ps[:, t, :], gatesA[:, i, t, :], ALU.mult))
                st.settle()
                dve.sem_inc(evacuated[0], 2)

            def gate_ret(i):
                for t in range(TT):
                    wait_chunk(dve, C_UP + 2 * i + 1, t)
                    st.link(V.tensor_tensor(gatesB[:, i, t, :], ps[:, 2 + t, :], gatesB[:, i, t, :], ALU.mult))
                    dve.sem_inc(evacuated[1], 1)
                    dve.wait_ge(transposed, 2 * (ST_MERGED + i) - 1 + t)
                    V.tensor_tensor(stage[:, t, :], gatesA[:, i, t, :], gatesB[:, i, t, :], ALU.add).then_inc(stage_ready, 1)

            def add_chunk(c, col):
                for t in range(TT):
                    wait_chunk(dve, c, t)
                    st.link(V.tensor_tensor(xa[:, t, col:col + CW], ps[:, 2 * (c % 2) + t, :], xa[:, t, col:col + CW], ALU.add))
                    dve.sem_inc(evacuated[c % 2], 1)
                    dve.sem_inc(x1_ready, 1)

            norm(0, xin, hh)
            split_w(0, 2)
            dve.wait_ge(first_in, 2 * 16)
            store_rowsT_lo(0, 0)
            split_w(2, NRING)
            dve.wait_ge(tables_in, 14 * 16)
            st.mark(V.tensor_scalar(hgain[:, 0:1], hgain[:, 0:1], HD ** -0.5, None, ALU.mult))
            st.settle()
            V.tensor_scalar(hgain[:, 5:6], hgain[:, 5:6], HD ** -0.5, None, ALU.mult).then_inc(hgain_ready, 1)
            dve.wait_ge(wff_hi, 1)
            V.tensor_tensor(wffs[:, :, 1, :], wff[:, :, :], wffs[:, :, 0, :].bitcast(f32), ALU.subtract).then_inc(wff_lo, 1)
            for c in range(C_RV):
                u = NU * c
                split_w(u + 4, u + 12)
                if c < 4:
                    norm_chunk(c % 2, c, c)
                elif c < 8:
                    rope_chunk(c)
                elif c == 8:
                    dve.wait_ge(ff_done, 1)
                    ff = ps[:, M + 2, 0:32].rearrange("p (t w h) -> p t w h", w=2, h=8)
                    st.link(V.tensor_tensor(lx[:, :, :], ff[:, :, 0, :], bf[:, :].unsqueeze(1).to_broadcast([P, TT, 8]), ALU.add))
                    V.tensor_tensor(lx[:, :, :], ff[:, :, 1, :], lx[:, :, :], ALU.add).then_inc(lf_x, 1)
                    dve.wait_ge(lf_e, 1)
                    st.mark(V.scalar_tensor_tensor(lf[:, :, 0:8], lx[:, :, :], 0.0, le[:, :, :], ALU.min, ALU.subtract))
                    st.link(V.scalar_tensor_tensor(lf[:, :, 32:40], lx[:, :, :], 0.0, le[:, :, :], ALU.min, ALU.subtract))
                    dve.sem_inc(lf_ready, 1)
                else:
                    dve.wait_ge(cum_done, 1)
                    st.link(V.memset(cq, 1.0))
                    st.mark(V.tensor_copy(cq[0:8, :], ps[0:8, M + 3, 0:SEQ]))
                    db = delta[:, :].unsqueeze(2).to_broadcast([40, 8, SEQ])
                    st.link(V.scalar_tensor_tensor(rh, db, -1.0, ps[0:40, M + 3, 0:SEQ].unsqueeze(1).to_broadcast([40, 8, SEQ]),
                                                   ALU.mult, ALU.mult))
                    V.tensor_copy(rh[0:8], db[0:8]).then_inc(cum_ready, 1)
            for f in range(4):
                u = NU * (C_RV + f)
                split_w(u + 4, u + 6)
                mask_logits(f)
                divide_probs(f)
                split_w(u + 6, u + 12)
            for r in range(4):
                u = NU * (C_GATE + r)
                split_w(u + 4, u + 6)
                decay_scores(r)
                split_w(u + 6, u + 9)
                group_norm(r)
                split_w(u + 9, u + 12)
            for c in range(18, C_UP):
                u = NU * c
                for i in range(NU):
                    split_w(u + 4 + i, u + 5 + i)
                    if c == 21:
                        split_src(0, i, memT)
                    if c == C_MV:
                        split_src(1, i, oT)
                if c == 18:
                    norm(1, memx, memx)
                if c == 20:
                    store_rowsT(1, memT, 1)
                if c == C_MK:
                    norm_chunk(0, 4, ST_MK)
            for c in range(C_UP, C_OUT):
                u = first_unit(c)
                for i in range(4):
                    split_w(u + 4 + i, u + 5 + i)
                    if c == C_OUT - 1:
                        split_src(2, i, mergedT)
                if c % 2:
                    gate_ret((c - C_UP) // 2)
                else:
                    gate_fox((c - C_UP) // 2)
            for i in range(4, 6):
                split_src(2, i, mergedT)
            for c in range(C_OUT, C_MQ):
                u = first_unit(c)
                split_w(u + 4, u + 8)
                if c == C_OUT:
                    for i in range(6, 8):
                        split_src(2, i, mergedT)
                    dve.wait_ge(x_again, 16 * TT)
                split_w(u + 8, u + (11 if c == C_MQ - 1 else 12))
                add_chunk(c, (c - C_OUT) * CW)
            sum_squares(2)
            norm(2, xa, hh)
            u = first_unit(C_MQ)
            split_w(u + 3, u + 4)
            store_rowsT_lo(2, 2)
            split_w(u + 4, u + 11)
            norm_chunk(0, 5, ST_MQ)
            split_w(u + 11, u + 12)
            for h in range(MEMH + 1):
                if h < MEMH:
                    dve.wait_ge(mlog, h + 1)
                    V.tensor_reduce(nm[:, 2 * h:2 * h + 2], ps[:, M + h, :].rearrange("p (t m) -> p t m", m=SEQ), AX.X,
                                    ALU.max, negate=True).then_inc(mmax, 1)
                if h:
                    a, b = 2 * (h - 1), 2 * h
                    dve.wait_ge(mexp, b)
                    st.link(V.reciprocal(rs[:, a:b], rs[:, a:b]))
                    V.tensor_tensor(mp[:, a:b, :], mp[:, a:b, :], rs[:, a:b].unsqueeze(2).to_broadcast([P, 2, SEQ]),
                                    ALU.mult).then_inc(mprobs, 1)
            for j in range(2):
                dve.wait_ge(moT_hi, j + 1)
                V.tensor_tensor(hTs[:, 1, 2 * j:2 * j + 2, :], ps[:, M + j, :].rearrange("p (e q) -> p e q", q=SEQ),
                                hT_hi[:, 2 * j:2 * j + 2, :], ALU.subtract).then_inc(moT_ready, 1)
            for c in range(C_MO, C_MO + 4):
                if c < C_MO + 2:
                    u = first_unit(c)
                    split_w(u + 4, u + 6)
                col = (c - C_MO) * CW
                add_chunk(c, col)
                if c == C_MO:
                    dve.wait_ge(ffg_in, 16)
                if c == C_MO + 3:
                    sum_squares(3)
                for t in range(TT):
                    st.mark(V.tensor_tensor(hh[:, t, col:col + CW], xa[:, t, col:col + CW], ffn_gain[:, col:col + CW], ALU.mult))
            norm(3, hh, hh)
            store_rowsT(3, hT, None)

            def topk(dst_v, dst_i, srcs, tmps):
                n = len(srcs)
                for q in range(n):
                    st.mark(V.max(dst_v[q][:, 0:8], srcs[q]))
                st.settle()
                for q in range(n):
                    st.mark(V.max_index(dst_i[q][:, 0:8], dst_v[q][:, 0:8], srcs[q]))
                    st.mark(V.match_replace(tmps[q], dst_v[q][:, 0:8], srcs[q], LOWEST))
                st.settle()
                for q in range(n):
                    st.mark(V.max(dst_v[q][:, 8:16], tmps[q]))
                st.settle()
                for q in range(n):
                    st.mark(V.max_index(dst_i[q][:, 8:16], dst_v[q][:, 8:16], tmps[q]))
                st.settle()

            def route(t, h0, srcs):
                nh = len(srcs) // 2
                topk([tv[:, q, :] for q in range(2 * nh)], [ti[:, q, :] for q in range(2 * nh)],
                     srcs, [tmp[:, q, :] for q in range(2 * nh)])
                if t == 0:
                    dve.sem_inc(scores_read, nh)
                st.mark(V.tensor_copy(tif[:, 0:nh, :, :], ti[:, 0:2 * nh, :].rearrange("p (e h) k -> p e h k", h=2)))
                for e in range(nh):
                    st.mark(V.tensor_tensor(cand[:, e, :].rearrange("p (a b) -> p a b", b=TOPK),
                                            tv[:, 2 * e, :].unsqueeze(2).to_broadcast([P, TOPK, TOPK]),
                                            tv[:, 2 * e + 1, :].unsqueeze(1).to_broadcast([P, TOPK, TOPK]), ALU.add))
                st.settle()
                topk([gate[:, t * PH + h0 + e, :] for e in range(nh)], [pos[:, e, :] for e in range(nh)],
                     [cand[:, e, :] for e in range(nh)], [tmp2[:, e, :] for e in range(nh)])
                n = nh * TOPK
                posf = pos[:, 0:nh, :].rearrange("p e k -> p (e k)")
                st.mark(V.tensor_scalar(pab[:, 0, 0:n], posf, 4, None, ALU.logical_shift_right))
                st.link(V.tensor_scalar(pab[:, 1, 0:n], posf, TOPK - 1, None, ALU.bitwise_and))
                st.mark(V.tensor_copy(af[:, 0:n], pab[:, 0, 0:n]))
                st.link(V.tensor_copy(bfl[:, 0:n], pab[:, 1, 0:n]))
                for half, (pf, key) in enumerate(((af, e0), (bfl, e1))):
                    st.link(V.tensor_tensor(eq[:, 0:n, :], pf[:, 0:n].unsqueeze(2).to_broadcast([P, n, TOPK]),
                                            iota[:, :].unsqueeze(1).to_broadcast([P, n, TOPK]), ALU.is_equal))
                    for e in range(nh):
                        st.mark(V.tensor_tensor(eq[:, e * 16:(e + 1) * 16, :], eq[:, e * 16:(e + 1) * 16, :],
                                                tif[:, e, half, :].unsqueeze(1).to_broadcast([P, TOPK, TOPK]), ALU.mult))
                    st.settle()
                    st.link(V.tensor_reduce(key[:, 0:n], eq[:, 0:n, :], AX.X, ALU.add))
                c0 = t * SLOTS + h0 * TOPK
                st.link(V.scalar_tensor_tensor(idx[:, c0:c0 + n], e0[:, 0:n], float(NKEY), e1[:, 0:n], ALU.mult, ALU.add))
                dve.sem_inc(routed, nh)

            def shift_gates(t):
                g, m = gate[:, t * PH:(t + 1) * PH, :], gsum[:, t * PH:(t + 1) * PH]
                st.link(V.tensor_copy(m, g[:, :, 0]))
                V.tensor_tensor(g, g, m.unsqueeze(2).to_broadcast([P, PH, TOPK]), ALU.subtract).then_inc(sfin_ready, 1)

            def divide_gates(t):
                g, m = gate[:, t * PH:(t + 1) * PH, :], gsum[:, t * PH:(t + 1) * PH]
                dve.wait_ge(gexp, t + 1)
                st.link(V.tensor_reduce(m, g, AX.X, ALU.add))
                st.link(V.reciprocal(m, m))
                V.tensor_tensor(g, g, m.unsqueeze(2).to_broadcast([P, PH, TOPK]), ALU.mult).then_inc(gate_ready, 1)

            def dots(g, tile, par):
                for k in range(NG):
                    if k == 0 and not (isinstance(g, int) and g < 2):
                        dve.wait_ge(gelued, g - 1)
                    dve.wait_ge(u_ready[k], g * 16 + 16)
                    V.tensor_tensor_reduce(out=urows[k], in0=urows[k], in1=hh[:, tile, :], scale=1.0,
                                           scalar=0.0, op0=ALU.mult, op1=ALU.add,
                                           accum_out=acts[:, par, k:k + 1]).then_inc(dotted, 1)

            for cc in range(4):
                scores0 = [ps[:, M + q // 2, (q % 2) * NKEY:(q % 2 + 1) * NKEY] for q in range(4)]
                if cc == 0:
                    for h in range(2):
                        dve.wait_ge(scores_done, h + 1)
                        route(0, h, scores0[2 * h:2 * h + 2])
                else:
                    dve.wait_ge(scores_done, 2 * cc + 2)
                    route(0, 2 * cc, scores0)
                if cc < 3:
                    dots(cc, 0, cc % 2)
            shift_gates(0)
            divide_gates(0)
            dots(3, 0, 1)
            for j in range(4):
                dots(AHEAD + j, 0, j % 2)
                dve.wait_ge(scores1_stored, 2 * j + 2)
                route(1, 2 * j, [scores1[:, 2 * j + q // 2, (q % 2) * NKEY:(q % 2 + 1) * NKEY] for q in range(4)])
            dve.sem_inc(routed, 1)
            shift_gates(1)
            divide_gates(1)
            for tile in range(TT):
                with dve.Fori(GROUPS // 2 * tile if tile else AHEAD, GROUPS // 2 * (tile + 1)) as i:
                    for par in range(2):
                        dots(2 * i + par, tile, par)

        @block.tensor
        def _(pe):
            T = nc.tensor

            PARTS = ((0, 0), (0, 1), (1, 0))

            def units(c, a, b, k0=0, n_units=NU):
                par = c % 2
                if a == 0 and c >= 2:
                    pe.wait_ge(evacuated[par], 2 * (c // 2))
                for i in range(a, b):
                    n = first_unit(c) + i
                    pe.wait_ge(lo_ready, n + 1)
                    if c in (0, C_MQ):
                        pe.wait_ge(rows_lo, (KT if c else 0) + KU * (i + 1))
                    if c in SOURCE:
                        pe.wait_ge(src_lo, SOURCE[c] + i + 1)
                    for t in range(TT):
                        for kk in range(KU):
                            for rp, wp in PARTS:
                                ins = T.matmul(ps[:, 2 * par + t, :],
                                               hTs[:, rp, k0 + KU * i + kk, t * P:(t + 1) * P], ws[:, wp, n % NRING, kk, :],
                                               start=i == 0 and kk == 0 and rp + wp == 0,
                                               stop=i == n_units - 1 and kk == KU - 1 and rp == 1)
                        if t == 0 and i == n_units - 1:
                            ins.then_inc(projected, 1)
                    ins.then_inc(units_used, 1)

            SOURCE = {C_MK: 0, C_UP: NU, C_UP + 1: NU + 4, C_OUT: 2 * NU}

            def transpose_rows(n, src, k0, k1):
                if k0 == 0:
                    pe.wait_ge(norm_ready, 2 * n + 2)
                for k in range(k0, k1):
                    if k >= 8 and k % 2 == 0:
                        if n % 2 == 0:
                            pe.wait_ge(rows_lo, KT * (n // 2) + k - 6)
                        else:
                            pe.wait_ge(rowsT_act if k // 2 % 2 else rowsT_dve, 8 * (n // 2) + (k // 2 - 4) // 2 * 2 + 2)
                    for t in range(TT):
                        ins = T.transpose(ps[:, M + k // 2 % 4, (k % 2) * SEQ + t * P:(k % 2) * SEQ + (t + 1) * P],
                                          src[:, t, k * P:(k + 1) * P], ident[:, :])
                    if k % 2:
                        ins.then_inc(rows_T, 1)

            def transpose_stage(s, blocks=CH):
                for t in range(TT):
                    pe.wait_ge(stage_ready, 2 * s + t + 1)
                    if s:
                        pe.wait_ge(tstored, 2 * s - 1 + t)
                    for b in range(blocks):
                        ins = T.transpose(ps[:, M + t, b * P:(b + 1) * P], stage[:, t, b * P:(b + 1) * P], ident[:, :])
                    ins.then_inc(transposed, 1)

            pe.wait_ge(first_in, 2 * 16)
            transpose_rows(0, hh, 0, KT)
            for c in range(C_RV):
                units(c, 0, 6)
                if 1 <= c <= 8:
                    transpose_stage(c - 1)
                if c == 8:
                    pe.wait_ge(wff_lo, 1)
                    for t in range(TT):
                        for k in range(KT):
                            for rp in range(2):
                                n = 16 - 8 * rp
                                ins = T.matmul(ps[:, M + 2, t * 16:t * 16 + n], hTs[:, rp, k, t * P:(t + 1) * P],
                                               wffs[:, k, :, :].rearrange("p w n -> p (w n)")[:, 0:n],
                                               start=k == 0 and rp == 0, stop=k == KT - 1 and rp == 1,
                                               skip_group_check=True)
                    ins.then_inc(ff_done, 1)
                if c == 9:
                    pe.wait_ge(lf_ready, 1)
                    T.matmul(ps[0:40, M + 3, 0:SEQ], lf[:, 0, :], tri[:, :], start=True, stop=False)
                    T.matmul(ps[0:40, M + 3, P:SEQ], lf[:, 1, :], tri[:, 0:P], start=False, stop=True).then_inc(cum_done, 1)
                units(c, 6, NU)
            for f in range(4):
                c = C_RV + f
                units(c, 0, 2)
                if f == 0:
                    pe.wait_ge(cum_ready, 1)
                pe.wait_ge(head_staged, 4 * (f + 1))
                if f:
                    pe.wait_ge(fox_stored, f)
                for e in range(2):
                    h = 2 * f + e
                    for t, (a, w) in enumerate(((0, P), (P, SEQ))):
                        T.matmul(ps[:, M + 2 + e, a:a + w], qs[:, e, t * P:(t + 1) * P], qkh[:, 8 + h, 0:w], start=True, stop=False)
                        ins = T.matmul(ps[:, M + 2 + e, a:a + w], cq[:, t * P:(t + 1) * P], rh[:, h, 0:w], start=False, stop=True)
                    ins.then_inc(logits_done, 1)
                units(c, 2, 5)
                if f == 0:
                    pe.wait_ge(tstored, 16)
                for e in range(2):
                    pe.wait_ge(probs_ready, 2 * f + e + 1)
                    if f:
                        pe.wait_ge(probsT_ready, 2 * (f - 1) + e + 1)
                    for b in range(3):
                        ins = T.transpose(ps[:, M + e, b * P:(b + 1) * P], pb[:, e, b * P:(b + 1) * P], ident[:, :])
                    ins.then_inc(probs_T, 1)
                units(c, 5, NU)
                pe.wait_ge(probsT_ready, 2 * f + 2)
                for e in range(2):
                    o = ps[:, M + 2, e * SEQ:(e + 1) * SEQ]
                    T.matmul(o, vs[:, e, 0, :], pT[:, e, 0:SEQ], start=e == 0, stop=False, skip_group_check=True)
                    ins = T.matmul(o[:, P:SEQ], vs[:, e, 1, :], pT[:, e, SEQ:384], start=False, stop=e == 1,
                                   skip_group_check=True)
                ins.then_inc(fox_done, 1)
            for r in range(4):
                c = C_GATE + r
                units(c, 0, 2)
                pe.wait_ge(rhead_staged, 2 * (r + 1))
                if r == 0:
                    pe.wait_ge(fox_stored, 4)
                    pe.wait_ge(probsT_ready, 8)
                if r:
                    pe.wait_ge(stage_ready, 2 * (ST_RET + r))
                for e in range(2):
                    h = 2 * r + e
                    T.matmul(ps[:, M + 2 + e, 0:SEQ], qs[:, e, 0:P], qkh[:, 16 + h, :], start=True, stop=True)
                    T.matmul(ps[:, M + 2 + e, SEQ:384], qs[:, e, P:SEQ], qkh[:, 16 + h, P:SEQ], start=True,
                             stop=True).then_inc(rscores, 1)
                units(c, 2, 5)
                pe.wait_ge(rdecayed, 2 * (r + 1))
                for e in range(2):
                    h = 2 * r + e
                    cc, o = 2 + h // 4, (h % 4) * HD
                    T.matmul(ps[:, M + 2, e * HD:(e + 1) * HD], pb[:, e, 0:P], val[:, cc, 0, o:o + HD], start=True, stop=True)
                    y1 = ps[:, M + 2, (2 + e) * HD:(3 + e) * HD]
                    T.matmul(y1, pb[:, e, P:SEQ], val[:, cc, 0, o:o + HD], start=True, stop=False)
                    ins = T.matmul(y1, pb[:, e, SEQ:384], val[:, cc, 1, o:o + HD], start=False, stop=True)
                ins.then_inc(ry_done, 1)
                units(c, 5, NU)
                transpose_stage(ST_RET + r, 2)
            for c in range(18, C_MK):
                units(c, 0, 4)
                units(c, 4, NU)
                if c == 20:
                    pe.wait_ge(tstored, 2 * ST_MK)
                    transpose_rows(1, memx, 0, KT)
            for c in (C_MK, C_MV):
                units(c, 0, 6)
                if c == C_MV:
                    transpose_stage(ST_MK)
                units(c, 6, NU)
            for i in range(4):
                units(C_UP + 2 * i, 0, 4, 0, 4)
                if i:
                    transpose_stage(ST_MERGED + i - 1)
                units(C_UP + 2 * i + 1, 0, 4, 8, 4)
            units(C_OUT, 0, 4)
            transpose_stage(ST_MERGED + 3)
            units(C_OUT, 4, NU)
            pe.wait_ge(keys_in, 16)
            for j in range(4):
                if j:
                    units(C_OUT + j, 0, NU)
                if j >= 2:
                    pe.wait_ge(keys_stored, j - 1)
                for b in range(4):
                    ins = T.transpose(ps[:, M + 2 + j % 2, b * P:(b + 1) * P], keys_raw[:, 4 * j + b, :], ident[:, :])
                ins.then_inc(keys_T, 1)
            pe.wait_ge(keys_stored, 4)
            transpose_rows(2, hh, 0, KT)
            units(C_MQ, 0, NU)
            transpose_stage(ST_MQ)
            pe.wait_ge(tstored, 2 * (ST_MQ + 1))
            for g in range(8):
                h, t = g // 2, g % 2
                ins = T.matmul(ps[:, M + h, t * SEQ:(t + 1) * SEQ], qTm[:, h, t * P:(t + 1) * P], kmT[:, h, :], start=True, stop=True)
                if t:
                    ins.then_inc(mlog, 1)
            pe.wait_ge(evacuated[0], 2 * 19)
            pe.wait_ge(evacuated[1], 2 * 18)
            for h in range(MEMH):
                pe.wait_ge(mprobs, h + 1)
                for m in range(2):
                    for t in range(TT):
                        ins = T.transpose(ps[:, h, m * SEQ + t * P:m * SEQ + (t + 1) * P],
                                          mp[:, 2 * h + t, m * P:(m + 1) * P], ident[:, :])
                ins.then_inc(mpT_done, 1)
            for h in range(MEMH):
                pe.wait_ge(mpT_ready, h + 1)
                o = ps[:, M + h // 2, (h % 2) * SEQ:(h % 2 + 1) * SEQ]
                for m in range(2):
                    ins = T.matmul(o, vm[:, m, h * HD:(h + 1) * HD], mpT[:, h, m, :], start=m == 0, stop=m == 1)
                if h % 2:
                    ins.then_inc(mo_done, 1)
            pe.wait_ge(moT_ready, 2)
            for c in range(C_MO, C_MO + 4):
                units(c, 0, 2, 0, 2)
            transpose_rows(3, hh, 0, KT)
            pe.wait_ge(evacuated[0], 2 * 21)
            pe.wait_ge(evacuated[1], 2 * 20)

            def scores(q):
                h, half = q // 2, q % 2
                pe.wait_ge(pq_stored, q + 1)
                if half == 0 and h >= 2:
                    pe.wait_ge(scores_read, h // 2 * 2)
                    pe.wait_ge(scores1_stored, h - 1)
                for t in range(TT):
                    b = half * NKEY
                    ins = T.matmul(ps[:, M + 2 * t + h % 2, b:b + NKEY], qTp[q][:, t * P:(t + 1) * P], keysT[:, q, :], start=True, stop=True)
                if half:
                    ins.then_inc(scores_done, 1)

            for cc in range(4):
                if cc >= 2:
                    pe.wait_ge(pq_stored, 4 * (cc - 1))
                for ns in ((0, 1), (2, 3)) if cc == 0 else (range(4),):
                    for j in range(NRING):
                        weights, loaded, value = pq_place(NRING * cc + j)
                        if ns[0] == 0:
                            pe.wait_ge(loaded, value)
                            if cc == 0:
                                pe.wait_ge(rowsT_act, NU + 2 * j + 2)
                                pe.wait_ge(rowsT_dve, NU + 2 * j + 2)
                        elif j == 1:
                            scores(0)
                            scores(1)
                        for n in ns:
                            if cc and j == 0 and n == 2:
                                for q in range(max(4 * (cc - 1), 2), 4 * cc):
                                    scores(q)
                            for k in range(KPC):
                                first = j == 0 and k == 0
                                ins = T.matmul(ps[:, 2 * (cc % 2) + n // 2, (n % 2) * SEQ:(n % 2 + 1) * SEQ],
                                               weights[:, k, n * P:(n + 1) * P], hT[:, KPC * j + k, :],
                                               start=first and n % 2 == 0, stop=j == NRING - 1 and k == KPC - 1,
                                               skip_group_check=True)
                        if ns[-1] == 1:
                            if j == NRING - 1:
                                ins.then_inc(pq_first, 1)
                        elif j < NRING - 1:
                            ins.then_inc(raw_used, 1)
                        else:
                            ins.then_inc(pq_done, 1)
            for q in range(12, 16):
                scores(q)
            pe.wait_ge(pq_stored, 16)
            for tile in range(TT):
                if tile:
                    pe.wait_ge(scores_read, PH)
                    pe.wait_ge(scores1_stored, PH)
                for b in range(4):
                    T.matmul(ps[:, 4 * tile + b, :], ident[:, :], xa[:, tile, b * CW:(b + 1) * CW], start=True, stop=False)

                def group(p, last):
                    for k in range(NG):
                        pe.wait_ge(diag_ready, p * NG + (tile * SLOTS + k + 1))
                        pe.wait_ge(v_ready[k], p * 16 + 16 * (tile * GROUPS + 1))
                        for b in range(4):
                            ins = T.matmul(ps[:, 4 * tile + b, :], diag[k], vrows[k][:, b * CW:(b + 1) * CW],
                                           start=False, stop=last and k == NG - 1)
                            if last and k == NG - 1 and b < 3:
                                ins.then_inc(bank_done, 1)
                        ins.then_inc(accumulated, 1)
                with pe.Fori(0, GROUPS - 1) as p:
                    group(p, False)
                group(GROUPS - 1, True)


def tables():
    f = np.float32
    ident = np.eye(P, dtype=f)
    s = np.arange(P)[:, None]
    tri = (s <= np.arange(SEQ)[None, :]).astype(f)
    q, k = np.arange(P)[:, None], np.arange(P)[None, :]
    causal = np.where(k <= q, 0.0, MASKED).astype(f)
    mask = np.concatenate([causal, np.zeros((P, P), f), causal], axis=1)
    half = HD // 2
    inv = np.exp(-math.log(10000.0) * np.arange(half, dtype=f) / half).astype(f)
    ang = (np.arange(SEQ, dtype=f)[:, None] * inv[None, :]).reshape(TT, P, half).transpose(1, 0, 2)
    rope = np.stack([np.cos(ang.astype(f)), np.sin(ang.astype(f))], axis=1).astype(f)
    lg = np.log1p(-np.exp2(-5.0 - np.arange(RETH, dtype=f))).astype(f)
    i, j = np.arange(SEQ)[None, :], np.arange(SEQ)[:, None]
    dec = np.exp(lg[:, None, None].astype(np.float64) * np.abs(i - j)) * (j // RET_CHUNK <= i // RET_CHUNK)
    dec = np.concatenate([dec[:, 0:P, :], dec[:, P:SEQ, P:SEQ]], axis=2).astype(f)
    delta = np.zeros((40, 8), f)
    delta[np.arange(8), np.arange(8)] = 1
    delta[32 + np.arange(8), np.arange(8)] = 1
    iota = np.tile(np.arange(TOPK, dtype=f), (P, 1))
    return {"t_ident": ident, "t_tri": tri, "t_mask": mask, "t_rope": rope, "t_decay": dec, "t_delta": delta, "t_iota": iota}


_INS = ['x', 'mem', 'ln_mix_g', 'w_in', 'b_forget', 'fox_q_norm_g', 'fox_k_norm_g', 'ret_norm_g', 'w_fox_up',
        'w_ret_up', 'w_out', 'ln_mem_g', 'mem_norm_g', 'w_mq', 'w_mkv', 'mem_q_norm_g', 'mem_k_norm_g', 'w_mo',
        'ln_ffn_g', 'w_peer_q', 'peer_sub_keys', 'peer_u', 'peer_v']


def kernel(**inputs):
    import concourse.bacc as _bacc
    from concourse.bass_utils import run_bass_kernel_spmd as _run

    nc = _bacc.Bacc("TRN2", target_bir_lowering=False, num_devices=1)
    arrays, args = {}, []
    for name, a in [(n, inputs[n]) for n in _INS] + list(tables().items()):
        a = np.ascontiguousarray(a)
        arrays[f"in_{name}"] = a
        args.append(nc.dram_tensor(f"in_{name}", a.shape, mybir.dt.from_np(a.dtype), kind="ExternalInput").ap())
    args.append(nc.dram_tensor("out", (1, SEQ, D), mybir.dt.float32, kind="ExternalOutput").ap())
    build(nc, *args)
    r = _run(nc, [arrays], core_ids=[0])
    return r.results[0]["out"]
```
